# Optimizing a Trainium2 kernel written in Bass

```python
import math
import jax, jax.numpy as jnp
from jax import lax
import numpy as np

D_MODEL = 1024
BATCH = 1
SEQ = 256
DEPTH = 2

PLE_DIM = 256
ROPE_THETA = 10000.0
EPS = 1e-6
NEG_INF = -1e30
HEAD_DIM = 64

A_HEADS = 8
A_KV_GROUPS = 2
A_CMP_LEN = 32
A_CMP_STRIDE = 16
A_CMP_HIDDEN = 256
A_SEL_LEN = 64
A_TOPK = 16
A_WINDOW = 512
A_Q_CHUNK = 128
A_FORCE_BONUS = 1e4

B_HEADS = 8
B_KV_HEADS = 2
B_WINDOW = 128
B_BLOCK = 128

C_HEADS = 8
C_Q_RANK = 256
C_KV_RANK = 256
C_NOPE = 64
C_ROPE = 32
C_V = 64
C_Q_BLOCK = 128

D_FF = int(math.ceil(8 * D_MODEL / 3 / 256)) * 256

A_Q = A_HEADS * HEAD_DIM
A_KV = A_KV_GROUPS * HEAD_DIM
A_GATES = A_HEADS * 3
B_Q = B_HEADS * HEAD_DIM
B_KV = B_KV_HEADS * HEAD_DIM
IN_SIZES = (A_Q, A_KV, A_KV, A_KV, A_KV, A_KV, A_KV, A_GATES, B_Q, B_KV, B_KV, C_Q_RANK, C_KV_RANK, C_ROPE)
IN_COLS = sum(IN_SIZES)
A_OUT = A_HEADS * HEAD_DIM
B_OUT = B_HEADS * HEAD_DIM
C_OUT = C_HEADS * C_V


def rmsnorm(x, g):
    xf = x.astype(jnp.float32)
    y = xf * lax.rsqrt(jnp.mean(xf * xf, axis=-1, keepdims=True) + EPS)
    return (y * g.astype(jnp.float32)).astype(x.dtype)

def rope_tables(positions, dim):
    inv_freq = jnp.power(jnp.float32(ROPE_THETA), -jnp.arange(0, dim, 2, dtype=jnp.float32) / dim)
    ang = positions.astype(jnp.float32)[..., None] * inv_freq
    return jnp.cos(ang), jnp.sin(ang)

def apply_rope(x, cos, sin):
    half = x.shape[-1] // 2
    xf = x.astype(jnp.float32)
    x1, x2 = xf[..., :half], xf[..., half:]
    c, s = cos[:, :, None, :], sin[:, :, None, :]
    return jnp.concatenate([x1 * c - x2 * s, x2 * c + x1 * s], axis=-1).astype(x.dtype)

def masked_softmax(scores, mask):
    p = jax.nn.softmax(jnp.where(mask, scores, NEG_INF), axis=-1)
    return jnp.where(mask, p, 0.0)

def compress_blocks(t, tok, pos, w1, w2):
    B, _, G, dh = t.shape
    n_cmp, L = tok.shape
    blocks = t[:, tok] + pos[:, None, :].astype(t.dtype)
    flat = blocks.transpose(0, 1, 3, 2, 4).reshape(B, n_cmp, G, L * dh)
    return jax.nn.gelu(flat @ w1) @ w2

def nsa_attention(q, kc, vc, ks, vs, kw, vw, gate_logits, pos_k, w1_k, w2_k, pos_v, w1_v, w2_v):
    B, S = q.shape[0], q.shape[1]
    G, R, dh = A_KV_GROUPS, A_HEADS // A_KV_GROUPS, HEAD_DIM
    QC = A_Q_CHUNK
    scale = dh ** -0.5
    dt = q.dtype
    qg = q.reshape(B, S, G, R, dh)
    gates = jax.nn.sigmoid(gate_logits.astype(jnp.float32)).reshape(B, S, G, R, 3).astype(dt)
    n_cmp = (S - A_CMP_LEN) // A_CMP_STRIDE + 1
    tok = np.arange(n_cmp)[:, None] * A_CMP_STRIDE + np.arange(A_CMP_LEN)[None, :]
    k_cmp = compress_blocks(kc, tok, pos_k, w1_k, w2_k)
    v_cmp = compress_blocks(vc, tok, pos_v, w1_v, w2_v)
    cmp_end = jnp.asarray(tok[:, -1], jnp.int32)
    n_sel = S // A_SEL_LEN
    sel_map = np.zeros((n_cmp, n_sel), np.float32)
    np.add.at(sel_map, (np.repeat(np.arange(n_cmp), A_CMP_LEN), (tok // A_SEL_LEN).reshape(-1)), 1.0 / A_CMP_LEN)
    sel_map = jnp.asarray(sel_map)
    top_k = min(A_TOPK, n_sel)
    ks_blk = ks.transpose(0, 2, 1, 3).reshape(B, G, n_sel, A_SEL_LEN * dh)
    vs_blk = vs.transpose(0, 2, 1, 3).reshape(B, G, n_sel, A_SEL_LEN * dh)
    gather_blocks = jax.vmap(jax.vmap(lambda t, i: t[i]))
    kw_pad = jnp.pad(kw, ((0, 0), (A_WINDOW, 0), (0, 0), (0, 0)))
    vw_pad = jnp.pad(vw, ((0, 0), (A_WINDOW, 0), (0, 0), (0, 0)))
    blk_ids = jnp.arange(n_sel)

    def chunk(c):
        t0 = c * QC
        tq = t0 + jnp.arange(QC)
        qc = lax.dynamic_slice_in_dim(qg, t0, QC, axis=1)
        gc = lax.dynamic_slice_in_dim(gates, t0, QC, axis=1)
        s = jnp.einsum('bqgrd,bngd->bgrqn', qc, k_cmp).astype(jnp.float32) * scale
        p_cmp = masked_softmax(s, cmp_end[None, :] <= tq[:, None])
        o_cmp = jnp.einsum('bgrqn,bngd->bqgrd', p_cmp.astype(dt), v_cmp)
        imp = jnp.einsum('bgrqn,nj->bgqj', p_cmp, sel_map)
        cur = tq // A_SEL_LEN
        valid = blk_ids[None, :] <= cur[:, None]
        forced = (blk_ids[None, :] == 0) | (blk_ids[None, :] == cur[:, None]) | (blk_ids[None, :] == cur[:, None] - 1)
        imp = jnp.where(valid, imp + jnp.where(forced, A_FORCE_BONUS, 0.0), NEG_INF)
        _, top_idx = lax.top_k(imp, top_k)
        idx_flat = top_idx.reshape(B, G, QC * top_k)
        kb = gather_blocks(ks_blk, idx_flat).reshape(B, G, QC, top_k * A_SEL_LEN, dh)
        vb = gather_blocks(vs_blk, idx_flat).reshape(B, G, QC, top_k * A_SEL_LEN, dh)
        key_pos = (top_idx[..., None] * A_SEL_LEN + jnp.arange(A_SEL_LEN)).reshape(B, G, QC, top_k * A_SEL_LEN)
        m_sel = key_pos <= tq[None, None, :, None]
        s = jnp.einsum('bqgrd,bgqkd->bgrqk', qc, kb).astype(jnp.float32) * scale
        p_sel = masked_softmax(s, m_sel[:, :, None])
        o_sel = jnp.einsum('bgrqk,bgqkd->bqgrd', p_sel.astype(dt), vb)
        kwc = lax.dynamic_slice_in_dim(kw_pad, t0, QC + A_WINDOW, axis=1)
        vwc = lax.dynamic_slice_in_dim(vw_pad, t0, QC + A_WINDOW, axis=1)
        kp = t0 - A_WINDOW + jnp.arange(QC + A_WINDOW)
        m_win = (kp[None, :] <= tq[:, None]) & (kp[None, :] > tq[:, None] - A_WINDOW) & (kp[None, :] >= 0)
        s = jnp.einsum('bqgrd,bkgd->bgrqk', qc, kwc).astype(jnp.float32) * scale
        p_win = masked_softmax(s, m_win)
        o_win = jnp.einsum('bgrqk,bkgd->bqgrd', p_win.astype(dt), vwc)
        return gc[..., 0:1] * o_cmp + gc[..., 1:2] * o_sel + gc[..., 2:3] * o_win

    out = lax.map(chunk, jnp.arange(S // QC))
    return out.transpose(1, 0, 2, 3, 4, 5).reshape(B, S, A_HEADS * dh)

def swa_sink_attention(q, k, v, sinks):
    B, S = q.shape[0], q.shape[1]
    G, R, dh, BLK = B_KV_HEADS, B_HEADS // B_KV_HEADS, HEAD_DIM, B_BLOCK
    nb = S // BLK
    qb = q.reshape(B, nb, BLK, G, R, dh)

    def band(t):
        tb = t.reshape(B, nb, BLK, G, dh)
        prev = jnp.pad(tb, ((0, 0), (1, 0), (0, 0), (0, 0), (0, 0)))[:, :-1]
        return jnp.concatenate([prev, tb], axis=2)

    kb, vb = band(k), band(v)
    s = jnp.einsum('bnqgrd,bnkgd->bngrqk', qb, kb).astype(jnp.float32) * (dh ** -0.5)
    qi = jnp.arange(BLK)[:, None]
    kj = jnp.arange(2 * BLK)[None, :] - BLK
    rel = (kj <= qi) & (kj > qi - B_WINDOW)
    mask = rel[None] & ((jnp.arange(nb)[:, None, None] > 0) | (kj[None] >= 0))
    s = jnp.where(mask[None, :, None, None], s, NEG_INF)
    sink = jnp.broadcast_to(sinks.astype(jnp.float32).reshape(G, R)[None, None, :, :, None, None], s.shape[:-1] + (1,))
    p = jax.nn.softmax(jnp.concatenate([s, sink], axis=-1), axis=-1)[..., :-1]
    o = jnp.einsum('bngrqk,bnkgd->bnqgrd', p.astype(v.dtype), vb)
    return o.reshape(B, S, B_HEADS * dh)

def causal_block_attention(q, k, v, scale):
    B, S, H, _ = q.shape
    dv = v.shape[-1]
    key_pos = jnp.arange(S)

    def body(c):
        t0 = c * C_Q_BLOCK
        qb = lax.dynamic_slice_in_dim(q, t0, C_Q_BLOCK, axis=1)
        s = jnp.einsum('bqhd,bkhd->bhqk', qb, k).astype(jnp.float32) * scale
        mask = key_pos[None, :] <= (t0 + jnp.arange(C_Q_BLOCK))[:, None]
        p = jax.nn.softmax(jnp.where(mask, s, NEG_INF), axis=-1)
        return jnp.einsum('bhqk,bkhd->bqhd', p.astype(v.dtype), v)

    out = lax.map(body, jnp.arange(S // C_Q_BLOCK))
    return out.transpose(1, 0, 2, 3, 4).reshape(B, S, H * dv)

def mla_attention(cq, ckv, k_pe_raw, q_norm, w_q_up, kv_norm, w_kv_up, cos32, sin32):
    B, S = cq.shape[0], cq.shape[1]
    q = (rmsnorm(cq, q_norm) @ w_q_up).reshape(B, S, C_HEADS, C_NOPE + C_ROPE)
    q_nope, q_pe = q[..., :C_NOPE], apply_rope(q[..., C_NOPE:], cos32, sin32)
    kv = (rmsnorm(ckv, kv_norm) @ w_kv_up).reshape(B, S, C_HEADS, C_NOPE + C_V)
    k_nope, v = kv[..., :C_NOPE], kv[..., C_NOPE:]
    k_pe = apply_rope(k_pe_raw[:, :, None, :], cos32, sin32)
    qf = jnp.concatenate([q_nope, q_pe], axis=-1)
    kf = jnp.concatenate([k_nope, jnp.broadcast_to(k_pe, (B, S, C_HEADS, C_ROPE))], axis=-1)
    return causal_block_attention(qf, kf, v, (C_NOPE + C_ROPE) ** -0.5)

def hybrid_layer(x, p_i, rope64, rope32, mix_norm, w_in, a_cmp_pos_k, a_cmp_w1_k, a_cmp_w2_k,
                 a_cmp_pos_v, a_cmp_w1_v, a_cmp_w2_v, b_sinks, c_q_norm, c_w_q_up, c_kv_norm, c_w_kv_up,
                 w_branch_gate, w_branch_a, w_branch_b, w_branch_c, w_out, ffn_norm, w_ffn_gate, w_ffn_up,
                 w_ffn_down, ple_norm, w_ple_proj, w_ple_gate):
    B, S, _ = x.shape
    cos64, sin64 = rope64
    cos32, sin32 = rope32
    h = rmsnorm(x, mix_norm)
    z = h @ w_in
    split_points = [int(v) for v in np.cumsum(IN_SIZES)[:-1]]
    (a_q, a_kc, a_vc, a_ks, a_vs, a_kw, a_vw, a_g, b_q, b_k, b_v, c_cq, c_ckv, c_kpe) = jnp.split(z, split_points, axis=-1)

    def heads(t, n):
        return t.reshape(B, S, n, -1)

    def rot(t, n):
        return apply_rope(heads(t, n), cos64, sin64)

    G = A_KV_GROUPS
    o_a = nsa_attention(rot(a_q, A_HEADS), rot(a_kc, G), heads(a_vc, G), rot(a_ks, G), heads(a_vs, G),
                        rot(a_kw, G), heads(a_vw, G), a_g, a_cmp_pos_k, a_cmp_w1_k, a_cmp_w2_k,
                        a_cmp_pos_v, a_cmp_w1_v, a_cmp_w2_v)
    o_b = swa_sink_attention(rot(b_q, B_HEADS), rot(b_k, B_KV_HEADS), heads(b_v, B_KV_HEADS), b_sinks)
    o_c = mla_attention(c_cq, c_ckv, c_kpe, c_q_norm, c_w_q_up, c_kv_norm, c_w_kv_up, cos32, sin32)

    g = jax.nn.sigmoid((h @ w_branch_gate).astype(jnp.float32)).astype(x.dtype)
    g_a, g_b, g_c = jnp.split(g, 3, axis=-1)
    merged = g_a * (o_a @ w_branch_a) + g_b * (o_b @ w_branch_b) + g_c * (o_c @ w_branch_c)
    x = x + merged @ w_out

    h2 = rmsnorm(x, ffn_norm)
    x = x + (jax.nn.silu(h2 @ w_ffn_gate) * (h2 @ w_ffn_up)) @ w_ffn_down

    gate = jax.nn.sigmoid((rmsnorm(x, ple_norm) @ w_ple_gate).astype(jnp.float32)).astype(x.dtype)
    return x + gate * (p_i.astype(x.dtype) @ w_ple_proj)

def first_inputs(seed: int = 0) -> dict:
    key = jax.random.key(seed)
    ks = jax.random.split(key, 32)

    def dense(k, shape, fan_in):
        return jax.random.normal(k, shape, jnp.float32) * (fan_in ** -0.5)

    def gain(k, shape):
        return 1.0 + 0.05 * jax.random.normal(k, shape, jnp.float32)

    L, dh = A_CMP_LEN, HEAD_DIM
    return {
        "x": jax.random.normal(ks[0], (BATCH, SEQ, D_MODEL), jnp.float32),
        "p": jax.random.normal(ks[1], (DEPTH, BATCH, SEQ, PLE_DIM), jnp.float32),
        "positions": jnp.broadcast_to(jnp.arange(SEQ, dtype=jnp.int32)[None, :], (BATCH, SEQ)),
        "mix_norm": gain(ks[2], (DEPTH, D_MODEL)),
        "w_in": dense(ks[3], (DEPTH, D_MODEL, IN_COLS), D_MODEL),
        "a_cmp_pos_k": 0.2 * jax.random.normal(ks[4], (DEPTH, L, dh), jnp.float32),
        "a_cmp_w1_k": dense(ks[5], (DEPTH, L * dh, A_CMP_HIDDEN), L * dh),
        "a_cmp_w2_k": dense(ks[6], (DEPTH, A_CMP_HIDDEN, dh), A_CMP_HIDDEN),
        "a_cmp_pos_v": 0.2 * jax.random.normal(ks[7], (DEPTH, L, dh), jnp.float32),
        "a_cmp_w1_v": dense(ks[8], (DEPTH, L * dh, A_CMP_HIDDEN), L * dh),
        "a_cmp_w2_v": dense(ks[9], (DEPTH, A_CMP_HIDDEN, dh), A_CMP_HIDDEN),
        "b_sinks": 0.5 * jax.random.normal(ks[10], (DEPTH, B_HEADS), jnp.float32),
        "c_q_norm": gain(ks[11], (DEPTH, C_Q_RANK)),
        "c_w_q_up": dense(ks[12], (DEPTH, C_Q_RANK, C_HEADS * (C_NOPE + C_ROPE)), C_Q_RANK),
        "c_kv_norm": gain(ks[13], (DEPTH, C_KV_RANK)),
        "c_w_kv_up": dense(ks[14], (DEPTH, C_KV_RANK, C_HEADS * (C_NOPE + C_V)), C_KV_RANK),
        "w_branch_gate": dense(ks[15], (DEPTH, D_MODEL, 3 * D_MODEL), D_MODEL),
        "w_branch_a": dense(ks[16], (DEPTH, A_OUT, D_MODEL), A_OUT),
        "w_branch_b": dense(ks[17], (DEPTH, B_OUT, D_MODEL), B_OUT),
        "w_branch_c": dense(ks[18], (DEPTH, C_OUT, D_MODEL), C_OUT),
        "w_out": dense(ks[19], (DEPTH, D_MODEL, D_MODEL), D_MODEL),
        "ffn_norm": gain(ks[20], (DEPTH, D_MODEL)),
        "w_ffn_gate": dense(ks[21], (DEPTH, D_MODEL, D_FF), D_MODEL),
        "w_ffn_up": dense(ks[22], (DEPTH, D_MODEL, D_FF), D_MODEL),
        "w_ffn_down": dense(ks[23], (DEPTH, D_FF, D_MODEL), D_FF),
        "ple_norm": gain(ks[24], (DEPTH, D_MODEL)),
        "w_ple_proj": dense(ks[25], (DEPTH, PLE_DIM, D_MODEL), PLE_DIM),
        "w_ple_gate": dense(ks[26], (DEPTH, D_MODEL, D_MODEL), D_MODEL),
        "final_norm": gain(ks[27], (D_MODEL,)),
    }

def first_block(x, p, positions, mix_norm, w_in, a_cmp_pos_k, a_cmp_w1_k, a_cmp_w2_k, a_cmp_pos_v,
              a_cmp_w1_v, a_cmp_w2_v, b_sinks, c_q_norm, c_w_q_up, c_kv_norm, c_w_kv_up, w_branch_gate,
              w_branch_a, w_branch_b, w_branch_c, w_out, ffn_norm, w_ffn_gate, w_ffn_up, w_ffn_down,
              ple_norm, w_ple_proj, w_ple_gate, final_norm):
    rope64 = rope_tables(positions, HEAD_DIM)
    rope32 = rope_tables(positions, C_ROPE)
    for i in range(DEPTH):
        x = hybrid_layer(x, p[i], rope64, rope32, mix_norm[i], w_in[i], a_cmp_pos_k[i], a_cmp_w1_k[i],
                         a_cmp_w2_k[i], a_cmp_pos_v[i], a_cmp_w1_v[i], a_cmp_w2_v[i], b_sinks[i],
                         c_q_norm[i], c_w_q_up[i], c_kv_norm[i], c_w_kv_up[i], w_branch_gate[i],
                         w_branch_a[i], w_branch_b[i], w_branch_c[i], w_out[i], ffn_norm[i],
                         w_ffn_gate[i], w_ffn_up[i], w_ffn_down[i], ple_norm[i], w_ple_proj[i],
                         w_ple_gate[i])
    return rmsnorm(x, final_norm)


MEM_LEN = 256
CONV_WIDTH = 4
SSD_D_INNER = D_MODEL
SSD_HEAD_DIM = 64
SSD_HEADS = SSD_D_INNER // SSD_HEAD_DIM
SSD_GROUPS = 2
SSD_STATE = 128
SSD_XBC = SSD_D_INNER + 2 * SSD_GROUPS * SSD_STATE
SSD_CHUNK = 128
MLSTM_D_INNER = D_MODEL
MLSTM_HEADS = 4
MLSTM_HEAD_DIM = MLSTM_D_INNER // MLSTM_HEADS
MLSTM_CHUNK = 128
EVEN_IN = SSD_D_INNER + SSD_XBC + SSD_HEADS + 2 * MLSTM_D_INNER + 2 * MLSTM_HEADS
HGRN_D_INNER = D_MODEL
HGRN_HEAD_DIM = 128
HGRN_HEADS = HGRN_D_INNER // HGRN_HEAD_DIM
HGRN_CHUNK = 64
XATTN_HEADS = 4
XATTN_HEAD_DIM = D_MODEL // XATTN_HEADS
PEER_HEADS = 8
PEER_N_KEYS = 128
PEER_N_EXPERTS = PEER_N_KEYS * PEER_N_KEYS
PEER_TOPK = 16
PEER_QUERY_DIM = 256
PEER_HALF = PEER_QUERY_DIM // 2
PEER_BLOCK = 128
N_EVEN = (DEPTH + 1) // 2
N_ODD = DEPTH // 2


F32 = jnp.float32

def head_rms_norm(x, w, n_groups):
    shp = x.shape
    x32 = x.astype(F32).reshape(shp[:-1] + (n_groups, shp[-1] // n_groups))
    y = x32 * lax.rsqrt(jnp.mean(x32 * x32, axis=-1, keepdims=True) + EPS)
    return (y.reshape(shp) * w.astype(F32)).astype(x.dtype)

def rms_norm(x, w):
    return head_rms_norm(x, w, 1)

def causal_conv(x, w, b):
    y = lax.conv_general_dilated(x, w[:, None, :], window_strides=(1,), padding=[(w.shape[0] - 1, 0)],
                                 dimension_numbers=('NWC', 'WIO', 'NWC'), feature_group_count=x.shape[-1])
    return y + b

def ssd_mixer(z, xbc, dt_raw, conv_w, conv_b, dt_bias, a_log, d_skip, norm_w):
    bsz, seq, _ = z.shape
    L = SSD_CHUNK; nc = seq // L; G = SSD_GROUPS; E = SSD_HEADS // SSD_GROUPS
    P = SSD_HEAD_DIM; N = SSD_STATE
    xbc = jax.nn.silu(causal_conv(xbc, conv_w, conv_b))
    xs = xbc[..., :SSD_D_INNER].astype(F32).reshape(bsz, nc, L, G, E, P)
    bm = xbc[..., SSD_D_INNER:SSD_D_INNER + G * N].astype(F32).reshape(bsz, nc, L, G, N)
    cm = xbc[..., SSD_D_INNER + G * N:].astype(F32).reshape(bsz, nc, L, G, N)
    dt = jax.nn.softplus(dt_raw.astype(F32) + dt_bias.astype(F32)).reshape(bsz, nc, L, G, E)
    a = -jnp.exp(a_log.astype(F32)).reshape(G, E)
    cs = jnp.cumsum(jnp.transpose(dt * a, (0, 3, 4, 1, 2)), axis=-1)
    x_dt = xs * dt[..., None]
    causal = jnp.tril(jnp.ones((L, L), dtype=bool))
    decay = jnp.exp(jnp.where(causal, cs[..., :, None] - cs[..., None, :], -jnp.inf))
    cb = jnp.einsum('bclgn,bcsgn->bgcls', cm, bm)
    y_diag = jnp.einsum('bgcls,bgecls,bcsgep->bclgep', cb, decay, x_dt)
    decay_to_end = jnp.exp(cs[..., -1:] - cs)
    chunk_states = jnp.einsum('bcsgn,bgecs,bcsgep->bcgepn', bm, decay_to_end, x_dt)
    chunk_decay = jnp.exp(cs[..., -1])

    def step(state, inp):
        s_c, a_c = inp
        return a_c[..., None, None] * state + s_c, state

    init = jnp.zeros((bsz, G, E, P, N), F32)
    _, prev = lax.scan(step, init, (jnp.moveaxis(chunk_states, 1, 0), jnp.moveaxis(chunk_decay, 3, 0)))
    y_off = jnp.einsum('bclgn,cbgepn,bgecl->bclgep', cm, prev, jnp.exp(cs))
    y = y_diag + y_off + xs * d_skip.astype(F32).reshape(G, E, 1)
    y = y.reshape(bsz, seq, SSD_D_INNER) * jax.nn.silu(z.astype(F32))
    return head_rms_norm(y, norm_w, G).astype(z.dtype)

def mlstm_mixer(xm, og, ig, fg, conv_w, conv_b, wq, wk, wv, i_bias, f_bias, norm_w):
    bsz, seq, _ = xm.shape
    H = MLSTM_HEADS; Dh = MLSTM_HEAD_DIM; L = MLSTM_CHUNK; nc = seq // L
    xc = jax.nn.silu(causal_conv(xm, conv_w, conv_b))

    def heads(t, w):
        y = jnp.einsum('bshd,hde->bhse', t.reshape(bsz, seq, H, Dh), w)
        return y.astype(F32).reshape(bsz, H, nc, L, Dh)

    q = heads(xc, wq)
    k = heads(xc, wk) * (Dh ** -0.5)
    v = heads(xm, wv)
    i_t = jnp.transpose(ig.astype(F32) + i_bias.astype(F32), (0, 2, 1)).reshape(bsz, H, nc, L)
    logf = jnp.transpose(jax.nn.log_sigmoid(fg.astype(F32) + f_bias.astype(F32)), (0, 2, 1)).reshape(bsz, H, nc, L)
    bcum = jnp.cumsum(logf, axis=-1)
    causal = jnp.tril(jnp.ones((L, L), dtype=bool))
    dlog = jnp.where(causal, bcum[..., :, None] - bcum[..., None, :] + i_t[..., None, :], -jnp.inf)
    m_intra = jnp.max(dlog, axis=-1)
    g_end = bcum[..., -1:] - bcum + i_t
    m_chunk = jnp.max(g_end, axis=-1)
    w_end = jnp.exp(g_end - m_chunk[..., None])
    c_local = jnp.einsum('bhcs,bhcsd,bhcse->bhcde', w_end, k, v)
    n_local = jnp.einsum('bhcs,bhcsd->bhcd', w_end, k)
    b_end = bcum[..., -1]

    def step(carry, inp):
        c_st, n_st, m_st = carry
        be, mc, cl, nl = inp
        m_new = jnp.maximum(be + m_st, mc)
        a_old = jnp.exp(be + m_st - m_new)
        a_new = jnp.exp(mc - m_new)
        c_new = a_old[..., None, None] * c_st + a_new[..., None, None] * cl
        n_new = a_old[..., None] * n_st + a_new[..., None] * nl
        return (c_new, n_new, m_new), (c_st, n_st, m_st)

    init = (jnp.zeros((bsz, H, Dh, Dh), F32), jnp.zeros((bsz, H, Dh), F32), jnp.zeros((bsz, H), F32))
    mv = lambda t: jnp.moveaxis(t, 2, 0)
    _, (c_prev, n_prev, m_prev) = lax.scan(step, init, (mv(b_end), mv(m_chunk), mv(c_local), mv(n_local)))
    m_prev_b = jnp.moveaxis(m_prev, 0, 2)[..., None]
    m_t = jnp.maximum(bcum + m_prev_b, m_intra)
    a_t = jnp.exp(bcum + m_prev_b - m_t)
    qk = jnp.einsum('bhcld,bhcsd->bhcls', q, k) * jnp.exp(dlog - m_t[..., None])
    num = a_t[..., None] * jnp.einsum('bhcld,cbhde->bhcle', q, c_prev) + jnp.einsum('bhcls,bhcse->bhcle', qk, v)
    den = a_t * jnp.einsum('bhcld,cbhd->bhcl', q, n_prev) + jnp.sum(qk, axis=-1)
    hid = num / jnp.maximum(jnp.abs(den), jnp.exp(-m_t))[..., None]
    hid = jnp.transpose(hid, (0, 2, 3, 1, 4)).reshape(bsz, seq, H * Dh)
    hid = head_rms_norm(hid, norm_w, H) * jax.nn.sigmoid(og.astype(F32))
    return hid.astype(xm.dtype)

def hgrn2_mixer(uq, uf, ui, ug, lb, norm_w):
    bsz, seq, _ = uq.shape
    H = HGRN_HEADS; Dk = HGRN_HEAD_DIM; L = HGRN_CHUNK; nc = seq // L

    def heads(t):
        return jnp.transpose(t.reshape(bsz, nc, L, H, -1), (0, 3, 1, 2, 4))

    uf32 = uf.astype(F32)
    lb = lb.astype(F32)
    logf = heads(jnp.log(lb + (1.0 - lb) * jax.nn.sigmoid(uf32)))
    k = heads((1.0 - lb) * jax.nn.sigmoid(-uf32))
    q = heads(jax.nn.silu(uq.astype(F32)))
    v = heads(ui.astype(F32))
    gc = jnp.cumsum(logf, axis=3)
    g_ref = gc[:, :, :, L // 2:L // 2 + 1, :]
    causal = jnp.tril(jnp.ones((L, L), dtype=bool))
    att = jnp.einsum('bhcld,bhcsd->bhcls', q * jnp.exp(gc - g_ref), k * jnp.exp(g_ref - gc))
    att = jnp.where(causal, att, 0.0)
    o = jnp.einsum('bhcls,bhcse->bhcle', att, v)
    s_local = jnp.einsum('bhcsd,bhcse->bhcde', k * jnp.exp(gc[..., -1:, :] - gc), v)
    chunk_decay = jnp.exp(gc[..., -1, :])

    def step(state, inp):
        a_c, s_c = inp
        return a_c[..., :, None] * state + s_c, state

    init = jnp.zeros((bsz, H, Dk, Dk), F32)
    _, s_prev = lax.scan(step, init, (jnp.moveaxis(chunk_decay, 2, 0), jnp.moveaxis(s_local, 2, 0)))
    o = o + jnp.einsum('bhcld,cbhde->bhcle', q * jnp.exp(gc), s_prev)
    o = jnp.transpose(o, (0, 2, 3, 1, 4)).reshape(bsz, seq, HGRN_D_INNER)
    o = head_rms_norm(o, norm_w, H) * jax.nn.silu(ug.astype(F32))
    return o.astype(uq.dtype)

def even_mixer(hn, w_in, w_out, ssd_conv_w, ssd_conv_b, ssd_dt_bias, ssd_a_log, ssd_d_skip, ssd_norm,
               ml_conv_w, ml_conv_b, ml_wq, ml_wk, ml_wv, ml_i_bias, ml_f_bias, ml_norm):
    proj = hn @ w_in
    o1 = SSD_D_INNER
    o2 = o1 + SSD_XBC
    o3 = o2 + SSD_HEADS
    o4 = o3 + MLSTM_D_INNER
    o5 = o4 + MLSTM_D_INNER
    o6 = o5 + MLSTM_HEADS
    z, xbc, dt_raw, xm, og, ig, fg = jnp.split(proj, [o1, o2, o3, o4, o5, o6], axis=-1)
    y_a = ssd_mixer(z, xbc, dt_raw, ssd_conv_w, ssd_conv_b, ssd_dt_bias, ssd_a_log, ssd_d_skip, ssd_norm)
    y_b = mlstm_mixer(xm, og, ig, fg, ml_conv_w, ml_conv_b, ml_wq, ml_wk, ml_wv, ml_i_bias, ml_f_bias, ml_norm)
    return jnp.concatenate([y_a, y_b], axis=-1).astype(hn.dtype) @ w_out

def odd_mixer(hn, w_in, w_out, lb, norm_w):
    uq, uf, ui, ug = jnp.split(hn @ w_in, 4, axis=-1)
    return hgrn2_mixer(uq, uf, ui, ug, lb, norm_w).astype(hn.dtype) @ w_out

def mem_cross_attention(hn, mem_n, wq, wkv, wo):
    bsz, seq, _ = hn.shape
    q = (hn @ wq).reshape(bsz, seq, XATTN_HEADS, XATTN_HEAD_DIM)
    k, v = jnp.split(mem_n @ wkv, 2, axis=-1)
    k = k.reshape(bsz, -1, XATTN_HEADS, XATTN_HEAD_DIM)
    v = v.reshape(bsz, -1, XATTN_HEADS, XATTN_HEAD_DIM)
    scores = jnp.einsum('bshd,bmhd->bhsm', q, k).astype(F32) * (XATTN_HEAD_DIM ** -0.5)
    p = jax.nn.softmax(scores, axis=-1).astype(v.dtype)
    o = jnp.einsum('bhsm,bmhd->bshd', p, v).reshape(bsz, seq, D_MODEL)
    return o @ wo

def peer_ffn(hn, wq, subkeys, u_tab, v_tab):
    bsz, seq, _ = hn.shape
    T = bsz * seq
    xt = hn.reshape(T, D_MODEL)
    q = (xt @ wq).reshape(T, PEER_HEADS, 2, PEER_HALF)
    s = jnp.einsum('thpd,hpkd->thpk', q, subkeys).astype(F32)
    s1, i1 = lax.top_k(s[:, :, 0], PEER_TOPK)
    s2, i2 = lax.top_k(s[:, :, 1], PEER_TOPK)
    cand = (s1[..., :, None] + s2[..., None, :]).reshape(T, PEER_HEADS, PEER_TOPK * PEER_TOPK)
    cand_idx = (i1[..., :, None] * PEER_N_KEYS + i2[..., None, :]).reshape(T, PEER_HEADS, PEER_TOPK * PEER_TOPK)
    top_s, pos = lax.top_k(cand, PEER_TOPK)
    idx = jnp.take_along_axis(cand_idx, pos, axis=-1)
    gate = jax.nn.softmax(top_s, axis=-1)
    nb = T // PEER_BLOCK

    def expert_block(args):
        xb, ib, gb = args
        ub = u_tab[ib]
        vb = v_tab[ib]
        act = jax.nn.gelu(jnp.einsum('td,thkd->thk', xb, ub).astype(F32), approximate=False)
        return jnp.einsum('thk,thkd->td', (gb * act).astype(vb.dtype), vb)

    out = lax.map(expert_block, (xt.reshape(nb, PEER_BLOCK, D_MODEL),
                                 idx.reshape(nb, PEER_BLOCK, PEER_HEADS, PEER_TOPK),
                                 gate.reshape(nb, PEER_BLOCK, PEER_HEADS, PEER_TOPK)))
    return out.reshape(bsz, seq, D_MODEL).astype(hn.dtype)

def second_inputs(seed: int = 0) -> dict:
    key = jax.random.key(seed)
    ks = jax.random.split(key, 40)
    nrm = lambda k, shape, scale: jax.random.normal(k, shape, F32) * scale
    gain = lambda k, shape: 1.0 + 0.02 * jax.random.normal(k, shape, F32)
    dt = jnp.exp(jax.random.uniform(ks[10], (N_EVEN, SSD_HEADS), F32) * (np.log(0.1) - np.log(0.001)) + np.log(0.001))
    f_bias = jnp.linspace(3.0, 6.0, MLSTM_HEADS, dtype=F32)[None, :] + 0.1 * jax.random.normal(ks[21], (N_EVEN, MLSTM_HEADS), F32)
    return {
        'x': nrm(ks[0], (BATCH, SEQ, D_MODEL), 1.0),
        'mem': nrm(ks[1], (BATCH, MEM_LEN, D_MODEL), 1.0),
        'norm_mix': gain(ks[2], (DEPTH, D_MODEL)),
        'norm_xattn': gain(ks[3], (DEPTH, D_MODEL)),
        'norm_mem': gain(ks[4], (DEPTH, D_MODEL)),
        'norm_ffn': gain(ks[5], (DEPTH, D_MODEL)),
        'norm_final': gain(ks[6], (D_MODEL,)),
        'ev_w_in': nrm(ks[7], (N_EVEN, D_MODEL, EVEN_IN), D_MODEL ** -0.5),
        'ev_w_out': nrm(ks[8], (N_EVEN, SSD_D_INNER + MLSTM_D_INNER, D_MODEL), (SSD_D_INNER + MLSTM_D_INNER) ** -0.5),
        'ssd_conv_w': nrm(ks[9], (N_EVEN, CONV_WIDTH, SSD_XBC), CONV_WIDTH ** -0.5),
        'ssd_conv_b': nrm(ks[11], (N_EVEN, SSD_XBC), 0.02),
        'ssd_dt_bias': dt + jnp.log(-jnp.expm1(-dt)),
        'ssd_a_log': jnp.log(jax.random.uniform(ks[12], (N_EVEN, SSD_HEADS), F32, 1.0, 16.0)),
        'ssd_d_skip': 1.0 + 0.1 * jax.random.normal(ks[13], (N_EVEN, SSD_HEADS), F32),
        'ssd_norm': gain(ks[14], (N_EVEN, SSD_D_INNER)),
        'ml_conv_w': nrm(ks[15], (N_EVEN, CONV_WIDTH, MLSTM_D_INNER), CONV_WIDTH ** -0.5),
        'ml_conv_b': nrm(ks[16], (N_EVEN, MLSTM_D_INNER), 0.02),
        'ml_wq': nrm(ks[17], (N_EVEN, MLSTM_HEADS, MLSTM_HEAD_DIM, MLSTM_HEAD_DIM), MLSTM_HEAD_DIM ** -0.5),
        'ml_wk': nrm(ks[18], (N_EVEN, MLSTM_HEADS, MLSTM_HEAD_DIM, MLSTM_HEAD_DIM), MLSTM_HEAD_DIM ** -0.5),
        'ml_wv': nrm(ks[19], (N_EVEN, MLSTM_HEADS, MLSTM_HEAD_DIM, MLSTM_HEAD_DIM), MLSTM_HEAD_DIM ** -0.5),
        'ml_i_bias': nrm(ks[20], (N_EVEN, MLSTM_HEADS), 0.1),
        'ml_f_bias': f_bias,
        'ml_norm': gain(ks[22], (N_EVEN, MLSTM_D_INNER)),
        'od_w_in': nrm(ks[23], (N_ODD, D_MODEL, 4 * HGRN_D_INNER), D_MODEL ** -0.5),
        'od_w_out': nrm(ks[24], (N_ODD, HGRN_D_INNER, D_MODEL), HGRN_D_INNER ** -0.5),
        'hgrn_lb_logits': nrm(ks[25], (DEPTH, HGRN_D_INNER), 0.1),
        'hgrn_norm': gain(ks[26], (N_ODD, HGRN_D_INNER)),
        'xa_wq': nrm(ks[27], (DEPTH, D_MODEL, D_MODEL), D_MODEL ** -0.5),
        'xa_wkv': nrm(ks[28], (DEPTH, D_MODEL, 2 * D_MODEL), D_MODEL ** -0.5),
        'xa_wo': nrm(ks[29], (DEPTH, D_MODEL, D_MODEL), D_MODEL ** -0.5),
        'peer_wq': nrm(ks[30], (DEPTH, D_MODEL, PEER_HEADS * PEER_QUERY_DIM), D_MODEL ** -0.5),
        'peer_subkeys': nrm(ks[31], (DEPTH, PEER_HEADS, 2, PEER_N_KEYS, PEER_HALF), PEER_HALF ** -0.5),
        'peer_u': nrm(ks[32], (DEPTH, PEER_N_EXPERTS, D_MODEL), D_MODEL ** -0.5),
        'peer_v': nrm(ks[33], (DEPTH, PEER_N_EXPERTS, D_MODEL), (PEER_HEADS * PEER_TOPK) ** -0.5),
    }

def second_block(x, mem, norm_mix, norm_xattn, norm_mem, norm_ffn, norm_final,
              ev_w_in, ev_w_out, ssd_conv_w, ssd_conv_b, ssd_dt_bias, ssd_a_log, ssd_d_skip, ssd_norm,
              ml_conv_w, ml_conv_b, ml_wq, ml_wk, ml_wv, ml_i_bias, ml_f_bias, ml_norm,
              od_w_in, od_w_out, hgrn_lb_logits, hgrn_norm,
              xa_wq, xa_wkv, xa_wo,
              peer_wq, peer_subkeys, peer_u, peer_v):
    lb_cum = jnp.cumsum(jax.nn.softmax(hgrn_lb_logits.astype(F32), axis=0), axis=0)
    h = x
    for layer in range(DEPTH):
        hn = rms_norm(h, norm_mix[layer])
        if layer % 2 == 0:
            e = layer // 2
            mix = even_mixer(hn, ev_w_in[e], ev_w_out[e], ssd_conv_w[e], ssd_conv_b[e], ssd_dt_bias[e],
                             ssd_a_log[e], ssd_d_skip[e], ssd_norm[e], ml_conv_w[e], ml_conv_b[e],
                             ml_wq[e], ml_wk[e], ml_wv[e], ml_i_bias[e], ml_f_bias[e], ml_norm[e])
        else:
            o = layer // 2
            mix = odd_mixer(hn, od_w_in[o], od_w_out[o], lb_cum[layer - 1], hgrn_norm[o])
        h = h + mix.astype(h.dtype)
        mem_n = rms_norm(mem, norm_mem[layer])
        h = h + mem_cross_attention(rms_norm(h, norm_xattn[layer]), mem_n, xa_wq[layer], xa_wkv[layer], xa_wo[layer]).astype(h.dtype)
        h = h + peer_ffn(rms_norm(h, norm_ffn[layer]), peer_wq[layer], peer_subkeys[layer], peer_u[layer], peer_v[layer]).astype(h.dtype)
    return rms_norm(h, norm_final)


def setup_inputs(seed=0):
    out = dict(first_inputs(seed))
    for name, value in second_inputs(seed + 1).items():
        if name != "x":
            out[name + "_2"] = value
    return out


def reference(
    x, p, positions, mix_norm, w_in, a_cmp_pos_k, a_cmp_w1_k, a_cmp_w2_k, a_cmp_pos_v,
    a_cmp_w1_v, a_cmp_w2_v, b_sinks, c_q_norm, c_w_q_up, c_kv_norm, c_w_kv_up, w_branch_gate,
    w_branch_a, w_branch_b, w_branch_c, w_out, ffn_norm, w_ffn_gate, w_ffn_up, w_ffn_down,
    ple_norm, w_ple_proj, w_ple_gate, final_norm, mem_2, norm_mix_2, norm_xattn_2, norm_mem_2,
    norm_ffn_2, norm_final_2, ev_w_in_2, ev_w_out_2, ssd_conv_w_2, ssd_conv_b_2, ssd_dt_bias_2,
    ssd_a_log_2, ssd_d_skip_2, ssd_norm_2, ml_conv_w_2, ml_conv_b_2, ml_wq_2, ml_wk_2, ml_wv_2,
    ml_i_bias_2, ml_f_bias_2, ml_norm_2, od_w_in_2, od_w_out_2, hgrn_lb_logits_2, hgrn_norm_2,
    xa_wq_2, xa_wkv_2, xa_wo_2, peer_wq_2, peer_subkeys_2, peer_u_2, peer_v_2,
):
    x = first_block(
        x, p, positions, mix_norm, w_in, a_cmp_pos_k, a_cmp_w1_k, a_cmp_w2_k, a_cmp_pos_v,
        a_cmp_w1_v, a_cmp_w2_v, b_sinks, c_q_norm, c_w_q_up, c_kv_norm, c_w_kv_up,
        w_branch_gate, w_branch_a, w_branch_b, w_branch_c, w_out, ffn_norm, w_ffn_gate,
        w_ffn_up, w_ffn_down, ple_norm, w_ple_proj, w_ple_gate, final_norm,
    )
    return second_block(
        x, mem_2, norm_mix_2, norm_xattn_2, norm_mem_2, norm_ffn_2, norm_final_2, ev_w_in_2,
        ev_w_out_2, ssd_conv_w_2, ssd_conv_b_2, ssd_dt_bias_2, ssd_a_log_2, ssd_d_skip_2,
        ssd_norm_2, ml_conv_w_2, ml_conv_b_2, ml_wq_2, ml_wk_2, ml_wv_2, ml_i_bias_2,
        ml_f_bias_2, ml_norm_2, od_w_in_2, od_w_out_2, hgrn_lb_logits_2, hgrn_norm_2, xa_wq_2,
        xa_wkv_2, xa_wo_2, peer_wq_2, peer_subkeys_2, peer_u_2, peer_v_2,
    )


_drawn_inputs = setup_inputs


def setup_inputs(seed=0):
    import zlib

    import numpy as np

    out = dict(_drawn_inputs(seed))
    spreads = {}
    factors = {'a_cmp_pos_k': 5.27,
     'b_sinks': 5.005,
     'c_q_norm': 5.286,
     'c_kv_norm': 3.265,
     'ple_norm': 3.438,
     'norm_xattn_2': 8.0,
     'norm_mem_2': 8.0,
     'norm_ffn_2': 7.651,
     'norm_final_2': 8.698,
     'ssd_conv_b_2': 3.256,
     'ssd_norm_2': 4.419,
     'ml_conv_b_2': 4.407,
     'ml_i_bias_2': 64.0,
     'ml_norm_2': 7.428,
     'hgrn_lb_logits_2': 8.0,
     'hgrn_norm_2': 6.205}
    for name, (base, spread) in spreads.items():
        noise = np.random.default_rng([zlib.crc32(name.encode()), seed]).standard_normal(out[name].shape)
        drawn = base * np.exp(spread * noise) if base else spread * noise
        out[name] = __import__('jax').numpy.asarray(drawn.astype(out[name].dtype))
    for name, factor in factors.items():
        out[name] = (out[name] * factor).astype(out[name].dtype)
    return out
```

```python
from contextlib import ExitStack, contextmanager

import numpy as np
import concourse.bass as bass
from concourse import mybir

F32 = mybir.dt.float32
I32 = mybir.dt.int32
U32 = mybir.dt.uint32
ALU = mybir.AluOpType
ACT = mybir.ActivationFunctionType
AX = mybir.AxisListType.X

P = 128
D = 1024
KT = D // P
T = 256
MT = T // P
DEPTH = 2
EPS = 1e-6
NEG = -1e30
HD = 64
BLK = 512
CHUNK_BLOCKS = 4
CHUNK = BLK * CHUNK_BLOCKS
SLOTS = 8
N_CMP = (T - 32) // 16 + 1
D_FF = 2816
FF_T = D_FF // P
XBC_T = 12
PE_HEADS, PE_KEYS, PE_TOP = 8, 128, 16
SLOTS_PER_TOKEN = PE_HEADS * PE_TOP
GATHER = 4
N_GATHER = SLOTS_PER_TOKEN // GATHER



def columns(*sizes):
    at, out = 0, {}
    for name, n in sizes:
        out[name] = (at, n)
        at += n
    return out, at


P1, P1_W = columns(("mix_norm", KT), ("ffn_norm", KT), ("ple_norm", KT), ("cq_norm", 2), ("ckv_norm", 2),
                   ("w_small", KT * 56), ("w2k", 2 * HD), ("w2v", 2 * HD), ("posT", 32), ("sinks", 8))
P2, P2_W = columns(("norm_mix", KT), ("norm_xattn", KT), ("norm_mem", KT), ("norm_ffn", KT),
                   ("w_small", KT * 24), ("small_bias", 24), ("a_log", 16), ("d_skip", 16),
                   ("conv_w", XBC_T * 4), ("conv_b", XBC_T), ("ssd_norm", KT),
                   ("ml_conv_w", KT * 4), ("ml_conv_b", KT), ("ml_norm", KT),
                   ("lb_logits", DEPTH * KT), ("hgrn_norm", KT))
PAR_W = max(P1_W, P2_W)


STREAM_1 = [("rot0", 8, 1), ("rot1", 8, 1), ("rot2", 8, 1), ("values", 8, 1), ("latents", 8, 1),
            ("gates", 8, 6), ("cmp_w1", 16, 1), ("q_up", 2, 2), ("kv_up", 2, 2),
            ("branch_a", 4, 2), ("branch_b", 4, 2), ("branch_c", 4, 2), ("w_out", 8, 2),
            ("ffn_in", 8, 11), ("ffn_down", FF_T, 2), ("ple_gate", 8, 2), ("ple_proj", 2, 2)]
ATTEND_2 = [("xa_q", 8, 2), ("xa_k", 8, 2), ("xa_v", 8, 2), ("xa_o", 8, 2), ("peer_q", 8, 4), ("subkeys", 4, 1)]
STREAM_2 = ([("ssd_z", 8, 2), ("xbc", 8, 3), ("xm", 8, 2), ("og", 8, 2), ("ml_wq", 4, 1), ("ml_wk", 4, 1),
             ("ml_wv", 4, 1), ("ev_out", 16, 2)] + ATTEND_2
            + [("hgrn_f", 8, 2), ("hgrn_q", 8, 2), ("hgrn_v", 8, 2), ("hgrn_g", 8, 2), ("od_out", 8, 2)] + ATTEND_2)


def chunks_of(k, n):
    return -(-k * n // CHUNK_BLOCKS)


CHUNKS_1 = sum(chunks_of(k, n) for _, k, n in STREAM_1)
CHUNKS_2 = sum(chunks_of(k, n) for _, k, n in STREAM_2)
VIRTUAL_1 = -(-CHUNKS_1 // SLOTS) * SLOTS
USES_1 = [sum(1 for v in range(CHUNKS_1) if v % SLOTS == s) for s in range(SLOTS)]


def bc(ap, shape):
    return ap.to_broadcast(list(shape))


class Chain:

    def __init__(self, eng, sem):
        self.eng, self.sem, self.n = eng, sem, 0

    def note(self, ins):
        ins.then_inc(self.sem, 1)
        self.n += 1

    def sync(self):
        self.eng.wait_ge(self.sem, self.n)

    def __call__(self, ins):
        self.note(ins)
        self.sync()


class Linear:

    def __init__(self, k, n, chunk0, group0):
        self.k, self.n, self.chunk0, self.group0 = k, n, chunk0, group0

    def chunk_ends(self, block):
        return block % CHUNK_BLOCKS == CHUNK_BLOCKS - 1 or block == self.k * self.n - 1


class Phase:

    def __init__(self, kern, name, stack):
        self.kern, self.name, self.stack, self.sems = kern, name, stack, {}
        self.first_chunk, self.groups = kern.next_chunk, 0

    def sem(self, what):
        if what not in self.sems:
            self.sems[what] = self.kern.nc.alloc_semaphore(name=f"{self.name}_{what}_{self.kern.n_phases}")
        return self.sems[what]

    def linear(self, name, grouped=True):
        k = self.kern
        want, kt, n = k.stream[k.stream_at]
        assert want == name, (want, name)
        lin = Linear(kt, n, k.next_chunk, self.groups)
        k.stream_at += 1
        k.next_chunk += chunks_of(kt, n)
        if grouped:
            self.groups += n
        return lin


class Kernel:
    def __init__(self, nc, dram, stack):
        self.nc, self.dram, self.stack = nc, dram, stack
        self.n_phases = 0
        self.stream, self.stream_at, self.next_chunk = STREAM_1, 0, 0
        self.layer = None

        def sb(name, shape, dt=F32):
            return stack.enter_context(nc.sbuf_tensor(name, shape, dt))

        self.ring = sb("ring", [P, SLOTS, CHUNK])
        self.x = sb("x", [P, MT, D])
        self.hT = sb("hT", [P, KT, T])
        self.par = sb("par", [P, PAR_W])
        self.gain_row = sb("gain_row", [P, D])
        self.ident = sb("ident", [P, P])
        self.ones = sb("ones", [P, P])
        self.causal = sb("causal", [P, 2 * P])
        self.band = sb("band", [P, 2 * P])
        self.cmp_mask = sb("cmp_mask", [P, MT, N_CMP])
        self.row_valid = sb("row_valid", [P, MT])
        self.upper = sb("upper", [P, P])
        self.upper_add = sb("upper_add", [P, P])
        self.chunk_upper = sb("chunk_upper", [P, P])
        self.rope = sb("rope", [P, 2, MT, 48])
        self.stat = sb("stat", [P, 8, 64])
        self.stage_index = sb("stage_index", [P, 2, GATHER], U32)
        self.arena = sb("arena", [P, 28600])
        self.ps = stack.enter_context(nc.psum_tensor("ps", [P, 8, BLK], F32))
        self.ring_full = [stack.enter_context(nc.semaphore(f"ring_full{s}")) for s in range(SLOTS)]
        self.gathered = [[stack.enter_context(nc.semaphore(f"gathered{b}_{e}")) for e in range(GATHER)] for b in range(2)]
        self.ring_free = [stack.enter_context(nc.semaphore(f"ring_free{s}")) for s in range(SLOTS)]


    def at(self, start, *shape):
        n = int(np.prod(shape))
        assert start + n <= 28600, (start, shape)
        view = self.arena[:, start:start + n]
        if len(shape) > 1:
            names = "abcde"[:len(shape)]
            view = view.rearrange(f"p ({' '.join(names)}) -> p {' '.join(names)}",
                                  **{c: s for c, s in zip(names[1:], shape[1:])})
        return view, start + n

    def p1(self, name, n=None):
        a, w = P1[name]
        v = self.par[:, a:a + w]
        return v if n is None else v.rearrange("p (a b) -> p a b", a=n)

    def p2(self, name, n=None):
        a, w = P2[name]
        v = self.par[:, a:a + w]
        return v if n is None else v.rearrange("p (a b) -> p a b", a=n)


    @contextmanager
    def phase(self, name):
        with ExitStack() as stack:
            ph = Phase(self, name, stack)
            yield ph
        self.n_phases += 1

    @contextmanager
    def engines(self, ph):
        nc = self.nc
        with nc.Block(no_gpsimd_drain=True) as block:
            yield block
        for s in ph.sems.values():
            nc.gpsimd.sem_clear(s)
        nc.all_engine_barrier()
        for s in ph.sems.values():
            nc.release_semaphore(s)


    def uses_before(self, v):
        s = v % SLOTS
        if self.layer is not None:
            return self.layer * USES_1[s] + v // SLOTS
        return (DEPTH * USES_1[s] if self.stream is STREAM_2 else 0) + v // SLOTS

    def wait_chunk(self, eng, v):
        uses = self.uses_before(v)
        eng.wait_ge(self.ring_full[v % SLOTS], uses * 16 + 16)

    def load_ahead(self, sp, ph):
        for v in range(ph.first_chunk, self.next_chunk):
            a = v + SLOTS
            s = a % SLOTS
            if self.layer is not None:
                if a < CHUNKS_1:
                    source, uses = self.layer * CHUNKS_1 + a, self.uses_before(a)
                elif a >= VIRTUAL_1:
                    source, uses = (self.layer + 1) * CHUNKS_1 + (a - VIRTUAL_1), (self.layer + 1) * USES_1[s]
                else:
                    continue
            elif a < CHUNKS_2:
                source, uses = DEPTH * CHUNKS_1 + a, self.uses_before(a)
            else:
                continue
            sp.wait_ge(self.ring_free[s], uses)
            sp.dma_start(self.ring[:, s, :], self.dram["stream"][bass.ds(source, 1)].rearrange("a p c -> (a p) c")
                         ).then_inc(self.ring_full[s], 16)
        if self.layer is not None and self.next_chunk == CHUNKS_1:
            for a in range(max(CHUNKS_1 + SLOTS, VIRTUAL_1), VIRTUAL_1 + SLOTS):
                s = a % SLOTS
                sp.wait_ge(self.ring_free[s], (self.layer + 1) * USES_1[s])
                sp.dma_start(self.ring[:, s, :], self.dram["stream"][
                    bass.ds((self.layer + 1) * CHUNKS_1 + (a - VIRTUAL_1), 1)].rearrange("a p c -> (a p) c")
                             ).then_inc(self.ring_full[s], 16)


    def linear_tok(self, pe, ph, lin, xT, widths=None):
        self._linear(pe, ph, lin, xT, False, widths)

    def linear_T(self, pe, ph, lin, xT):
        self._linear(pe, ph, lin, xT, True, None)

    def _linear(self, pe, ph, lin, xT, feature_major, widths):
        for n in range(lin.n):
            g = lin.group0 + n
            pair = g % 2
            if g >= 2:
                pe.wait_ge(ph.sem(f"pair_free{pair}"), g // 2)
            for k in range(lin.k):
                block = n * lin.k + k
                v = lin.chunk0 + block // CHUNK_BLOCKS
                if block % CHUNK_BLOCKS == 0:
                    self.wait_chunk(pe, v)
                w = self.ring[:, v % SLOTS, (block % CHUNK_BLOCKS) * BLK:(block % CHUNK_BLOCKS + 1) * BLK]
                if feature_major:
                    for f in range(4):
                        last = pe.matmul(self.ps[:, 2 * pair + f // 2, (f % 2) * T:(f % 2 + 1) * T],
                                         w[:, f * P:(f + 1) * P], xT[:, k, :],
                                         start=(k == 0 and f % 2 == 0), stop=(k == lin.k - 1 and f % 2 == 1),
                                         skip_group_check=True)
                else:
                    width = widths[n] if widths else BLK
                    for m in range(MT):
                        last = pe.matmul(self.ps[:, 2 * pair + m, 0:width], xT[:, k, m * P:(m + 1) * P],
                                         w[:, 0:width], start=(k == 0), stop=(k == lin.k - 1))
                if lin.chunk_ends(block) and k < lin.k - 1:
                    last.then_inc(self.ring_free[v % SLOTS], 1)
            last.then_inc(ph.sem("pair_done"), 1)

    def take(self, eng, ph, lin, n, release=True):
        g = lin.group0 + n
        eng.wait_ge(ph.sem("pair_done"), g + 1)
        block = n * lin.k + lin.k - 1
        if release and lin.chunk_ends(block):
            eng.sem_inc(self.ring_free[(lin.chunk0 + block // CHUNK_BLOCKS) % SLOTS], 1)
        pair = g % 2
        return self.ps[:, 2 * pair:2 * pair + 2, :], ph.sem(f"pair_free{pair}")


    def transposes(self, pe, ph, name, groups, banks):
        for i, group in enumerate(groups):
            if i >= len(banks):
                pe.wait_ge(ph.sem(f"{name}_copied"), i - len(banks) + 1)
            for src, col in group:
                p, f = src.shape[0], int(np.prod(src.shape[1:]))
                last = pe.transpose(self.ps[0:f, banks[i % len(banks)], col:col + p], src, self.ident[0:p, 0:p])
            last.then_inc(ph.sem(f"{name}_turned"), 1)

    def turned(self, eng, ph, name, i, banks):
        eng.wait_ge(ph.sem(f"{name}_turned"), i + 1)
        return self.ps[:, banks[i % len(banks)], :]


    def rstd_vector_before(self, dve, ph, link, ss, ms, width, tag=""):
        ins = dve.tensor_scalar(ms, ss, 1.0 / width, EPS, ALU.mult, ALU.add)
        ins.then_inc(ph.sem("mean_ready" + tag), 1)

    def rstd_scalar(self, act, ph, link, ms, y, tag="", turn=1):
        act.wait_ge(ph.sem("mean_ready" + tag), turn)
        link(act.activation(y, ms, ACT.Ln))
        act.activation(y, y, ACT.Exp, scale=-0.5).then_inc(ph.sem("rough_ready" + tag), 1)

    def rstd_vector_after(self, dve, ph, link, ms, y, t, tag="", turn=1):
        dve.wait_ge(ph.sem("rough_ready" + tag), turn)
        link(dve.tensor_tensor(t, y, y, ALU.mult))
        link(dve.tensor_tensor(t, t, ms, ALU.mult))
        link(dve.tensor_scalar(t, t, -0.5, 1.5, ALU.mult, ALU.add))
        link(dve.tensor_tensor(y, y, t, ALU.mult))


def feature_groups(tile, first, count):
    return [[(tile[:, m, (first + 2 * j + i) * P:(first + 2 * j + i + 1) * P], i * T + m * P)
             for i in range(2) for m in range(MT)] for j in range(count // 2)]


def norm_phase(k, name, src, gain, dst, loads=None, out_tok=None, source=None, scratch=0):
    with k.phase(name) as ph:
        junk, a = k.at(scratch, D)
        xn, _ = k.at(a, MT, D)
        ss, ms, y, t = (k.stat[:, i, 0:MT] for i in range(4))
        banks = [4, 5, 6, 7]
        jobs = feature_groups(xn, 0, KT) if dst is not None else []
        n_loads = len(loads or []) + (source is not None)
        with k.engines(ph) as block:
            @block.sync
            def _(sp):
                if source is not None:
                    sp.dma_start(src[:], source).then_inc(ph.sem("source_loaded"), 16)
                for i, (to, frm) in enumerate(loads or []):
                    sp.dma_start(to, frm).then_inc(ph.sem(f"small_loaded{i}"), 16)
                for i in range(len(loads or [])):
                    sp.wait_ge(ph.sem(f"small_loaded{i}"), 16)

            @block.scalar
            def _(act):
                link = Chain(act, ph.sem("act_chain"))
                if source is not None:
                    act.wait_ge(ph.sem("source_loaded"), 16)
                for m in range(MT):
                    link(act.activation(junk, src[:, m, :], ACT.Square, accum_out=ss[:, m:m + 1]))
                act.sem_inc(ph.sem("squares_summed"), 1)
                k.rstd_scalar(act, ph, link, ms, y)

            @block.vector
            def _(dve):
                link = Chain(dve, ph.sem("dve_chain"))
                dve.wait_ge(ph.sem("squares_summed"), 1)
                k.rstd_vector_before(dve, ph, link, ss, ms, D)
                k.rstd_vector_after(dve, ph, link, ms, y, t)
                for m in range(MT):
                    dve.tensor_scalar(xn[:, m, :], src[:, m, :], y[:, m:m + 1], None, ALU.mult
                                      ).then_inc(ph.sem("normed"), 1)
                for i in range(len(loads or [])):
                    dve.wait_ge(ph.sem(f"small_loaded{i}"), 16)
                for i in range(len(jobs)):
                    bank = k.turned(dve, ph, "h", i, banks)
                    dve.tensor_tensor(dst[:, 2 * i:2 * i + 2, :], bank.rearrange("p (a t) -> p a t", a=2),
                                      bc(gain[:, 2 * i:2 * i + 2].unsqueeze(2), [P, 2, T]), ALU.mult)
                if out_tok is not None:
                    dve.wait_ge(ph.sem("normed"), MT)
                    dve.tensor_tensor(out_tok[:], xn, bc(k.gain_row[:].unsqueeze(1), [P, MT, D]), ALU.mult)

            @block.tensor
            def _(pe):
                if jobs:
                    pe.wait_ge(ph.sem("normed"), MT)
                    k.transposes(pe, ph, "h", jobs, banks)


def constants_phase(k):
    with k.phase("constants") as ph:
        pos, a = k.at(0, MT)
        posi, a = k.at(a, MT)
        freq, a = k.at(a, 48)
        ang, a = k.at(a, MT, 48)
        turns, a = k.at(a, MT, 48)
        turnsi, a = k.at(a, MT, 48)
        red, a = k.at(a, MT, 48)
        posi, turnsi = posi.bitcast(I32), turnsi.bitcast(I32)
        two_pi = [float(np.float32(6.28125)), float(np.float32(2 * np.pi - 6.28125))]
        two_pi.append(float(2 * np.pi - two_pi[0] - two_pi[1]))
        with k.engines(ph) as block:
            @block.sync
            def _(sp):
                sp.dma_start(posi, k.dram["positions"]).then_inc(ph.sem("positions_loaded"), 16)
                sp.dma_start(freq, k.dram["freq"]).then_inc(ph.sem("freq_loaded"), 16)
                sp.dma_start(k.x[:], k.dram["x"]).then_inc(ph.sem("x_loaded"), 16)
                for s in range(SLOTS):
                    sp.dma_start(k.ring[:, s, :], k.dram["stream"][s]).then_inc(k.ring_full[s], 16)
                sp.wait_ge(ph.sem("x_loaded"), 16)

            @block.gpsimd
            def _(pool):
                link = Chain(pool, ph.sem("pool_chain"))
                for tile, value in ((k.ident, 0.0), (k.ones, 1.0), (k.causal, 0.0), (k.band, 0.0),
                                    (k.cmp_mask, 0.0), (k.row_valid, 1.0), (k.upper, 1.0),
                                    (k.upper_add, 0.0), (k.chunk_upper, 1.0)):
                    link.note(pool.memset(tile[:], value))
                link.sync()

                def select(tile, op, fill, base, pattern, channel):
                    link(pool.affine_select(out=tile, in_=tile, compare_op=op, fill=fill, base=base,
                                            pattern=pattern, channel_multiplier=channel))

                select(k.ident[:], ALU.not_equal, 1.0, 0, [[-1, P]], 1)
                select(k.causal[:], ALU.is_ge, NEG, P, [[-1, 2 * P]], 1)
                select(k.band[:], ALU.is_ge, NEG, P, [[-1, 2 * P]], 1)
                select(k.band[:], ALU.is_gt, NEG, 0, [[1, 2 * P]], -1)
                select(k.cmp_mask[:], ALU.is_ge, NEG, -31, [[P, MT], [-16, N_CMP]], 1)
                select(k.row_valid[:], ALU.is_ge, 0.0, -31, [[P, MT]], 1)
                select(k.upper[:], ALU.is_ge, 0.0, 0, [[1, P]], -1)
                select(k.upper_add[:], ALU.is_ge, NEG, 0, [[1, P]], -1)
                select(k.chunk_upper[:], ALU.is_ge, 0.0, 0, [[1, P]], -1)
                select(k.chunk_upper[:, HD:P], ALU.is_ge, 0.0, -HD, [[0, HD]], 1)

            @block.vector
            def _(dve):
                link = Chain(dve, ph.sem("dve_chain"))
                dve.wait_ge(ph.sem("positions_loaded"), 16)
                dve.wait_ge(ph.sem("freq_loaded"), 16)
                link(dve.tensor_copy(pos, posi))
                link(dve.tensor_tensor(ang, bc(pos.unsqueeze(2), [P, MT, 48]), bc(freq.unsqueeze(1), [P, MT, 48]), ALU.mult))
                link(dve.tensor_scalar(turns, ang, float(1 / (2 * np.pi)), None, ALU.mult))
                link(dve.tensor_copy(turnsi, turns))
                link(dve.tensor_copy(turns, turnsi))
                for part in two_pi:
                    link(dve.scalar_tensor_tensor(out=ang, in0=turns, scalar=-part, in1=ang, op0=ALU.mult, op1=ALU.add))
                for sign, op in ((-1.0, ALU.is_gt), (1.0, ALU.is_lt)):
                    link(dve.tensor_scalar(red, ang, float(-sign * np.pi), float(sign * 2 * np.pi), op, ALU.mult))
                    link(dve.tensor_tensor(ang, ang, red, ALU.add))
                pi = float(np.nextafter(np.float32(np.pi), np.float32(0)))
                link(dve.tensor_scalar(ang, ang, pi, -pi, ALU.min, ALU.max))
                link(dve.tensor_scalar(red, ang, -1.0, None, ALU.mult))
                link(dve.tensor_tensor(red, red, ang, ALU.max))
                link(dve.tensor_scalar(red, red, -1.0, float(np.pi / 2), ALU.mult, ALU.add))
                dve.sem_inc(ph.sem("angles_ready"), 1)

            @block.scalar
            def _(act):
                act.wait_ge(ph.sem("angles_ready"), 1)
                act.activation(k.rope[:, 0], red, ACT.Sin)
                act.activation(k.rope[:, 1], ang, ACT.Sin)

STAGE = 2


def rotate(dve, link, x, out, cos, sin, t1, t2):
    _, mt, heads, width = x.shape
    half = width // 2
    shape = [P, mt, heads, half]
    c, s = bc(cos.unsqueeze(2), shape), bc(sin.unsqueeze(2), shape)
    x1, x2 = x[:, :, :, 0:half], x[:, :, :, half:width]
    link.note(dve.tensor_tensor(t1, x1, s, ALU.mult))
    link.note(dve.tensor_tensor(t2, x2, s, ALU.mult))
    link.note(dve.tensor_tensor(out[:, :, :, 0:half], x1, c, ALU.mult))
    link(dve.tensor_tensor(out[:, :, :, half:width], x2, c, ALU.mult))
    link.note(dve.tensor_tensor(out[:, :, :, 0:half], out[:, :, :, 0:half], t2, ALU.subtract))
    return dve.tensor_tensor(out[:, :, :, half:width], out[:, :, :, half:width], t1, ALU.add)


class Tiles1:

    def __init__(self, k):
        a = 0
        self.gT, a = k.at(a, 24, T)
        self.qaT, a = k.at(a, 4, T)
        self.qbT, a = k.at(a, 4, T)
        self.keysT, a = k.at(a, 3, T)
        self.kvcT, a = k.at(a, 2, T)
        self.values, a = k.at(a, MT, 8, HD)
        self.cqkv, a = k.at(a, MT, 2, T)
        self.small, a = k.at(a, MT, 56)
        self.sgate, a = k.at(a, MT, 24)
        self.kcmpT, a = k.at(a, N_CMP)
        self.vcmp, a = k.at(a, 2, HD)
        self.vC, a = k.at(a, MT, 8, HD)
        self.oT, a = k.at(a, 3, 4, T)
        shared = a
        self.rot, a = k.at(shared, MT, 3, 8, HD)
        self.kvc, a = k.at(a, MT, 2, P)
        self.t1, a = k.at(a, MT, 8, 32)
        self.t2, a = k.at(a, MT, 8, 32)
        self.qcT, a = k.at(shared, 8, T)
        self.kcT, a = k.at(a, 8, T)
        latent = a
        self.qC, a = k.at(latent, MT, 8, 96)
        self.kC, a = k.at(a, MT, 8, 96)
        self.cT, a = k.at(a, 4, T)
        self.cn, a = k.at(a, MT, 2, T)
        self.t3, a = k.at(a, MT, 8, 16)
        self.t4, a = k.at(a, MT, 8, 16)
        self.kpr, a = k.at(a, MT, 32)
        self.win, a = k.at(a, 32, 2, N_CMP)
        self.hid, a = k.at(a, 4, 2 * N_CMP)
        self.hid2, a = k.at(a, 4, 2 * N_CMP)
        self.probs, a = k.at(latent, 2, 4, T)
        self.probsT, a = k.at(a, 2, 2, 4, P)
        self.sum, a = k.at(a, 32, 4)
        self.nmax, a = k.at(a, 32, 4)
        self.mergedT, a = k.at(shared, KT, T)
        self.tmp, a = k.at(a, 4, T)


def project_phase(k, z):
    with k.phase("project") as ph:
        lins = [ph.linear(n) for n in ("rot0", "rot1", "rot2", "values", "latents")]
        gates = ph.linear("gates")
        cos, sin = k.rope[:, 0, :, 0:32], k.rope[:, 1, :, 0:32]
        w_small = k.p1("w_small", KT)
        small_ps = k.ps[:, 4:6, 0:56]
        with k.engines(ph) as block:
            @block.sync
            def _(sp):
                k.load_ahead(sp, ph)

            @block.tensor
            def _(pe):
                for lin in lins:
                    k.linear_tok(pe, ph, lin, k.hT)
                for kt in range(KT):
                    for m in range(MT):
                        last = pe.matmul(small_ps[:, m, :], k.hT[:, kt, m * P:(m + 1) * P], w_small[:, kt, :],
                                         start=(kt == 0), stop=(kt == KT - 1))
                last.then_inc(ph.sem("small_done"), 1)
                k.linear_T(pe, ph, gates, k.hT)
                pe.wait_ge(ph.sem("rotated"), 3)
                rot = z.rot
                jobs = [[(rot[:, m, j, 2 * (first + i):2 * (first + i) + 2, :].rearrange("p a b -> p (a b)"), i * T + m * P)
                         for i in range(2) for m in range(MT)] for j, first in ((0, 0), (0, 2), (1, 0), (2, 0), (2, 2))]
                jobs.append([(rot[:, m, 1, 4:6, :].rearrange("p a b -> p (a b)"), m * P) for m in range(MT)])
                jobs.append([(z.kvc[:, m, g, :], g * T + m * P) for g in range(2) for m in range(MT)])
                k.transposes(pe, ph, "heads", jobs, [6, 7])

            @block.vector
            def _(dve):
                link = Chain(dve, ph.sem("dve_chain"))
                for j in range(3):
                    pair, free = k.take(dve, ph, lins[j], 0)
                    x = pair.rearrange("p m (h d) -> p m h d", h=8)
                    if j == 1:
                        rotate(dve, link, x[:, :, 0:6, :], z.rot[:, :, 1, 0:6, :], cos, sin, z.t1[:, :, 0:6], z.t2[:, :, 0:6]
                               ).then_inc(ph.sem("keys_rotated"), 1)
                        dve.wait_ge(ph.sem("keys_rotated"), 1)
                        last = rotate(dve, link, x[:, :, 6:8, :], z.kvc[:, :, :, 0:HD], cos, sin,
                                      z.t1[:, :, 6:8], z.t2[:, :, 6:8])
                    else:
                        last = rotate(dve, link, x, z.rot[:, :, j], cos, sin, z.t1, z.t2)
                    last.then_inc(free, 1)
                    dve.wait_ge(free, (lins[j].group0 + 2) // 2)
                    dve.sem_inc(ph.sem("rotated"), 1)
                for n in range(gates.n):
                    dve.wait_ge(ph.sem("gates_exp"), n + 1)
                    part = z.gT[:, 4 * n:4 * n + 4, :]
                    link(dve.tensor_scalar(part, part, 1.0, None, ALU.add))
                    link(dve.reciprocal(part, part))
                link(dve.tensor_scalar(z.sgate, z.sgate, 1.0, None, ALU.add))
                link(dve.reciprocal(z.sgate, z.sgate))
                for m in range(MT):
                    link(dve.tensor_scalar(z.sgate[:, m, 0:8], z.sgate[:, m, 0:8], k.row_valid[:, m:m + 1], None, ALU.mult))
                for i in range(7):
                    bank = k.turned(dve, ph, "heads", i, [6, 7])
                    dst = [z.qaT[:, 0:2], z.qaT[:, 2:4], z.keysT[:, 0:2], z.qbT[:, 0:2], z.qbT[:, 2:4],
                           z.keysT[:, 2:3], z.kvcT][i]
                    n = T if i == 5 else 2 * T
                    dve.tensor_copy(dst.rearrange("p a t -> p (a t)"), bank[:, 0:n]
                                    ).then_inc(ph.sem("heads_copied"), 1)

            @block.scalar
            def _(act):
                link = Chain(act, ph.sem("act_chain"))
                pair, free = k.take(act, ph, lins[3], 0)
                values = pair.rearrange("p m (h d) -> p m h d", h=8)
                link(act.activation(z.kvc[:, :, :, HD:P], values[:, :, 0:2, :], ACT.Copy))
                link(act.activation(z.values, values, ACT.Copy))
                act.sem_inc(free, 1)
                pair, free = k.take(act, ph, lins[4], 0)
                act.activation(z.cqkv, pair.rearrange("p m (a b) -> p m a b", a=2), ACT.Copy).then_inc(free, 1)
                act.wait_ge(ph.sem("small_done"), 1)
                link(act.activation(z.small, small_ps, ACT.Copy))
                link(act.activation(z.sgate, z.small[:, :, 32:56], ACT.Exp, scale=-1.0))
                for n in range(gates.n):
                    pair, free = k.take(act, ph, gates, n)
                    act.activation(z.gT[:, 4 * n:4 * n + 4, :].rearrange("p a t -> p (a t)"),
                                   pair.rearrange("p a b -> p (a b)"), ACT.Exp, scale=-1.0).then_inc(free, 1)
                    act.wait_ge(free, (gates.group0 + n + 2) // 2)
                    act.sem_inc(ph.sem("gates_exp"), 1)


def latent_phase(k, z):
    with k.phase("latent") as ph:
        w1, qup, kvup = ph.linear("cmp_w1", grouped=False), ph.linear("q_up"), ph.linear("kv_up")
        cos, sin = k.rope[:, 0, :, 32:48], k.rope[:, 1, :, 32:48]
        ss, ms, y, t = (k.stat[:, i, 0:4] for i in range(4))
        ss2, ms2, y2, t2 = (k.stat[:, i, 0:4].rearrange("p (a b) -> p a b", a=MT) for i in range(4))
        pos = k.p1("posT")
        w2k, w2v = k.p1("w2k", 2), k.p1("w2v", 2)
        n2 = 2 * N_CMP
        with k.engines(ph) as block:
            @block.sync
            def _(sp):
                k.load_ahead(sp, ph)

            @block.scalar
            def _(act):
                link = Chain(act, ph.sem("act_chain"))
                for m in range(MT):
                    for j in range(2):
                        link(act.activation(z.cn[:, m, j], z.cqkv[:, m, j], ACT.Square,
                                            accum_out=ss[:, 2 * m + j:2 * m + j + 1]))
                act.sem_inc(ph.sem("squares_summed"), 1)
                k.rstd_scalar(act, ph, link, ms, y)
                act.wait_ge(ph.sem("cubes_ready"), 1)
                act.activation(z.hid2, z.hid2, ACT.Exp, scale=-1.5957691216057308).then_inc(ph.sem("hidden_exp"), 1)
                pair, free = k.take(act, ph, qup, 0)
                q = z.qC.rearrange("p m h d -> p m (h d)")
                act.activation(q[:, :, 0:BLK], pair, ACT.Copy).then_inc(free, 1)
                pair, free = k.take(act, ph, qup, 1)
                act.activation(q[:, :, BLK:768], pair[:, :, 0:256], ACT.Copy).then_inc(free, 1)
                act.wait_ge(free, qup.group0 // 2 + 1)
                act.wait_ge(ph.sem("pair_free0"), qup.group0 // 2 + 1)
                act.sem_inc(ph.sem("queries_up"), 1)
                for n in range(2):
                    pair, free = k.take(act, ph, kvup, n)
                    x = pair.rearrange("p m (h d) -> p m h d", h=4)
                    for m in range(MT):
                        link(act.activation(z.kC[:, m, 4 * n:4 * n + 4, 0:HD], x[:, m, :, 0:HD], ACT.Copy))
                        link(act.activation(z.vC[:, m, 4 * n:4 * n + 4, :], x[:, m, :, HD:P], ACT.Copy))
                    act.sem_inc(free, 1)
                act.sem_inc(ph.sem("keys_up"), 1)

            @block.vector
            def _(dve):
                link = Chain(dve, ph.sem("dve_chain"))
                for g in range(2):
                    steps = z.kvcT[:, g, :].rearrange("p (n s) -> p s n", s=16)
                    for a in range(2):
                        link.note(dve.tensor_tensor(z.win[:, 16 * a:16 * a + 16, g, :], steps[:, :, a:a + N_CMP],
                                                    bc(pos[:, 16 * a:16 * a + 16].unsqueeze(2), [P, 16, N_CMP]), ALU.add))
                link.sync()
                dve.sem_inc(ph.sem("windows_ready"), 1)
                dve.wait_ge(ph.sem("squares_summed"), 1)
                k.rstd_vector_before(dve, ph, link, ss, ms, T)
                k.rstd_vector_after(dve, ph, link, ms, y, t)
                dve.tensor_tensor(z.cn, z.cqkv, bc(y2.unsqueeze(3), [P, MT, 2, T]), ALU.mult).then_inc(ph.sem("latents_normed"), 1)
                for i in range(2):
                    bank = k.turned(dve, ph, "latents", i, [4, 5])
                    gain = k.p1(("cq_norm", "ckv_norm")[i])
                    dve.tensor_tensor(z.cT[:, 2 * i:2 * i + 2, :], bank.rearrange("p (a t) -> p a t", a=2),
                                      bc(gain.unsqueeze(2), [P, 2, T]), ALU.mult).then_inc(ph.sem("latents_turned_gained"), 1)
                dve.wait_ge(ph.sem("hidden_done"), 1)
                for kv in range(2):
                    link(dve.tensor_copy(z.hid[:, 2 * kv:2 * kv + 2, :].rearrange("p a b -> p (a b)"), k.ps[:, 6 + kv, 0:2 * n2]))
                link(dve.tensor_tensor(z.hid2, z.hid, z.hid, ALU.mult))
                link(dve.tensor_scalar(z.hid2, z.hid2, 0.044715, 1.0, ALU.mult, ALU.add))
                dve.tensor_tensor(z.hid2, z.hid2, z.hid, ALU.mult).then_inc(ph.sem("cubes_ready"), 1)
                dve.wait_ge(ph.sem("hidden_exp"), 1)
                link(dve.tensor_scalar(z.hid2, z.hid2, 1.0, None, ALU.add))
                link(dve.reciprocal(z.hid2, z.hid2))
                dve.tensor_tensor(z.hid, z.hid, z.hid2, ALU.mult).then_inc(ph.sem("hidden_ready"), 1)
                dve.wait_ge(ph.sem("compressed_done"), 1)
                link(dve.tensor_copy(z.kcmpT, k.ps[:, 4, 0:N_CMP]))
                link(dve.tensor_copy(z.vcmp[0:N_CMP], k.ps[0:N_CMP, 5, 0:P].rearrange("p (a b) -> p a b", a=2)))
                dve.sem_inc(ph.sem("compressed_copied"), 1)
                kpe = z.small[:, :, 0:32].unsqueeze(2)
                rotate(dve, link, kpe, z.kpr.unsqueeze(2), cos, sin, z.t3[:, :, 0:1], z.t4[:, :, 0:1]).then_inc(ph.sem("kpe_rotated"), 1)
                dve.wait_ge(ph.sem("kpe_rotated"), 1)
                link(dve.tensor_copy(z.kC[:, :, :, HD:96], bc(z.kpr.unsqueeze(2), [P, MT, 8, 32])))
                dve.wait_ge(ph.sem("queries_up"), 1)
                x1, x2 = z.qC[:, :, :, HD:HD + 16], z.qC[:, :, :, HD + 16:96]
                shape = [P, MT, 8, 16]
                c, s = bc(cos.unsqueeze(2), shape), bc(sin.unsqueeze(2), shape)
                link.note(dve.tensor_tensor(z.t3, x1, s, ALU.mult))
                link(dve.tensor_tensor(z.t4, x2, s, ALU.mult))
                link.note(dve.tensor_tensor(x1, x1, c, ALU.mult))
                link(dve.tensor_tensor(x2, x2, c, ALU.mult))
                link.note(dve.tensor_tensor(x1, x1, z.t4, ALU.subtract))
                link(dve.tensor_tensor(x2, x2, z.t3, ALU.add))
                dve.sem_inc(ph.sem("queries_rotated"), 1)
                for i in range(8):
                    bank = k.turned(dve, ph, "c", i, [4, 5])
                    dst = (z.qcT if i < 4 else z.kcT)[0:96, 2 * (i % 4):2 * (i % 4) + 2, :]
                    dve.tensor_copy(dst.rearrange("p a t -> p (a t)"), bank[0:96, :]).then_inc(ph.sem("c_copied"), 1)

            @block.tensor
            def _(pe):
                pe.wait_ge(ph.sem("windows_ready"), 1)
                for step in range(32):
                    v = w1.chunk0 + step // 8
                    if step % 8 == 0:
                        k.wait_chunk(pe, v)
                    w = k.ring[:, v % SLOTS, (step % 8) * 256:(step % 8 + 1) * 256]
                    for kv in range(2):
                        rows = slice(HD * kv, HD * kv + HD)
                        for j in range(2):
                            last = pe.matmul(k.ps[:, 6 + kv, j * n2:(j + 1) * n2], w[rows, j * P:(j + 1) * P],
                                             z.win[rows, step].rearrange("p a b -> p (a b)"),
                                             start=(step == 0 and j == 0), stop=(step == 31 and j == 1),
                                             skip_group_check=True)
                    if step % 8 == 7 and step < 31:
                        last.then_inc(k.ring_free[v % SLOTS], 1)
                last.then_inc(ph.sem("hidden_done"), 1)
                pe.wait_ge(ph.sem("latents_normed"), 1)
                jobs = [[(z.cn[:, m, j, i * P:(i + 1) * P], i * T + m * P) for i in range(2) for m in range(MT)] for j in range(2)]
                k.transposes(pe, ph, "latents", jobs, [4, 5])
                pe.wait_ge(ph.sem("hidden_ready"), 1)
                pe.sem_inc(k.ring_free[(w1.chunk0 + 3) % SLOTS], 1)
                pe.wait_ge(ph.sem("latents_turned_gained"), 2)
                for g in range(2):
                    for j in range(2):
                        pe.matmul(k.ps[HD * g:HD * g + HD, 4, 0:N_CMP], w2k[:, j, :], z.hid[:, j, g * N_CMP:(g + 1) * N_CMP],
                                  start=(j == 0), stop=(j == 1))
                for g in range(2):
                    for j in range(2):
                        last = pe.matmul(k.ps[0:N_CMP, 5, g * HD:(g + 1) * HD], z.hid[:, 2 + j, g * N_CMP:(g + 1) * N_CMP],
                                         w2v[:, j, :], start=(j == 0), stop=(j == 1))
                last.then_inc(ph.sem("compressed_done"), 1)
                k.linear_tok(pe, ph, qup, z.cT[:, 0:2], [BLK, 256])
                k.linear_tok(pe, ph, kvup, z.cT[:, 2:4])
                pe.wait_ge(ph.sem("queries_rotated"), 1)
                pe.wait_ge(ph.sem("keys_up"), 1)
                jobs = [[(src[:, m, 2 * j + i, :], i * T + m * P) for i in range(2) for m in range(MT)]
                        for src in (z.qC, z.kC) for j in range(4)]
                pe.wait_ge(ph.sem("compressed_copied"), 1)
                k.transposes(pe, ph, "c", jobs, [4, 5])


class Batch:

    def __init__(self, q, key, value, n_keys, scale, out, mask=None, coef=None, sink=None, add=False,
                 contract=1, pieces=1):
        self.q, self.key, self.value, self.n_keys, self.scale, self.out = q, key, value, n_keys, scale, out
        self.mask, self.coef, self.sink, self.add = mask, coef, sink, add
        self.contract, self.pieces = contract, pieces
        self.key_tiles = [(i, min(P, n_keys - i)) for i in range(0, n_keys, P)]


def attention_phase(k, name, batches, probs, probsT, sums, nmax, out_banks):
    nb = len(batches)
    with k.phase(name) as ph:
        def scores_ps(b):
            return k.ps[:, 2 * (b % 2):2 * (b % 2) + 2, :].rearrange("p a (h n) -> p (a h) n", h=2)

        def out_ps(b):
            return out_banks[b % len(out_banks)]

        with k.engines(ph) as block:
            @block.tensor
            def _(pe):
                def scores(b):
                    bt = batches[b]
                    if b >= 2:
                        pe.wait_ge(ph.sem("scores_masked"), b - 1)
                    for h in range(4):
                        for c in range(bt.contract):
                            last = pe.matmul(scores_ps(b)[:, h, 0:bt.n_keys], bt.q(h, c), bt.key(h, c),
                                             start=(c == 0), stop=(c == bt.contract - 1))
                    last.then_inc(ph.sem("scores_ready"), 1)

                def turn(b):
                    bt = batches[b]
                    pe.wait_ge(ph.sem("probs_scaled"), b + 1)
                    if b >= 1:
                        pe.wait_ge(ph.sem("probs_turned_copied"), b)
                    for i, (k0, n) in enumerate(bt.key_tiles):
                        for h in range(4):
                            last = pe.transpose(k.ps[0:n, 4 + i, h * P:(h + 1) * P], probs[:, b % 2, h, k0:k0 + n], k.ident[:])
                    last.then_inc(ph.sem("probs_turned"), 1)

                def values(b):
                    bt = batches[b]
                    pe.wait_ge(ph.sem("probs_turned_copied"), b + 1)
                    if b >= len(out_banks):
                        pe.wait_ge(ph.sem("out_copied"), b - len(out_banks) + 1)
                    for h in range(4):
                        for j in range(bt.pieces):
                            for i, (k0, n) in enumerate(bt.key_tiles):
                                v = bt.value(h, i, j)
                                first = v.shape[1]
                                base = bt.out.start_partition() if bt.pieces == 1 else 0
                                last = pe.matmul(out_ps(b)[base:base + first, (h * bt.pieces + j) // 4,
                                                           ((h * bt.pieces + j) % 4) * P:((h * bt.pieces + j) % 4 + 1) * P],
                                                 v, probsT[0:n, b % 2, i, h, :], start=(i == 0), stop=(i == len(bt.key_tiles) - 1))
                    last.then_inc(ph.sem("out_ready"), 1)

                scores(0)
                for b in range(nb):
                    if b + 1 < nb:
                        scores(b + 1)
                    turn(b)
                    if b >= 1:
                        values(b - 1)
                values(nb - 1)

            @block.vector
            def _(dve):
                link = Chain(dve, ph.sem("dve_chain"))

                def mask(b):
                    bt = batches[b]
                    dve.wait_ge(ph.sem("scores_ready"), b + 1)
                    if b >= 2:
                        dve.wait_ge(ph.sem("probs_turned"), b - 1)
                    s, p = scores_ps(b)[:, :, 0:bt.n_keys], probs[:, b % 2, :, 0:bt.n_keys]
                    if bt.mask is not None:
                        ins = dve.scalar_tensor_tensor(out=p, in0=s, scalar=bt.scale, in1=bc(bt.mask.unsqueeze(1), [P, 4, bt.n_keys]),
                                                       op0=ALU.mult, op1=ALU.add)
                    else:
                        ins = dve.tensor_scalar(p, s, bt.scale, None, ALU.mult)
                    ins.then_inc(ph.sem("scores_masked"), 1)
                    dve.wait_ge(ph.sem("scores_masked"), b + 1)
                    link(dve.tensor_reduce(nmax[:, b, :], p, AX, ALU.max))
                    if bt.sink is not None:
                        link(dve.tensor_tensor(nmax[:, b, :], nmax[:, b, :], bt.sink, ALU.max))
                    negated = dve.tensor_scalar(nmax[:, b, :], nmax[:, b, :], -1.0, None, ALU.mult)
                    if bt.sink is None:
                        negated.then_inc(ph.sem("max_ready"), 1)
                    else:
                        link(negated)
                        dve.tensor_tensor(k.stat[:, 7, 4 * (b % 16):4 * (b % 16) + 4], nmax[:, b, :], bt.sink, ALU.add
                                          ).then_inc(ph.sem("max_ready"), 1)

                def scale(b):
                    bt = batches[b]
                    dve.wait_ge(ph.sem("probs_exp"), b + 1)
                    s = sums[:, b, :]
                    if bt.sink is not None:
                        link(dve.tensor_tensor(s, s, nmax[:, b, :], ALU.add))
                    link(dve.reciprocal(s, s))
                    if bt.coef is not None:
                        link(dve.tensor_tensor(s, s, bt.coef, ALU.mult))
                    p = probs[:, b % 2, :, 0:bt.n_keys]
                    dve.tensor_tensor(p, p, bc(s.unsqueeze(2), [P, 4, bt.n_keys]), ALU.mult).then_inc(ph.sem("probs_scaled"), 1)

                def out(b):
                    bt = batches[b]
                    dve.wait_ge(ph.sem("out_ready"), b + 1)
                    base = bt.out.start_partition()
                    rows = bt.out.shape[0]
                    o = out_ps(b)[base:base + rows].rearrange("p a (h n) -> p (a h) n", h=4)
                    if bt.add:
                        dve.wait_ge(ph.sem("out_copied"), b)
                        ins = dve.tensor_tensor(bt.out, o, bt.out, ALU.add)
                    else:
                        ins = dve.tensor_copy(bt.out, o)
                    ins.then_inc(ph.sem("out_copied"), 1)

                mask(0)
                for b in range(nb):
                    if b + 1 < nb:
                        mask(b + 1)
                    scale(b)
                    if b >= 2:
                        out(b - 2)
                for b in range(max(0, nb - 2), nb):
                    out(b)

            @block.scalar
            def _(act):
                link = Chain(act, ph.sem("act_chain"))

                def exps(b):
                    bt = batches[b]
                    act.wait_ge(ph.sem("max_ready"), b + 1)
                    for h in range(4):
                        p = probs[:, b % 2, h, 0:bt.n_keys]
                        link.note(act.activation(p, p, ACT.Exp, bias=nmax[:, b, h:h + 1], accum_out=sums[:, b, h:h + 1]))
                    link.sync()
                    if bt.sink is not None:
                        link(act.activation(nmax[:, b, :], k.stat[:, 7, 4 * (b % 16):4 * (b % 16) + 4], ACT.Exp))
                    act.sem_inc(ph.sem("probs_exp"), 1)

                def copy(b):
                    bt = batches[b]
                    act.wait_ge(ph.sem("probs_turned"), b + 1)
                    if b >= 2:
                        act.wait_ge(ph.sem("out_ready"), b - 1)
                    n = bt.key_tiles[-1][1]
                    tiles = len(bt.key_tiles)
                    act.activation(probsT[0:n, b % 2, 0:tiles].rearrange("p a h q -> p a (h q)"), k.ps[0:n, 4:4 + tiles, :],
                                   ACT.Copy).then_inc(ph.sem("probs_turned_copied"), 1)

                exps(0)
                for b in range(nb):
                    if b + 1 < nb:
                        exps(b + 1)
                    copy(b)


def branches_phase(k, z):
    with k.phase("branches") as ph:
        lins = [ph.linear(f"branch_{c}") for c in "abc"]
        w_out = ph.linear("w_out")
        with k.engines(ph) as block:
            @block.sync
            def _(sp):
                k.load_ahead(sp, ph)

            @block.tensor
            def _(pe):
                for i, lin in enumerate(lins):
                    k.linear_T(pe, ph, lin, z.oT[:, i])
                pe.wait_ge(ph.sem("merged"), 2)
                k.linear_tok(pe, ph, w_out, z.mergedT)

            @block.vector
            def _(dve):
                link = Chain(dve, ph.sem("dve_chain"))
                for i, lin in enumerate(lins):
                    for n in range(2):
                        pair, free = k.take(dve, ph, lin, n)
                        x = pair.rearrange("p a (b t) -> p (a b) t", b=2)
                        gate = z.gT[:, KT * i + 4 * n:KT * i + 4 * n + 4, :]
                        part = z.mergedT[:, 4 * n:4 * n + 4, :]
                        to = part if i == 0 else z.tmp
                        dve.tensor_tensor(to, x, gate, ALU.mult).then_inc(free, 1)
                        dve.wait_ge(free, (lin.group0 + n + 2) // 2)
                        if i > 0:
                            link(dve.tensor_tensor(part, part, z.tmp, ALU.add))
                        if i == 2:
                            dve.sem_inc(ph.sem("merged"), 1)
                add_to_x(k, dve, ph, w_out)


def add_to_x(k, dve, ph, lin):
    for n in range(lin.n):
        pair, free = k.take(dve, ph, lin, n)
        x = k.x[:, :, n * BLK:(n + 1) * BLK]
        dve.tensor_tensor(x, pair, x, ALU.add).then_inc(free, 1)


def ffn_phase(k):
    with k.phase("ffn") as ph:
        lin, down = ph.linear("ffn_in"), ph.linear("ffn_down")
        hidden, a = k.at(0, FF_T, T)
        sig, a = k.at(a, 2, 2, T)
        with k.engines(ph) as block:
            @block.sync
            def _(sp):
                k.load_ahead(sp, ph)

            @block.tensor
            def _(pe):
                k.linear_T(pe, ph, lin, k.hT)
                pe.wait_ge(ph.sem("hidden_ready"), lin.n)
                k.linear_tok(pe, ph, down, hidden)

            @block.scalar
            def _(act):
                for n in range(lin.n):
                    pair, _ = k.take(act, ph, lin, n)
                    if n >= 2:
                        act.wait_ge(ph.sem("hidden_ready"), n - 1)
                    act.activation(sig[:, n % 2].rearrange("p a t -> p (a t)"), pair[:, 0, :], ACT.Exp, scale=-1.0
                                   ).then_inc(ph.sem("gate_exp"), 1)

            @block.vector
            def _(dve):
                link = Chain(dve, ph.sem("dve_chain"))
                for n in range(lin.n):
                    pair, free = k.take(dve, ph, lin, n, release=False)
                    gate, up = (pair[:, i, :].rearrange("p (a t) -> p a t", a=2) for i in range(2))
                    s = sig[:, n % 2]
                    dve.wait_ge(ph.sem("gate_exp"), n + 1)
                    link(dve.tensor_scalar(s, s, 1.0, None, ALU.add))
                    link(dve.reciprocal(s, s))
                    link(dve.tensor_tensor(s, gate, s, ALU.mult))
                    link(dve.tensor_tensor(hidden[:, 2 * n:2 * n + 2, :], up, s, ALU.mult))
                    dve.sem_inc(free, 1)
                    dve.sem_inc(ph.sem("hidden_ready"), 1)
                add_to_x(k, dve, ph, down)


def ple_phase(k):
    with k.phase("ple") as ph:
        gate, proj = ph.linear("ple_gate"), ph.linear("ple_proj")
        g, a = k.at(0, MT, D)
        pT, a = k.at(a, 2, T)
        with k.engines(ph) as block:
            @block.sync
            def _(sp):
                sp.dma_start(pT, k.dram["pT"][bass.ds(k.layer, 1)].rearrange("a p k t -> (a p) k t")
                             ).then_inc(ph.sem("p_loaded"), 16)
                k.load_ahead(sp, ph)

            @block.tensor
            def _(pe):
                k.linear_tok(pe, ph, gate, k.hT)
                pe.wait_ge(ph.sem("p_loaded"), 16)
                k.linear_tok(pe, ph, proj, pT)

            @block.scalar
            def _(act):
                for n in range(2):
                    pair, free = k.take(act, ph, gate, n)
                    act.activation(g[:, :, n * BLK:(n + 1) * BLK], pair, ACT.Exp, scale=-1.0).then_inc(free, 1)

            @block.vector
            def _(dve):
                link = Chain(dve, ph.sem("dve_chain"))
                for n in range(2):
                    dve.wait_ge(ph.sem(f"pair_free{n}"), 1)
                    part = g[:, :, n * BLK:(n + 1) * BLK]
                    link(dve.tensor_scalar(part, part, 1.0, None, ALU.add))
                    link(dve.reciprocal(part, part))
                for n in range(2):
                    pair, free = k.take(dve, ph, proj, n)
                    part = g[:, :, n * BLK:(n + 1) * BLK]
                    link(dve.tensor_tensor(part, pair, part, ALU.mult))
                    dve.sem_inc(free, 1)
                    x = k.x[:, :, n * BLK:(n + 1) * BLK]
                    link(dve.tensor_tensor(x, x, part, ALU.add))


def first_layer(k):
    k.next_chunk, k.stream_at = 0, 0
    z = Tiles1(k)
    params = k.dram["params1"][bass.ds(k.layer, 1)].rearrange("a p n -> (a p) n")
    norm_phase(k, "mix_norm", k.x, k.p1("mix_norm"), k.hT, loads=[(k.par[:, 0:P1_W], params)])
    project_phase(k, z)
    latent_phase(k, z)
    batches = []
    gate = z.sgate.rearrange("p m (c h) -> p m c h", c=3)
    sinks = k.p1("sinks")
    for g in range(2):
        rows = slice(HD * g, HD * g + HD)
        for m in range(MT):
            toks = slice(m * P, (m + 1) * P)
            n_keys = (m + 1) * P
            causal = k.causal[:, P:2 * P] if m == 0 else k.causal[:]
            band = k.band[:, P:2 * P] if m == 0 else k.band[:]
            heads = slice(4 * g, 4 * g + 4)
            q_a = lambda h, c, rows=rows, toks=toks: z.qaT[rows, h, toks]
            q_b = lambda h, c, rows=rows, toks=toks: z.qbT[rows, h, toks]
            q_c = lambda h, c, g=g, toks=toks: z.qcT[0:96, 4 * g + h, toks]
            keys = lambda i, n=n_keys, rows=rows: (lambda h, c: z.keysT[rows, i, 0:n])
            vals = lambda i, g=g: (lambda h, kt, j: z.values[:, kt, 2 * i + g, :])
            outs = [z.oT[rows, i, :, toks] for i in range(3)]
            batches += [
                Batch(q_a, lambda h, c, rows=rows: z.kcmpT[rows, :], lambda h, kt, j, g=g: z.vcmp[0:N_CMP, g, :], N_CMP,
                      HD ** -0.5, outs[0], k.cmp_mask[:, m], gate[:, m, 0, heads]),
                Batch(q_a, keys(0), vals(1), n_keys, HD ** -0.5, outs[0], causal, gate[:, m, 1, heads], add=True),
                Batch(q_a, keys(1), vals(2), n_keys, HD ** -0.5, outs[0], causal, gate[:, m, 2, heads], add=True),
                Batch(q_b, keys(2), vals(3), n_keys, HD ** -0.5, outs[1], band, sink=sinks[:, heads]),
                Batch(q_c, lambda h, c, g=g, n=n_keys: z.kcT[0:96, 4 * g + h, 0:n],
                      lambda h, kt, j, g=g: z.vC[:, kt, 4 * g + h, :], n_keys, 96 ** -0.5, outs[2], causal),
            ]
    attention_phase(k, "attention", batches, z.probs, z.probsT, z.sum, z.nmax, [k.ps[:, 6:7, :], k.ps[:, 7:8, :]])
    branches_phase(k, z)
    norm_phase(k, "ffn_norm", k.x, k.p1("ffn_norm"), k.hT)
    ffn_phase(k)
    norm_phase(k, "ple_norm", k.x, k.p1("ple_norm"), k.hT)
    ple_phase(k)
    assert k.stream_at == len(STREAM_1) and k.next_chunk == CHUNKS_1


class TilesEven:

    def __init__(self, k):
        a = 0
        self.xcT, a = k.at(a, 20, T)
        self.xmT, a = k.at(a, KT, T + 3)
        self.z, a = k.at(a, MT, D)
        self.og, a = k.at(a, MT, D)
        self.small, a = k.at(a, MT, 24)
        self.ya, a = k.at(a, MT, D)
        self.yb, a = k.at(a, MT, D)
        self.shared = a
        self.xbcT, a = k.at(self.shared, XBC_T, T + 3)
        self.sig, a = k.at(a, 5, T)


def silu_of(dve, link, e, x, out):
    link(dve.tensor_scalar(e, e, 1.0, None, ALU.add))
    link(dve.reciprocal(e, e))
    link(dve.tensor_tensor(out, x, e, ALU.mult))


def even_in_phase(k, z):
    with k.phase("even_in") as ph:
        lz, lx, lm, lo = (ph.linear(n) for n in ("ssd_z", "xbc", "xm", "og"))
        small_ps = k.ps[:, 4:6, 0:24]
        w_small = k.p2("w_small", KT)
        ssd_w, ssd_b = k.p2("conv_w", XBC_T), k.p2("conv_b")
        ml_w, ml_b = k.p2("ml_conv_w", KT), k.p2("ml_conv_b")
        fours = ([(z.xbcT[:, 4 * n:4 * n + 4], ssd_w[:, 4 * n:4 * n + 4], ssd_b[:, 4 * n:4 * n + 4], 4 * n) for n in range(3)]
                 + [(z.xmT[:, 4 * n:4 * n + 4], ml_w[:, 4 * n:4 * n + 4], ml_b[:, 4 * n:4 * n + 4], XBC_T + 4 * n) for n in range(2)])
        e = z.ya.rearrange("p m d -> p (m d)")[:, 0:4 * T].rearrange("p (a t) -> p a t", a=4)
        e2 = z.yb
        with k.engines(ph) as block:
            @block.sync
            def _(sp):
                k.load_ahead(sp, ph)

            @block.tensor
            def _(pe):
                k.linear_tok(pe, ph, lz, k.hT)
                for kt in range(KT):
                    for m in range(MT):
                        last = pe.matmul(small_ps[:, m, :], k.hT[:, kt, m * P:(m + 1) * P], w_small[:, kt, :],
                                         start=(kt == 0), stop=(kt == KT - 1))
                last.then_inc(ph.sem("small_done"), 1)
                k.linear_T(pe, ph, lx, k.hT)
                k.linear_T(pe, ph, lm, k.hT)
                k.linear_tok(pe, ph, lo, k.hT)

            @block.gpsimd
            def _(pool):
                pool.memset(z.xbcT[:, :, 0:3], 0.0).then_inc(ph.sem("padded"), 1)
                pool.memset(z.xmT[:, :, 0:3], 0.0).then_inc(ph.sem("padded"), 1)

            @block.scalar
            def _(act):
                link = Chain(act, ph.sem("act_chain"))
                for n in range(2):
                    pair, free = k.take(act, ph, lz, n)
                    cols = slice(n * BLK, (n + 1) * BLK)
                    link(act.activation(z.z[:, :, cols], pair, ACT.Copy))
                    link(act.activation(e2[:, :, cols], pair, ACT.Exp, scale=-1.0))
                    act.sem_inc(free, 1)
                act.sem_inc(ph.sem("z_exp"), 1)
                act.wait_ge(ph.sem("small_done"), 1)
                link(act.activation(z.small, small_ps, ACT.Copy))
                act.wait_ge(ph.sem("padded"), 2)
                for i, (pad, w, b, at) in enumerate(fours):
                    lin, n = (lx, i) if i < 3 else (lm, i - 3)
                    pair, free = k.take(act, ph, lin, n)
                    link(act.activation(pad[:, :, 3:3 + T], pair.rearrange("p a (b t) -> p (a b) t", b=2), ACT.Copy))
                    act.sem_inc(free, 1)
                    for f in range(4):
                        link.note(act.activation(z.xcT[:, at + f, :], pad[:, f, 3:3 + T], ACT.Identity,
                                                 bias=b[:, f:f + 1], scale=w[:, f, 3:4]))
                    link.sync()
                    act.sem_inc(ph.sem("last_tap"), 1)
                    if i >= 1:
                        act.wait_ge(ph.sem("convolved"), i)
                        act.activation(e, z.xcT[:, fours[i - 1][3]:fours[i - 1][3] + 4, :], ACT.Exp, scale=-1.0
                                       ).then_inc(ph.sem("conv_exp"), 1)
                act.wait_ge(ph.sem("convolved"), 5)
                act.activation(e, z.xcT[:, 16:20, :], ACT.Exp, scale=-1.0).then_inc(ph.sem("conv_exp"), 1)
                for n in range(2):
                    pair, free = k.take(act, ph, lo, n)
                    link(act.activation(z.og[:, :, n * BLK:(n + 1) * BLK], pair, ACT.Exp, scale=-1.0))
                    act.sem_inc(free, 1)
                    act.sem_inc(ph.sem("og_exp"), 1)

            @block.vector
            def _(dve):
                link = Chain(dve, ph.sem("dve_chain"))

                def silu(i):
                    x = z.xcT[:, fours[i][3]:fours[i][3] + 4, :]
                    dve.wait_ge(ph.sem("conv_exp"), i + 1)
                    silu_of(dve, link, e, x, x)

                dve.wait_ge(ph.sem("z_exp"), 1)
                silu_of(dve, link, e2, z.z, z.z)
                for i, (pad, w, b, at) in enumerate(fours):
                    dve.wait_ge(ph.sem("last_tap"), i + 1)
                    for j in range(3):
                        for f in range(4):
                            y = z.xcT[:, at + f, :]
                            link.note(dve.scalar_tensor_tensor(out=y, in0=pad[:, f, j:j + T], scalar=w[:, f, j:j + 1],
                                                               in1=y, op0=ALU.mult, op1=ALU.add))
                        link.sync()
                    if i >= 1:
                        silu(i - 1)
                    dve.sem_inc(ph.sem("convolved"), 1)
                silu(4)
                for n in range(2):
                    dve.wait_ge(ph.sem("og_exp"), n + 1)
                    part = z.og[:, :, n * BLK:(n + 1) * BLK]
                    link(dve.tensor_scalar(part, part, 1.0, None, ALU.add))
                    link(dve.reciprocal(part, part))


def ssd_phase(k, z):
    with k.phase("ssd") as ph:
        G, E, HP, N = 2, 8, HD, P
        a = z.shared
        xs, a = k.at(a, MT, 16, HP)
        xdt, a = k.at(a, MT, 16, HP)
        bmat, a = k.at(a, G, N)
        states, a = k.at(a, G, E * HP)
        decay, a = k.at(a, 16, P)
        dt, a = k.at(a, MT, 16)
        dta, a = k.at(a, MT, 16)
        ncs, a = k.at(a, MT, 16)
        ecs, a = k.at(a, 16)
        dend, a = k.at(a, 16)
        neg_a, a = k.at(a, 16)
        tmp, a = k.at(a, MT, 16)
        tmp2, a = k.at(a, MT, 16)
        yoff, a = k.at(a, E * HP)
        bias, a_log, d_skip = k.p2("small_bias")[:, 0:16], k.p2("a_log"), k.p2("d_skip")
        ya = z.ya.rearrange("p m (h d) -> p m h d", h=16)
        ss, ms, y, t = (k.stat[:, i, 0:4] for i in range(4))
        jobs = [[(z.xcT[:, 4 * j + i, m * P:(m + 1) * P], i * P) for i in range(4)] for m in range(MT) for j in range(2)]
        jobs.append([(z.xcT[:, KT + g, 0:P], g * P) for g in range(G)])
        with k.engines(ph) as block:
            @block.sync
            def _(sp):
                k.load_ahead(sp, ph)

            @block.scalar
            def _(act):
                link = Chain(act, ph.sem("act_chain"))
                act.wait_ge(ph.sem("neg_abs_ready"), 1)
                link(act.activation(tmp, tmp, ACT.Exp))
                link(act.activation(tmp, tmp, ACT.Ln, bias=1.0))
                act.sem_inc(ph.sem("log_ready"), 1)
                link(act.activation(neg_a, a_log, ACT.Exp))
                act.sem_inc(ph.sem("a_ready"), 1)
                for i in range(4):
                    bank = k.turned(act, ph, "x", i, [6, 7])
                    m, j = i // 2, i % 2
                    act.activation(xs[:, m, 8 * j:8 * j + 8, :].rearrange("p a b -> p (a b)"), bank, ACT.Copy
                                   ).then_inc(ph.sem("x_copied"), 1)
                bank = k.turned(act, ph, "x", 4, [6, 7])
                act.activation(bmat.rearrange("p a b -> p (a b)"), bank[:, 0:G * N], ACT.Copy).then_inc(ph.sem("x_copied"), 1)
                act.wait_ge(ph.sem("ends_ready"), 1)
                link(act.activation(dend, dend, ACT.Exp))
                link(act.activation(ecs, ncs[:, 1, :], ACT.Exp, scale=-1.0))
                act.sem_inc(ph.sem("ends_exp"), 1)
                for c in range(MT):
                    act.wait_ge(ph.sem("decay_masked"), c + 1)
                    for h in range(16):
                        link.note(act.activation(decay[:, h, :], decay[:, h, :], ACT.Exp, bias=ncs[:, c, h:h + 1]))
                    link.sync()
                    act.sem_inc(ph.sem("decay_exp"), 1)
                for c in range(MT):
                    act.wait_ge(ph.sem("y_ready"), 1)
                    for g in range(G):
                        link(act.activation(yoff, z.ya[:, c, g * 512:(g + 1) * 512], ACT.Square,
                                            accum_out=ss[:, 2 * c + g:2 * c + g + 1]))
                act.sem_inc(ph.sem("squares_summed"), 1)
                k.rstd_scalar(act, ph, link, ms, y)

            @block.vector
            def _(dve):
                link = Chain(dve, ph.sem("dve_chain"))
                link(dve.tensor_tensor(dt, z.small[:, :, 0:16], bc(bias.unsqueeze(1), [P, MT, 16]), ALU.add))
                link(dve.tensor_scalar(tmp, dt, -1.0, None, ALU.mult))
                dve.tensor_tensor(tmp, tmp, dt, ALU.min).then_inc(ph.sem("neg_abs_ready"), 1)
                link(dve.tensor_scalar(dt, dt, 0.0, None, ALU.max))
                dve.wait_ge(ph.sem("log_ready"), 1)
                link(dve.tensor_tensor(dt, dt, tmp, ALU.add))
                dve.wait_ge(ph.sem("a_ready"), 1)
                link(dve.scalar_tensor_tensor(out=dta, in0=dt, scalar=-1.0, in1=bc(neg_a.unsqueeze(1), [P, MT, 16]),
                                              op0=ALU.mult, op1=ALU.mult))
                dve.sem_inc(ph.sem("dta_ready"), 1)
                dve.wait_ge(ph.sem("cumsum_done"), 1)
                link(dve.tensor_scalar(ncs, k.ps[:, 4, 0:32].rearrange("p (m h) -> p m h", m=MT), -1.0, None, ALU.mult))
                link(dve.tensor_tensor(dend, k.ps[:, 4, 32:48], ncs[:, 0, :], ALU.add))
                dve.sem_inc(ph.sem("ends_ready"), 1)
                dve.wait_ge(ph.sem("x_copied"), 5)
                link(dve.tensor_tensor(xdt, xs, bc(dt.unsqueeze(3), [P, MT, 16, HP]), ALU.mult))
                dve.wait_ge(ph.sem("ends_exp"), 1)
                for c in range(MT):
                    dve.wait_ge(ph.sem("rows_done"), c + 1)
                    if c == 1:
                        dve.wait_ge(ph.sem("diag_done"), 1)
                    rows = k.ps[:, 0:4, :].rearrange("p a (h l) -> p (a h) l", l=P)
                    link(dve.tensor_tensor(decay, rows, bc(k.upper_add[:].unsqueeze(1), [P, 16, P]), ALU.add))
                    dve.sem_inc(ph.sem("decay_masked"), 1)
                    dve.wait_ge(ph.sem("decay_exp"), c + 1)
                    dve.wait_ge(ph.sem("cb_done"), c + 1)
                    for g in range(G):
                        part = decay[:, 8 * g:8 * g + 8, :]
                        link(dve.tensor_tensor(part, bc(k.ps[:, 5, g * P:(g + 1) * P].unsqueeze(1), [P, 8, P]), part, ALU.mult))
                    dve.sem_inc(ph.sem("mixing_ready"), 1)
                    if c == 0:
                        late = ya[:, 1]
                        link(dve.tensor_tensor(late, xdt[:, 0], bc(dend.unsqueeze(2), [P, 16, HP]), ALU.mult))
                        dve.sem_inc(ph.sem("late_ready"), 1)
                        dve.wait_ge(ph.sem("states_done"), 1)
                        link(dve.tensor_copy(states, k.ps[:, 0:2, :]))
                        dve.sem_inc(ph.sem("states_ready"), 1)
                    dve.wait_ge(ph.sem("diag_done"), c + 1)
                    out = z.ya[:, c]
                    link(dve.tensor_tensor(ya[:, c], xs[:, c], bc(d_skip.unsqueeze(2), [P, 16, HP]), ALU.mult))
                    link(dve.tensor_tensor(out, k.ps[:, 6:8, :].rearrange("p a b -> p (a b)"), out, ALU.add))
                    dve.sem_inc(ph.sem("diag_taken"), 1)
                    if c == 1:
                        for g in range(G):
                            dve.wait_ge(ph.sem("carried_done"), 1)
                            link(dve.tensor_tensor(yoff.rearrange("p (h d) -> p h d", h=8),
                                                   k.ps[:, 2 + g, :].rearrange("p (h d) -> p h d", h=8),
                                                   bc(ecs[:, 8 * g:8 * g + 8].unsqueeze(2), [P, 8, HP]), ALU.mult))
                            half = z.ya[:, 1, g * 512:(g + 1) * 512]
                            link(dve.tensor_tensor(half, half, yoff, ALU.add))
                link(dve.tensor_tensor(z.ya, z.ya, z.z, ALU.mult))
                dve.sem_inc(ph.sem("y_ready"), 1)
                dve.wait_ge(ph.sem("squares_summed"), 1)
                k.rstd_vector_before(dve, ph, link, ss, ms, 512)
                k.rstd_vector_after(dve, ph, link, ms, y, t)
                link(dve.tensor_tensor(z.ya.rearrange("p m (g d) -> p m g d", g=2), z.ya.rearrange("p m (g d) -> p m g d", g=2),
                                       bc(y.rearrange("p (m g) -> p m g", m=MT).unsqueeze(3), [P, MT, 2, 512]), ALU.mult))

            @block.tensor
            def _(pe):
                k.transposes(pe, ph, "x", jobs, [6, 7])
                pe.wait_ge(ph.sem("dta_ready"), 1)
                for c in range(MT):
                    pe.matmul(k.ps[:, 4, 16 * c:16 * c + 16], k.upper[:], dta[:, c, :], start=True, stop=True)
                pe.matmul(k.ps[:, 4, 32:48], k.ones[:], dta[:, 0, :], start=True, stop=True).then_inc(ph.sem("cumsum_done"), 1)
                for c in range(MT):
                    if c == 1:
                        pe.wait_ge(ph.sem("states_ready"), 1)
                    for h in range(16):
                        last = pe.matmul(k.ps[:, h // 4, (h % 4) * P:(h % 4 + 1) * P], bc(dta[:, c, h:h + 1], [P, P]),
                                         k.upper[:], start=True, stop=True)
                    last.then_inc(ph.sem("rows_done"), 1)
                    for g in range(G):
                        last = pe.matmul(k.ps[:, 5, g * P:(g + 1) * P], z.xcT[:, 8 + g, c * P:(c + 1) * P],
                                         z.xcT[:, 10 + g, c * P:(c + 1) * P], start=True, stop=True)
                    last.then_inc(ph.sem("cb_done"), 1)
                    pe.wait_ge(ph.sem("mixing_ready"), c + 1)
                    if c == 1:
                        pe.wait_ge(ph.sem("diag_taken"), 1)
                    for h in range(16):
                        last = pe.matmul(k.ps[:, 6 + h // 8, (h % 8) * HP:(h % 8 + 1) * HP], decay[:, h, :], xdt[:, c, h, :],
                                         start=True, stop=True)
                    last.then_inc(ph.sem("diag_done"), 1)
                    if c == 0:
                        pe.wait_ge(ph.sem("late_ready"), 1)
                        for g in range(G):
                            last = pe.matmul(k.ps[:, g, :], bmat[:, g, :], z.ya[:, 1, g * 512:(g + 1) * 512], start=True, stop=True)
                        last.then_inc(ph.sem("states_done"), 1)
                    else:
                        for g in range(G):
                            last = pe.matmul(k.ps[:, 2 + g, :], z.xcT[:, 10 + g, P:2 * P], states[:, g, :], start=True, stop=True)
                        last.then_inc(ph.sem("carried_done"), 1)


def mlstm_phase(k, z):
    with k.phase("mlstm") as ph:
        H, DH = 4, 256
        lq, lk, lv = (ph.linear(n, grouped=False) for n in ("ml_wq", "ml_wk", "ml_wv"))
        a = z.shared
        qT, a = k.at(a, KT, T)
        kT, a = k.at(a, KT, T)
        v, a = k.at(a, MT, H, DH + 1)
        kw, a = k.at(a, H, DH)
        state, a = k.at(a, H, 2, DH + 1)
        g, a = k.at(a, 2, P)
        qk, a = k.at(a, P)
        qkT, a = k.at(a, P)
        num, a = k.at(a, DH + 1)
        st = lambda i, n=8: k.stat[:, i // 8, 8 * (i % 8):8 * (i % 8) + n]
        it, logf, bcum, r, mt, at_, emt, rb = (st(i).rearrange("p (m h) -> p m h", m=MT) for i in range(8))
        tmp, mintra, bend, rmax, m_prev, wt, den, bmt = (st(8 + i) for i in range(8))
        tmp2 = tmp.rearrange("p (m h) -> p m h", m=MT)
        ss, ms, y, t = (st(16 + i) for i in range(4))
        bias = k.p2("small_bias")[:, 16:24]
        w = lambda lin: k.ring[:, lin.chunk0 % SLOTS, :].rearrange("p (h a e) -> p h a e", h=H, a=2)
        xc = z.xcT[:, XBC_T:20, :]
        with k.engines(ph) as block:
            @block.sync
            def _(sp):
                k.load_ahead(sp, ph)

            @block.scalar
            def _(act):
                link = Chain(act, ph.sem("act_chain"))
                act.wait_ge(ph.sem("neg_abs_ready"), 1)
                link(act.activation(tmp2, tmp2, ACT.Exp))
                link(act.activation(tmp2, tmp2, ACT.Ln, bias=1.0))
                act.sem_inc(ph.sem("log_ready"), 1)
                for i in range(4):
                    act.wait_ge(ph.sem("qk_done"), i + 1)
                    dst = (qT if i < 2 else kT)[:, 4 * (i % 2):4 * (i % 2) + 4, :].rearrange("p a t -> p (a t)")
                    act.activation(dst, k.ps[:, 2 * (i % 2):2 * (i % 2) + 2, :].rearrange("p a b -> p (a b)"), ACT.Copy,
                                   scale=1.0 if i < 2 else DH ** -0.5).then_inc(ph.sem("qk_copied"), 1)
                for i in range(2):
                    act.wait_ge(ph.sem("v_done"), i + 1)
                    act.activation(v[:, i, :, 0:DH], k.ps[:, 2 * i:2 * i + 2, :].rearrange("p a (h d) -> p (a h) d", h=2), ACT.Copy
                                   ).then_inc(ph.sem("v_copied"), 1)
                act.wait_ge(ph.sem("weights_arg"), 1)
                act.activation(wt[:, 0:H], wt[:, 0:H], ACT.Exp).then_inc(ph.sem("weights_exp"), 1)
                act.wait_ge(ph.sem("steady"), 1)
                link(act.activation(at_, at_, ACT.Exp))
                link(act.activation(emt, mt, ACT.Exp, scale=-1.0))
                act.sem_inc(ph.sem("steady_exp"), 1)
                for i in range(2 * H):
                    c, h = divmod(i, H)
                    act.wait_ge(ph.sem("g_ready"), i + 1)
                    act.activation(g[:, i % 2, :], g[:, i % 2, :], ACT.Exp, bias=bmt[:, i:i + 1]).then_inc(ph.sem("g_exp"), 1)
                    act.wait_ge(ph.sem("qk_turned"), i + 1)
                    act.activation(qkT, k.ps[:, 6, 0:P], ACT.Copy).then_inc(ph.sem("qkT_ready"), 1)
                act.wait_ge(ph.sem("hid_ready"), 1)
                for i in range(2 * H):
                    c, h = divmod(i, H)
                    link(act.activation(num[:, 0:DH], z.yb[:, c, h * DH:(h + 1) * DH], ACT.Square, accum_out=ss[:, i:i + 1]))
                act.sem_inc(ph.sem("squares_summed"), 1)
                k.rstd_scalar(act, ph, link, ms, y)

            @block.gpsimd
            def _(pool):
                pool.memset(v[:, :, :, DH:DH + 1], 1.0).then_inc(ph.sem("ones_column"), 1)

            @block.vector
            def _(dve):
                link = Chain(dve, ph.sem("dve_chain"))
                link(dve.tensor_tensor(it, z.small[:, :, 16:20], bc(bias[:, 0:4].unsqueeze(1), [P, MT, H]), ALU.add))
                link(dve.tensor_tensor(logf, z.small[:, :, 20:24], bc(bias[:, 4:8].unsqueeze(1), [P, MT, H]), ALU.add))
                link(dve.tensor_scalar(tmp2, logf, -1.0, None, ALU.mult))
                dve.tensor_tensor(tmp2, tmp2, logf, ALU.min).then_inc(ph.sem("neg_abs_ready"), 1)
                link(dve.tensor_scalar(logf, logf, 0.0, None, ALU.min))
                dve.wait_ge(ph.sem("log_ready"), 1)
                link(dve.tensor_tensor(logf, logf, tmp2, ALU.subtract))
                dve.sem_inc(ph.sem("logf_ready"), 1)
                dve.wait_ge(ph.sem("cumsum_done"), 1)
                link(dve.tensor_copy(bcum, k.ps[:, 4, 0:8].rearrange("p (m h) -> p m h", m=MT)))
                link(dve.tensor_copy(bend[:, 0:H], k.ps[:, 4, 8:12]))
                link(dve.tensor_tensor(r, it, bcum, ALU.subtract))
                dve.sem_inc(ph.sem("r_ready"), 1)
                dve.wait_ge(ph.sem("rows_done"), 1)
                rows = [k.ps[:, 4 + c, :].rearrange("p (h s) -> p h s", h=H) for c in range(MT)]
                link(dve.tensor_reduce(rmax[:, 0:H], rows[0], AX, ALU.max))
                link(dve.tensor_scalar(rmax[:, 0:H], rmax[:, 0:H], 0.0, None, ALU.max))
                link(dve.tensor_tensor(wt[:, 0:H], r[:, 0, :], rmax[:, 0:H], ALU.subtract))
                dve.sem_inc(ph.sem("weights_arg"), 1)
                link(dve.memset(m_prev[:, 0:H], 0.0))
                link(dve.tensor_tensor(m_prev[:, H:2 * H], bend[:, 0:H], rmax[:, 0:H], ALU.add))
                for i in range(2 * H):
                    c, h = divmod(i, H)
                    link(dve.tensor_tensor(num[:, 0:P], rows[c][:, h, :], k.causal[:, P:2 * P], ALU.add))
                    link(dve.tensor_reduce(mintra[:, i:i + 1], num[:, 0:P], AX, ALU.max))
                b8, m8, a8 = st(2), st(4), st(5)
                link(dve.tensor_tensor(mintra, mintra, m_prev, ALU.max))
                link(dve.tensor_tensor(m8, mintra, b8, ALU.add))
                link(dve.tensor_tensor(bmt, b8, m8, ALU.subtract))
                link(dve.tensor_tensor(a8, bmt, m_prev, ALU.add))
                dve.sem_inc(ph.sem("steady"), 1)
                dve.wait_ge(ph.sem("weights_exp"), 1)
                dve.wait_ge(ph.sem("k_done"), 1)
                link(dve.tensor_scalar(wt[:, 0:H], wt[:, 0:H], DH ** -0.5, None, ALU.mult))
                link(dve.tensor_tensor(kw, k.ps[:, 0:2, :].rearrange("p a (h d) -> p (a h) d", h=2),
                                       bc(wt[:, 0:H].unsqueeze(2), [P, H, DH]), ALU.mult))
                dve.sem_inc(ph.sem("kw_ready"), 1)
                dve.wait_ge(ph.sem("steady_exp"), 1)
                for j in range(8):
                    dve.wait_ge(ph.sem("state_done"), j + 1)
                    dve.tensor_copy(state[:, j // 2, j % 2, :], k.ps[:, 2 * (j % 2), 0:DH + 1]).then_inc(ph.sem("state_copied"), 1)
                for i in range(2 * H):
                    c, h = divmod(i, H)
                    if i >= 2:
                        dve.wait_ge(ph.sem("mixed"), i - 1)
                    link(dve.tensor_tensor(g[:, i % 2, :], rows[c][:, h, :], k.causal[:, P:2 * P], ALU.add))
                    dve.sem_inc(ph.sem("g_ready"), 1)
                    dve.wait_ge(ph.sem("g_exp"), i + 1)
                    dve.wait_ge(ph.sem("scores_done"), i + 1)
                    dve.tensor_tensor(qk, k.ps[:, 7, 0:P], g[:, i % 2, :], ALU.mult).then_inc(ph.sem("mixed"), 1)
                    dve.wait_ge(ph.sem("out_done"), i + 1)
                    link(dve.tensor_copy(num, k.ps[:, 0, 0:DH + 1]))
                    if c == 1:
                        link(dve.scalar_tensor_tensor(out=num, in0=k.ps[:, 1, 0:DH + 1], scalar=a8[:, i:i + 1], in1=num,
                                                      op0=ALU.mult, op1=ALU.add))
                    link(dve.tensor_scalar(den[:, i:i + 1], num[:, DH:DH + 1], -1.0, None, ALU.mult))
                    link(dve.tensor_tensor(den[:, i:i + 1], den[:, i:i + 1], num[:, DH:DH + 1], ALU.max))
                    link(dve.tensor_tensor(den[:, i:i + 1], den[:, i:i + 1], st(6)[:, i:i + 1], ALU.max))
                    link(dve.reciprocal(den[:, i:i + 1], den[:, i:i + 1]))
                    link(dve.tensor_scalar(z.yb[:, c, h * DH:(h + 1) * DH], num[:, 0:DH], den[:, i:i + 1], None, ALU.mult))
                    dve.sem_inc(ph.sem("out_taken"), 1)
                dve.sem_inc(ph.sem("hid_ready"), 1)
                dve.wait_ge(ph.sem("squares_summed"), 1)
                k.rstd_vector_before(dve, ph, link, ss, ms, DH)
                k.rstd_vector_after(dve, ph, link, ms, y, t)
                link(dve.tensor_tensor(z.yb, z.yb, z.og, ALU.mult))
                heads = z.yb.rearrange("p m (h d) -> p m h d", h=H)
                link(dve.tensor_tensor(heads, heads, bc(y.rearrange("p (m h) -> p m h", m=MT).unsqueeze(3), [P, MT, H, DH]), ALU.mult))

            @block.tensor
            def _(pe):
                for i in range(4):
                    lin = lq if i < 2 else lk
                    if i % 2 == 0:
                        k.wait_chunk(pe, lin.chunk0)
                    if i >= 2:
                        pe.wait_ge(ph.sem("qk_copied"), i - 1)
                    for f in range(4):
                        h, e = divmod(4 * (i % 2) + f, 2)
                        for d in range(2):
                            last = pe.matmul(k.ps[:, 2 * (i % 2) + f // 2, (f % 2) * T:(f % 2 + 1) * T],
                                             w(lin)[:, h, d, e * P:(e + 1) * P], xc[:, 2 * h + d, :], start=(d == 0), stop=(d == 1))
                    last.then_inc(ph.sem("qk_done"), 1)
                pe.wait_ge(ph.sem("logf_ready"), 1)
                for c in range(MT):
                    pe.matmul(k.ps[:, 4, 4 * c:4 * c + 4], k.upper[:], logf[:, c, :], start=True, stop=True)
                pe.matmul(k.ps[:, 4, 8:12], k.ones[:], logf[:, 0, :], start=True, stop=True).then_inc(ph.sem("cumsum_done"), 1)
                pe.wait_ge(ph.sem("qk_copied"), 4)
                pe.sem_inc(k.ring_free[lq.chunk0 % SLOTS], 1)
                k.wait_chunk(pe, lv.chunk0)
                for c in range(MT):
                    for h in range(H):
                        for d in range(2):
                            last = pe.matmul(k.ps[:, 2 * c + h // 2, (h % 2) * DH:(h % 2 + 1) * DH],
                                             z.xmT[:, 2 * h + d, 3 + c * P:3 + (c + 1) * P], w(lv)[:, h, d, :], start=(d == 0), stop=(d == 1))
                    last.then_inc(ph.sem("v_done"), 1)
                pe.wait_ge(ph.sem("r_ready"), 1)
                for c in range(MT):
                    for h in range(H):
                        last = pe.matmul(k.ps[:, 4 + c, h * P:(h + 1) * P], bc(r[:, c, h:h + 1], [P, P]), k.ident[:], start=True, stop=True)
                last.then_inc(ph.sem("rows_done"), 1)
                pe.wait_ge(ph.sem("v_copied"), 2)
                pe.sem_inc(k.ring_free[lv.chunk0 % SLOTS], 1)
                for h in range(H):
                    for d in range(2):
                        last = pe.matmul(k.ps[:, h // 2, (h % 2) * DH:(h % 2 + 1) * DH], xc[:, 2 * h + d, 0:P], w(lk)[:, h, d, :],
                                         start=(d == 0), stop=(d == 1))
                last.then_inc(ph.sem("k_done"), 1)
                pe.wait_ge(ph.sem("kw_ready"), 1)
                pe.sem_inc(k.ring_free[lk.chunk0 % SLOTS], 1)
                pe.wait_ge(ph.sem("ones_column"), 1)
                for j in range(8):
                    if j >= 2:
                        pe.wait_ge(ph.sem("state_copied"), j - 1)
                    h, d = divmod(j, 2)
                    pe.matmul(k.ps[:, 2 * (j % 2), 0:DH + 1], kw[:, h, d * P:(d + 1) * P], v[:, 0, h, :], start=True, stop=True
                              ).then_inc(ph.sem("state_done"), 1)
                pe.wait_ge(ph.sem("state_copied"), 8)
                for i in range(2 * H):
                    c, h = divmod(i, H)
                    toks = slice(c * P, (c + 1) * P)
                    if i >= 1:
                        pe.wait_ge(ph.sem("mixed"), i)
                    for d in range(2):
                        last = pe.matmul(k.ps[:, 7, 0:P], qT[:, 2 * h + d, toks], kT[:, 2 * h + d, toks], start=(d == 0), stop=(d == 1))
                    last.then_inc(ph.sem("scores_done"), 1)
                    pe.wait_ge(ph.sem("mixed"), i + 1)
                    if i >= 1:
                        pe.wait_ge(ph.sem("qkT_ready"), i)
                    pe.transpose(k.ps[:, 6, 0:P], qk, k.ident[:]).then_inc(ph.sem("qk_turned"), 1)
                    if i >= 1:
                        pe.wait_ge(ph.sem("out_taken"), i)
                    if c == 1:
                        for d in range(2):
                            pe.matmul(k.ps[:, 1, 0:DH + 1], qT[:, 2 * h + d, toks], state[:, h, d, :], start=(d == 0), stop=(d == 1))
                    pe.wait_ge(ph.sem("qkT_ready"), i + 1)
                    pe.matmul(k.ps[:, 0, 0:DH + 1], qkT, v[:, c, h, :], start=True, stop=True).then_inc(ph.sem("out_done"), 1)


def mixer_out_phase(k, name, sources, gains, lin_name, at=0):
    with k.phase(name) as ph:
        lin = ph.linear(lin_name)
        mixT, _ = k.at(at, KT * len(sources), T)
        jobs = [j for s in sources for j in feature_groups(s, 0, KT)]
        banks = [4, 5, 6, 7]
        with k.engines(ph) as block:
            @block.sync
            def _(sp):
                k.load_ahead(sp, ph)

            @block.tensor
            def _(pe):
                k.transposes(pe, ph, "mix", jobs, banks)
                pe.wait_ge(ph.sem("mix_copied"), len(jobs))
                k.linear_tok(pe, ph, lin, mixT)

            @block.vector
            def _(dve):
                for i in range(len(jobs)):
                    bank = k.turned(dve, ph, "mix", i, banks)
                    dst = mixT[:, 2 * i:2 * i + 2, :]
                    src = bank.rearrange("p (a t) -> p a t", a=2)
                    gain = gains[i // 4]
                    if gain is None:
                        ins = dve.tensor_copy(dst, src)
                    else:
                        ins = dve.tensor_tensor(dst, src, bc(gain[:, 2 * (i % 4):2 * (i % 4) + 2].unsqueeze(2), [P, 2, T]), ALU.mult)
                    ins.then_inc(ph.sem("mix_copied"), 1)
                add_to_x(k, dve, ph, lin)


class TilesOdd:

    def __init__(self, k):
        a = 0
        self.y, a = k.at(a, MT, D)
        self.v, a = k.at(a, MT, D)
        self.gate, a = k.at(a, MT, D)
        self.mixer = a
        self.fT, a = k.at(a, KT, T)
        self.kT, a = k.at(a, KT, T)
        self.qT, a = k.at(a, KT, T)
        self.e1, a = k.at(a, KT, T)
        self.e2, a = k.at(a, KT, T)
        self.reset, a = k.at(a, KT * T)
        self.lb, a = k.at(a, KT)
        self.oml, a = k.at(a, KT)
        self.t1, a = k.at(a, KT)
        self.t2, a = k.at(a, KT)
        shared = a
        self.att, a = k.at(shared, 8, P)
        self.kd, a = k.at(a, MT, 8, P)
        self.state, a = k.at(a, 2, 8, P)
        self.adec, a = k.at(a, 8, 4)


def odd_in_phase(k, z):
    with k.phase("odd_in") as ph:
        lf, lq, lv, lg = (ph.linear(n) for n in ("hgrn_f", "hgrn_q", "hgrn_v", "hgrn_g"))
        logits = k.p2("lb_logits", DEPTH)
        e = z.e1
        with k.engines(ph) as block:
            @block.sync
            def _(sp):
                k.load_ahead(sp, ph)

            @block.tensor
            def _(pe):
                k.linear_T(pe, ph, lf, k.hT)
                k.linear_T(pe, ph, lq, k.hT)
                k.linear_tok(pe, ph, lv, k.hT)
                k.linear_tok(pe, ph, lg, k.hT)

            @block.gpsimd
            def _(pool):
                link = Chain(pool, ph.sem("pool_chain"))
                link(pool.memset(z.reset, 1.0))
                link(pool.memset(z.reset.rearrange("p (c l) -> p c l", l=HD)[:, :, 0:1], 0.0))
                pool.sem_inc(ph.sem("reset_ready"), 1)

            @block.scalar
            def _(act):
                link = Chain(act, ph.sem("act_chain"))
                act.wait_ge(ph.sem("logits_shifted"), 1)
                link(act.activation(z.t1, z.t1, ACT.Exp))
                link(act.activation(z.t2, z.t2, ACT.Exp))
                act.sem_inc(ph.sem("logits_exp"), 1)
                for n in range(2):
                    pair, free = k.take(act, ph, lf, n)
                    link(act.activation(e[:, 4 * n:4 * n + 4, :].rearrange("p a t -> p (a t)"), pair.rearrange("p a b -> p (a b)"),
                                        ACT.Exp, scale=-1.0))
                    act.sem_inc(free, 1)
                act.sem_inc(ph.sem("f_exp"), 1)
                act.wait_ge(ph.sem("f_sigmoid"), 1)
                for i in range(KT):
                    link.note(act.activation(z.fT[:, i, :], z.fT[:, i, :], ACT.Ln, bias=z.lb[:, i:i + 1], scale=z.oml[:, i:i + 1]))
                link.sync()
                act.sem_inc(ph.sem("logf_ready"), 1)
                for n in range(2):
                    pair, free = k.take(act, ph, lq, n)
                    link(act.activation(z.qT[:, 4 * n:4 * n + 4, :].rearrange("p a t -> p (a t)"), pair.rearrange("p a b -> p (a b)"), ACT.Copy))
                    link(act.activation(z.e2[:, 4 * n:4 * n + 4, :].rearrange("p a t -> p (a t)"), pair.rearrange("p a b -> p (a b)"),
                                        ACT.Exp, scale=-1.0))
                    act.sem_inc(free, 1)
                act.sem_inc(ph.sem("q_exp"), 1)
                for n in range(2):
                    pair, free = k.take(act, ph, lv, n)
                    act.activation(z.v[:, :, n * BLK:(n + 1) * BLK], pair, ACT.Copy).then_inc(free, 1)
                for n in range(2):
                    pair, free = k.take(act, ph, lg, n)
                    link(act.activation(z.gate[:, :, n * BLK:(n + 1) * BLK], pair, ACT.Copy))
                    link(act.activation(z.y[:, :, n * BLK:(n + 1) * BLK], pair, ACT.Exp, scale=-1.0))
                    act.sem_inc(free, 1)
                act.sem_inc(ph.sem("gate_exp"), 1)

            @block.vector
            def _(dve):
                link = Chain(dve, ph.sem("dve_chain"))
                link(dve.tensor_tensor(z.lb, logits[:, 0], logits[:, 1], ALU.max))
                link(dve.tensor_tensor(z.t1, logits[:, 0], z.lb, ALU.subtract))
                link(dve.tensor_tensor(z.t2, logits[:, 1], z.lb, ALU.subtract))
                dve.sem_inc(ph.sem("logits_shifted"), 1)
                dve.wait_ge(ph.sem("logits_exp"), 1)
                link(dve.tensor_tensor(z.oml, z.t1, z.t2, ALU.add))
                link(dve.reciprocal(z.oml, z.oml))
                link(dve.tensor_tensor(z.lb, z.t1, z.oml, ALU.mult))
                link(dve.tensor_tensor(z.oml, z.t2, z.oml, ALU.mult))
                dve.wait_ge(ph.sem("f_exp"), 1)
                link(dve.tensor_scalar(e, e, 1e30, None, ALU.min))
                link(dve.tensor_scalar(z.fT, e, 1.0, None, ALU.add))
                link(dve.reciprocal(z.fT, z.fT))
                link(dve.tensor_tensor(z.kT, e, z.fT, ALU.mult))
                dve.sem_inc(ph.sem("f_sigmoid"), 1)
                link(dve.tensor_tensor(z.kT, z.kT, bc(z.oml.unsqueeze(2), [P, KT, T]), ALU.mult))
                dve.wait_ge(ph.sem("logf_ready"), 1)
                dve.wait_ge(ph.sem("reset_ready"), 1)
                flat = z.fT.rearrange("p a t -> p (a t)")
                link(dve.tensor_tensor_scan(e.rearrange("p a t -> p (a t)"), z.reset, flat, 0.0, ALU.mult, ALU.add))
                link(dve.tensor_copy(z.fT, e))
                dve.wait_ge(ph.sem("q_exp"), 1)
                silu_of(dve, link, z.e2, z.qT, z.qT)
                dve.wait_ge(ph.sem("gate_exp"), 1)
                silu_of(dve, link, z.y, z.gate, z.gate)


def hgrn_phase(k, z):
    with k.phase("hgrn") as ph:
        gc = z.fT.rearrange("p h (c l) -> p (h c) l", l=HD)
        e1 = z.e1.rearrange("p h (c l) -> p (h c) l", l=HD)
        e2 = z.e2.rearrange("p h (c l) -> p (h c) l", l=HD)
        qg = z.reset.rearrange("p (h t) -> p h t", h=8)
        kT = z.kT.rearrange("p h (c l) -> p (h c) l", l=HD)
        ref = bc(gc[:, :, HD // 2:HD // 2 + 1], [P, 32, HD])
        end = bc(gc[:, :, HD - 1:HD], [P, 32, HD])
        ss, ms, y, t = (k.stat[:, i, 0:16] for i in range(4))
        jobs = [[(z.e1[:, 4 * j + i, m * P:(m + 1) * P], i * P) for i in range(4)] for m in range(MT) for j in range(2)]
        with k.engines(ph) as block:
            @block.sync
            def _(sp):
                k.load_ahead(sp, ph)

            @block.vector
            def _(dve):
                link = Chain(dve, ph.sem("dve_chain"))
                link(dve.tensor_tensor(e1, end, gc, ALU.subtract))
                dve.sem_inc(ph.sem("to_end"), 1)
                dve.wait_ge(ph.sem("to_end_exp"), 1)
                link(dve.tensor_tensor(e1, e1, kT, ALU.mult))
                dve.sem_inc(ph.sem("keys_decayed"), 1)
                link(dve.tensor_tensor(e2, gc, ref, ALU.subtract))
                dve.sem_inc(ph.sem("to_middle"), 1)
                dve.wait_ge(ph.sem("middle_exp"), 1)
                link(dve.tensor_tensor(qg, qg, z.qT, ALU.mult))
                link(dve.tensor_tensor(z.qT, z.qT, z.e2, ALU.mult))
                link(dve.tensor_tensor(z.kT, z.kT, z.fT, ALU.mult))
                dve.sem_inc(ph.sem("operands_ready"), 1)
                for m in range(MT):
                    dve.wait_ge(ph.sem("att_done"), m + 1)
                    if m == 1:
                        dve.wait_ge(ph.sem("own_done"), 1)
                    link(dve.tensor_scalar(z.att.rearrange("p h l -> p (h l)"), k.ps[:, 0:2, :].rearrange("p a b -> p (a b)"),
                                           3e38, -3e38, ALU.min, ALU.max))
                    link(dve.tensor_tensor(z.att, z.att, bc(k.chunk_upper[:].unsqueeze(1), [P, 8, P]), ALU.mult))
                    dve.sem_inc(ph.sem("att_masked"), 1)
                    dve.wait_ge(ph.sem("own_done"), m + 1)
                    link(dve.tensor_copy(z.y[:, m, :], k.ps[:, 2:4, :].rearrange("p a b -> p (a b)")))
                    dve.sem_inc(ph.sem("own_taken"), 1)
                for c in range(1, 4):
                    dve.wait_ge(ph.sem("local_done"), c)
                    new, old = z.state[:, c % 2], z.state[:, (c + 1) % 2]
                    local = k.ps[:, 6:8, :].rearrange("p a (h e) -> p (a h) e", h=4)
                    if c == 1:
                        link(dve.tensor_copy(new, local))
                    else:
                        for h in range(8):
                            link.note(dve.scalar_tensor_tensor(out=new[:, h, :], in0=old[:, h, :], scalar=z.adec[:, h, c - 1:c],
                                                               in1=local[:, h, :], op0=ALU.mult, op1=ALU.add))
                        link.sync()
                    dve.sem_inc(ph.sem("state_ready"), 1)
                    dve.wait_ge(ph.sem("carried_done"), c)
                    rows = slice(HD * (c % 2), HD * (c % 2) + HD)
                    o = z.y[rows, c // 2, :]
                    link(dve.tensor_tensor(o, k.ps[rows, 4:6, :].rearrange("p a b -> p (a b)"), o, ALU.add))
                    dve.sem_inc(ph.sem("carried_taken"), 1)
                dve.sem_inc(ph.sem("y_ready"), 1)
                dve.wait_ge(ph.sem("squares_summed"), 1)
                k.rstd_vector_before(dve, ph, link, ss, ms, P)
                k.rstd_vector_after(dve, ph, link, ms, y, t)
                link(dve.tensor_tensor(z.y, z.y, z.gate, ALU.mult))
                heads = z.y.rearrange("p m (h d) -> p (m h) d", h=8)
                link(dve.tensor_tensor(heads, heads, bc(y.unsqueeze(2), [P, 16, P]), ALU.mult))

            @block.scalar
            def _(act):
                link = Chain(act, ph.sem("act_chain"))
                act.wait_ge(ph.sem("to_end"), 1)
                link(act.activation(z.e1, z.e1, ACT.Exp))
                act.sem_inc(ph.sem("to_end_exp"), 1)
                act.wait_ge(ph.sem("to_middle"), 1)
                link.note(act.activation(z.adec, z.fT.rearrange("p h (c l) -> p h c l", l=HD)[:, :, :, HD - 1], ACT.Exp))
                link(act.activation(qg, z.fT, ACT.Exp))
                link(act.activation(z.fT, z.e2, ACT.Exp, scale=-1.0))
                link(act.activation(z.e2, z.e2, ACT.Exp))
                act.sem_inc(ph.sem("middle_exp"), 1)
                for i in range(4):
                    bank = k.turned(act, ph, "kd", i, [4, 5])
                    act.activation(z.kd[:, i // 2, 4 * (i % 2):4 * (i % 2) + 4, :].rearrange("p a b -> p (a b)"), bank, ACT.Copy
                                   ).then_inc(ph.sem("kd_copied"), 1)
                act.wait_ge(ph.sem("y_ready"), 1)
                for i in range(16):
                    m, h = divmod(i, 8)
                    link.note(act.activation(z.e1[:, h, 0:P] if m == 0 else z.e1[:, h, P:T], z.y[:, m, h * P:(h + 1) * P], ACT.Square,
                                             accum_out=ss[:, i:i + 1]))
                link.sync()
                act.sem_inc(ph.sem("squares_summed"), 1)
                k.rstd_scalar(act, ph, link, ms, y)

            @block.tensor
            def _(pe):
                pe.wait_ge(ph.sem("keys_decayed"), 1)
                k.transposes(pe, ph, "kd", jobs, [4, 5])
                pe.wait_ge(ph.sem("operands_ready"), 1)
                for m in range(MT):
                    toks = slice(m * P, (m + 1) * P)
                    if m == 1:
                        pe.wait_ge(ph.sem("att_masked"), 1)
                    for h in range(8):
                        last = pe.matmul(k.ps[:, h // 4, (h % 4) * P:(h % 4 + 1) * P], z.kT[:, h, toks], z.qT[:, h, toks], start=True, stop=True)
                    last.then_inc(ph.sem("att_done"), 1)
                    pe.wait_ge(ph.sem("att_masked"), m + 1)
                    if m == 1:
                        pe.wait_ge(ph.sem("own_taken"), 1)
                    for h in range(8):
                        last = pe.matmul(k.ps[:, 2 + h // 4, (h % 4) * P:(h % 4 + 1) * P], z.att[:, h, :], z.v[:, m, h * P:(h + 1) * P],
                                         start=True, stop=True)
                    last.then_inc(ph.sem("own_done"), 1)
                pe.wait_ge(ph.sem("kd_copied"), 4)
                for c in range(3):
                    rows, m = slice(HD * (c % 2), HD * (c % 2) + HD), c // 2
                    for h in range(8):
                        last = pe.matmul(k.ps[:, 6 + h // 4, (h % 4) * P:(h % 4 + 1) * P], z.kd[rows, m, h, :], z.v[rows, m, h * P:(h + 1) * P],
                                         start=True, stop=True)
                    last.then_inc(ph.sem("local_done"), 1)
                    pe.wait_ge(ph.sem("state_ready"), c + 1)
                    if c >= 1:
                        pe.wait_ge(ph.sem("carried_taken"), c)
                    n = c + 1
                    out = slice(HD * (n % 2), HD * (n % 2) + HD)
                    for h in range(8):
                        last = pe.matmul(k.ps[out, 4 + h // 4, (h % 4) * P:(h % 4 + 1) * P], qg[:, h, n * HD:(n + 1) * HD], z.state[:, n % 2, h, :],
                                         start=True, stop=True)
                    last.then_inc(ph.sem("carried_done"), 1)


def cross_attention(k, layer):
    a = 0
    memT, a = k.at(a, KT, T)
    qT, a = k.at(a, KT, T)
    kT, a = k.at(a, KT, T)
    v, a = k.at(a, MT, D)
    oT, a = k.at(a, KT, T)
    probs, a = k.at(a, 2, 4, T)
    probsT, a = k.at(a, 2, 2, 4, P)
    sums, a = k.at(a, MT, 4)
    nmax, a = k.at(a, MT, 4)
    norm_phase_over(k, a, "norm_xattn", k.x, k.p2("norm_xattn"), k.hT)
    norm_phase_over(k, a, "norm_mem", qT.rearrange("p a t -> p (a t)").rearrange("p (m d) -> p m d", m=MT), k.p2("norm_mem"), memT,
                    source=k.dram["mem"])
    with k.phase("xa_in") as ph:
        lq, lk, lv = (ph.linear(n) for n in ("xa_q", "xa_k", "xa_v"))
        with k.engines(ph) as block:
            @block.sync
            def _(sp):
                k.load_ahead(sp, ph)

            @block.tensor
            def _(pe):
                k.linear_T(pe, ph, lq, k.hT)
                k.linear_T(pe, ph, lk, memT)
                k.linear_tok(pe, ph, lv, memT)

            @block.scalar
            def _(act):
                for lin, dst in ((lq, qT), (lk, kT)):
                    for n in range(2):
                        pair, free = k.take(act, ph, lin, n)
                        act.activation(dst[:, 4 * n:4 * n + 4, :].rearrange("p a t -> p (a t)"), pair.rearrange("p a b -> p (a b)"), ACT.Copy
                                       ).then_inc(free, 1)
                for n in range(2):
                    pair, free = k.take(act, ph, lv, n)
                    act.activation(v[:, :, n * BLK:(n + 1) * BLK], pair, ACT.Copy).then_inc(free, 1)

    batches = []
    for m in range(MT):
        toks = slice(m * P, (m + 1) * P)
        batches.append(Batch(lambda h, c, toks=toks: qT[:, 2 * h + c, toks], lambda h, c: kT[:, 2 * h + c, :],
                             lambda h, kt, j: v[:, kt, h * T + j * P:h * T + (j + 1) * P], T, T ** -0.5, oT[:, :, toks],
                             contract=2, pieces=2))
    attention_phase(k, "xa_attend", batches, probs, probsT, sums, nmax, [k.ps[:, 6:8, :]])
    with k.phase("xa_out") as ph:
        lin = ph.linear("xa_o")
        with k.engines(ph) as block:
            @block.sync
            def _(sp):
                k.load_ahead(sp, ph)

            @block.tensor
            def _(pe):
                k.linear_tok(pe, ph, lin, oT)

            @block.vector
            def _(dve):
                add_to_x(k, dve, ph, lin)


def peer(k, layer):
    a = 0
    xt, a = k.at(a, MT, D)
    index, a = k.at(a, MT * SLOTS_PER_TOKEN + 2 * GATHER)
    gates, a = k.at(a, MT * SLOTS_PER_TOKEN)
    start = a
    qT, a = k.at(a, 16, T)
    scores, a = k.at(a, MT, 16, PE_KEYS)
    best, a = k.at(a, MT, 16, PE_TOP)
    best_at, a = k.at(a, MT, 16, PE_TOP)
    cand, a = k.at(a, PE_HEADS, PE_TOP * PE_TOP)
    chosen, a = k.at(a, PE_HEADS, PE_TOP)
    chosen_at, a = k.at(a, 2, SLOTS_PER_TOKEN)
    raw, a = k.at(a, 16, PE_TOP)
    raw2, a = k.at(a, PE_HEADS, PE_TOP)
    hot, a = k.at(a, SLOTS_PER_TOKEN, PE_TOP)
    iota, a = k.at(a, PE_TOP)
    part, a = k.at(a, 2, SLOTS_PER_TOKEN)
    norm_phase_over(k, start, "norm_ffn", k.x, k.p2("norm_ffn"), k.hT, loads=[(k.gain_row[:], k.dram["gain_rows"][1 + layer])], out_tok=xt)
    rawi, raw2i, parti = raw.bitcast(U32), raw2.bitcast(U32), part.bitcast(U32)
    with k.phase("peer_route") as ph:
        lq, sub = ph.linear("peer_q"), ph.linear("subkeys", grouped=False)
        with k.engines(ph) as block:
            @block.sync
            def _(sp):
                k.load_ahead(sp, ph)

            @block.gpsimd
            def _(pool):
                pool.iota(iota, pattern=[[1, PE_TOP]], base=0, channel_multiplier=0, allow_small_or_imprecise_dtypes=True
                          ).then_inc(ph.sem("iota_ready"), 1)

            @block.tensor
            def _(pe):
                k.linear_T(pe, ph, lq, k.hT)
                k.wait_chunk(pe, sub.chunk0)
                keys = k.ring[:, sub.chunk0 % SLOTS, :]
                pe.wait_ge(ph.sem("queries_ready"), 4)
                for m in range(MT):
                    for hp in range(16):
                        last = pe.matmul(k.ps[:, 4 * m + hp // 4, (hp % 4) * P:(hp % 4 + 1) * P], qT[:, hp, m * P:(m + 1) * P],
                                         keys[:, hp * P:(hp + 1) * P], start=True, stop=True)
                    last.then_inc(ph.sem("scores_done"), 1)

            @block.scalar
            def _(act):
                link = Chain(act, ph.sem("act_chain"))
                for n in range(4):
                    pair, free = k.take(act, ph, lq, n)
                    link(act.activation(qT[:, 4 * n:4 * n + 4, :].rearrange("p a t -> p (a t)"), pair.rearrange("p a b -> p (a b)"), ACT.Copy))
                    act.sem_inc(free, 1)
                    act.sem_inc(ph.sem("queries_ready"), 1)
                for m in range(MT):
                    act.wait_ge(ph.sem("scores_done"), m + 1)
                    act.activation(scores[:, m].rearrange("p a b -> p (a b)"), k.ps[:, 4 * m:4 * m + 4, :].rearrange("p a b -> p (a b)"), ACT.Copy
                                   ).then_inc(ph.sem("scores_copied"), 1)
                act.sem_inc(k.ring_free[sub.chunk0 % SLOTS], 1)
                for m in range(MT):
                    act.wait_ge(ph.sem("chosen_shifted"), m + 1)
                    act.activation(chosen, chosen, ACT.Exp).then_inc(ph.sem("chosen_exp"), 1)

            @block.vector
            def _(dve):
                link = Chain(dve, ph.sem("dve_chain"))
                link(dve.memset(index, 0.0))

                def top16(values, to, at):
                    link(dve.max(to[:, 0:8], values))
                    link(dve.max_index(at[:, 0:8], to[:, 0:8], values))
                    link(dve.match_replace(values, to[:, 0:8], values, -3e38))
                    link(dve.max(to[:, 8:16], values))
                    link(dve.max_index(at[:, 8:16], to[:, 8:16], values))

                dve.wait_ge(ph.sem("iota_ready"), 1)
                for m in range(MT):
                    dve.wait_ge(ph.sem("scores_copied"), m + 1)
                    for hp in range(16):
                        top16(scores[:, m, hp, :], best[:, m, hp, :], rawi[:, hp, :])
                    link(dve.tensor_copy(best_at[:, m], rawi))
                    pairs = best[:, m].rearrange("p (h two) i -> p h two i", two=2)
                    grid = [P, PE_HEADS, PE_TOP, PE_TOP]
                    link(dve.tensor_tensor(cand.rearrange("p h (i j) -> p h i j", i=PE_TOP), bc(pairs[:, :, 0, :].unsqueeze(3), grid),
                                           bc(pairs[:, :, 1, :].unsqueeze(2), grid), ALU.add))
                    for h in range(PE_HEADS):
                        top16(cand[:, h, :], chosen[:, h, :], raw2i[:, h, :])
                    link(dve.tensor_copy(hot[:, 0:PE_HEADS, 0:1], chosen[:, :, 0:1]))
                    link(dve.tensor_tensor(chosen, chosen, bc(hot[:, 0:PE_HEADS, 0:1], [P, PE_HEADS, PE_TOP]), ALU.subtract))
                    dve.sem_inc(ph.sem("chosen_shifted"), 1)
                    flat = raw2i.rearrange("p h i -> p (h i)")
                    link(dve.tensor_scalar(parti[:, 0], flat, 4, None, ALU.logical_shift_right))
                    link(dve.tensor_scalar(parti[:, 1], flat, 15, None, ALU.bitwise_and))
                    link(dve.tensor_copy(chosen_at, parti))
                    at_pairs = best_at[:, m].rearrange("p (h two) i -> p h two i", two=2)
                    for i in range(2):
                        link(dve.tensor_tensor(hot, bc(chosen_at[:, i].unsqueeze(2), [P, SLOTS_PER_TOKEN, PE_TOP]),
                                               bc(iota.unsqueeze(1), [P, SLOTS_PER_TOKEN, PE_TOP]), ALU.is_equal))
                        hot4 = hot.rearrange("p (h s) i -> p h s i", h=PE_HEADS)
                        link(dve.tensor_tensor(hot4, hot4, bc(at_pairs[:, :, i, :].unsqueeze(2), grid), ALU.mult))
                        link(dve.tensor_reduce(part[:, i], hot, AX, ALU.add))
                    slots = slice(m * SLOTS_PER_TOKEN, (m + 1) * SLOTS_PER_TOKEN)
                    link(dve.scalar_tensor_tensor(out=index[:, slots], in0=part[:, 0], scalar=float(PE_KEYS), in1=part[:, 1],
                                                  op0=ALU.mult, op1=ALU.add))
                    dve.wait_ge(ph.sem("chosen_exp"), m + 1)
                    total = hot[:, 0:PE_HEADS, 1:2]
                    link(dve.tensor_reduce(total, chosen, AX, ALU.add))
                    link(dve.reciprocal(total, total))
                    link(dve.tensor_tensor(gates[:, slots].rearrange("p (h i) -> p h i", h=PE_HEADS), chosen,
                                           bc(total, [P, PE_HEADS, PE_TOP]), ALU.mult))

    a = start
    rows, a = k.at(a, 2, GATHER, 2 * D)
    table = k.dram[f"experts{layer}"]
    staged = k.stage_index
    with k.phase("peer_experts") as ph:
        dots, _ = k.at(a, 2, 2, GATHER)
        with k.engines(ph) as block:
            @block.gpsimd
            def _(pool):
                with pool.Fori(0, MT * N_GATHER // 2) as step:
                    for b in range(2):
                        pool.wait_ge(ph.sem(f"slot_ready{b}"), step + 1)
                        pool.sem_inc(ph.sem("gathers_begun"), 1)
                        for e in range(GATHER):
                            pool.indirect_dma_start(rows[:, b, e, :], None, table, bass.IndirectOffsetOnAxis(ap=staged[:, b, e:e + 1], axis=0)
                                                    ).then_inc(k.gathered[b][e], 16)

            @block.vector
            def _(dve):
                chain = ph.sem("dve_chain")
                for b in range(2):
                    dve.tensor_copy(staged[:, b, :], index[:, b * GATHER:(b + 1) * GATHER]).then_inc(ph.sem(f"slot_ready{b}"), 1)
                for m in range(MT):
                    steps = N_GATHER // 2
                    with dve.Fori(m * steps, (m + 1) * steps) as step:
                        per_step = 2 * (GATHER + 2)
                        for b in range(2):
                            base = step * per_step + b * (GATHER + 2)
                            for e in range(GATHER):
                                dve.wait_ge(k.gathered[b][e], step * 16 + 16 + layer * MT * N_GATHER // 2 * 16)
                                dve.tensor_tensor_reduce(rows[:, b, e, 0:D], rows[:, b, e, 0:D], xt[:, m, :], 1.0, 0.0, ALU.mult, ALU.add,
                                                         dots[:, 0, b, e:e + 1]).then_inc(ph.sem("dots_done"), 1)
                            dve.tensor_copy(staged[:, b, :], index[:, bass.ds((step + 1) * 2 * GATHER + b * GATHER, GATHER)]).then_inc(chain, 1)
                            dve.wait_ge(ph.sem("gelu_done"), step * 2 + b + 1)
                            dve.tensor_tensor(dots[:, 1, b, :], dots[:, 1, b, :], gates[:, bass.ds(step * 2 * GATHER + b * GATHER, GATHER)], ALU.mult
                                              ).then_inc(chain, 1)
                            dve.wait_ge(chain, base + 2)
                            for e in range(GATHER):
                                x = k.x[:, m, :]
                                ins = dve.scalar_tensor_tensor(out=x, in0=rows[:, b, e, D:2 * D], scalar=dots[:, 1, b, e:e + 1], in1=x,
                                                               op0=ALU.mult, op1=ALU.add)
                                ins.then_inc(chain, 1)
                                dve.wait_ge(chain, base + 3 + e)
                            dve.sem_inc(ph.sem(f"slot_ready{b}"), 1)

            @block.scalar
            def _(act):
                with act.Fori(0, MT * N_GATHER // 2) as step:
                    for b in range(2):
                        act.wait_ge(ph.sem("dots_done"), step * 2 * GATHER + (b + 1) * GATHER)
                        act.activation(dots[:, 1, b, :], dots[:, 0, b, :], ACT.Gelu).then_inc(ph.sem("gelu_done"), 1)


def norm_phase_over(k, start, name, src, gain, dst, **more):
    norm_phase(k, name, src, gain, dst, scratch=start, **more)


def second_stack(k):
    even, odd = TilesEven(k), TilesOdd(k)
    for layer in range(DEPTH):
        norm_phase(k, "norm_mix", k.x, k.p2("norm_mix"), k.hT, loads=[(k.par[:, 0:P2_W], k.dram["params2"][layer])])
        if layer % 2 == 0:
            even_in_phase(k, even)
            ssd_phase(k, even)
            mlstm_phase(k, even)
            mixer_out_phase(k, "even_out", [even.ya, even.yb], [k.p2("ssd_norm"), k.p2("ml_norm")], "ev_out")
        else:
            odd_in_phase(k, odd)
            hgrn_phase(k, odd)
            mixer_out_phase(k, "odd_out", [odd.y], [k.p2("hgrn_norm")], "od_out", at=odd.mixer)
        cross_attention(k, layer)
        peer(k, layer)
    norm_phase(k, "final_norm", k.x, None, None, loads=[(k.gain_row[:], k.dram["gain_rows"][3])], out_tok=k.x)
    assert k.stream_at == len(STREAM_2) and k.next_chunk == CHUNKS_2


def build(nc, dram):
    with ExitStack() as stack:
        k = Kernel(nc, dram, stack)
        constants_phase(k)
        with nc.Fori(0, DEPTH) as layer:
            k.layer = layer
            first_layer(k)
        k.layer = None
        final = [(k.gain_row[:], dram["gain_rows"][0])]
        norm_phase(k, "first_final_norm", k.x, None, None, loads=final, out_tok=k.x)
        if STAGE >= 2:
            k.stream, k.stream_at, k.next_chunk = STREAM_2, 0, 0
            second_stack(k)
        with k.phase("store") as ph:
            with k.engines(ph) as block:
                @block.sync
                def _(sp):
                    sp.dma_start(dram["out"], k.x[:]).then_inc(ph.sem("stored"), 16)
                    sp.wait_ge(ph.sem("stored"), 16)




def rows_of(w, order=None):
    return w.reshape(w.shape[0] // P, P, w.shape[1]).transpose(1, 0, 2)


def chunked(w):
    kk, n = w.shape
    if n % BLK:
        w = np.concatenate([w, np.zeros((kk, BLK - n % BLK), w.dtype)], axis=1)
        n = w.shape[1]
    b = w.reshape(kk // P, P, n // BLK, BLK).transpose(2, 0, 1, 3).reshape(-1, P, BLK)
    if len(b) % CHUNK_BLOCKS:
        b = np.concatenate([b, np.zeros((CHUNK_BLOCKS - len(b) % CHUNK_BLOCKS, P, BLK), w.dtype)])
    return b.reshape(-1, CHUNK_BLOCKS, P, BLK).transpose(0, 2, 1, 3).reshape(-1, P, CHUNK)


def col(v):
    return v.reshape(-1, P).T


def every(v):
    return np.broadcast_to(v.reshape(1, -1), (P, v.size))


PAIRED = [h for i in range(4) for h in (i, 4 + i)]


def paired(w, width=HD):
    return w.reshape(w.shape[0], 8, width)[:, PAIRED].reshape(w.shape[0], -1)


def layer_chunks(i, a):
    sizes = [512, 128, 128, 128, 128, 128, 128, 24, 512, 128, 128, 256, 256, 32]
    names = ["q", "kc", "vc", "ks", "vs", "kw", "vw", "g", "bq", "bk", "bv", "cq", "ckv", "kpe"]
    cut = dict(zip(names, np.split(a["w_in"][i], np.cumsum(sizes)[:-1], axis=1)))
    cat = lambda *names: np.concatenate([cut[n] for n in names], axis=1)
    gate, up = a["w_ffn_gate"][i], a["w_ffn_up"][i]
    both = np.stack([gate.reshape(D, FF_T // 2, 256), up.reshape(D, FF_T // 2, 256)], axis=2).reshape(D, -1)
    w1 = np.concatenate([a["a_cmp_w1_k"][i].reshape(32, HD, 256).transpose(1, 0, 2),
                         a["a_cmp_w1_v"][i].reshape(32, HD, 256).transpose(1, 0, 2)])
    w1 = w1.reshape(P, 4, CHUNK).transpose(1, 0, 2)
    pair_rows = lambda w: paired(w.T).T
    parts = [chunked(paired(cut["q"])), chunked(cat("ks", "kw", "bk", "kc")), chunked(paired(cut["bq"])),
             chunked(cat("vc", "vs", "vw", "bv")), chunked(cat("cq", "ckv")), chunked(a["w_branch_gate"][i]), w1,
             chunked(a["c_w_q_up"][i]), chunked(a["c_w_kv_up"][i])]
    parts += [chunked(pair_rows(a[f"w_branch_{c}"][i])) for c in "abc"]
    parts += [chunked(a["w_out"][i]), chunked(both), chunked(a["w_ffn_down"][i]), chunked(a["w_ple_gate"][i]),
              chunked(a["w_ple_proj"][i])]
    small = np.concatenate([cut["kpe"], cut["g"].reshape(D, 8, 3).transpose(0, 2, 1).reshape(D, 24)], axis=1)
    two = lambda w: rows_of(w).reshape(P, -1)
    pos = np.concatenate([a["a_cmp_pos_k"][i].T, a["a_cmp_pos_v"][i].T])
    params = np.concatenate([col(a["mix_norm"][i]), col(a["ffn_norm"][i]), col(a["ple_norm"][i]), col(a["c_q_norm"][i]),
                             col(a["c_kv_norm"][i]), two(small), two(a["a_cmp_w2_k"][i]), two(a["a_cmp_w2_v"][i]), pos,
                             every(a["b_sinks"][i])], axis=1)
    return parts, params


def in_pairs(w):
    return w.reshape(4, 2, P, T).transpose(2, 0, 1, 3).reshape(1, P, CHUNK)


def second_chunks(a):
    w = a["ev_w_in_2"][0]
    z, xbc, dt, xm, og, ig, fg = np.split(w, np.cumsum([D, 1536, 16, D, D, 4])[:6], axis=1)
    attend = lambda i: [chunked(a["xa_wq_2"][i]), chunked(a["xa_wkv_2"][i][:, :D]), chunked(a["xa_wkv_2"][i][:, D:]),
                        chunked(a["xa_wo_2"][i]), chunked(a["peer_wq_2"][i]),
                        a["peer_subkeys_2"][i].reshape(16, PE_KEYS, P).transpose(2, 0, 1).reshape(1, P, CHUNK)]
    q, f, v, g = np.split(a["od_w_in_2"][0], 4, axis=1)
    parts = ([chunked(z), chunked(xbc), chunked(xm), chunked(og), in_pairs(a["ml_wq_2"][0]), in_pairs(a["ml_wk_2"][0]),
              in_pairs(a["ml_wv_2"][0]), chunked(a["ev_w_out_2"][0])] + attend(0)
             + [chunked(f), chunked(q), chunked(v), chunked(g), chunked(a["od_w_out_2"][0])] + attend(1))
    taps = lambda w: w.T.reshape(-1, P, 4).transpose(1, 0, 2).reshape(P, -1)
    small = rows_of(np.concatenate([dt, ig, fg], axis=1)).reshape(P, -1)
    bias = np.concatenate([a["ssd_dt_bias_2"][0], a["ml_i_bias_2"][0], a["ml_f_bias_2"][0]])
    params = []
    for i in range(DEPTH):
        params.append(np.concatenate(
            [col(a[n][i]) for n in ("norm_mix_2", "norm_xattn_2", "norm_mem_2", "norm_ffn_2")]
            + [small, every(bias), every(a["ssd_a_log_2"][0]), every(a["ssd_d_skip_2"][0]), taps(a["ssd_conv_w_2"][0]),
               col(a["ssd_conv_b_2"][0]), col(a["ssd_norm_2"][0]), taps(a["ml_conv_w_2"][0]), col(a["ml_conv_b_2"][0]),
               col(a["ml_norm_2"][0]), col(a["hgrn_lb_logits_2"].reshape(-1)), col(a["hgrn_norm_2"][0])], axis=1))
    arrays = {"params2": np.stack(params), "mem": a["mem_2"][0].reshape(MT, P, D).transpose(1, 0, 2)}
    for i in range(DEPTH):
        arrays[f"experts{i}"] = np.concatenate([a["peer_u_2"][i], a["peer_v_2"][i]], axis=1)
    return parts, arrays


def kernel(**inputs):
    import concourse.bacc as bacc
    from concourse.bass_utils import run_bass_kernel_spmd

    a = {n: np.asarray(v) for n, v in inputs.items()}
    tok = lambda v: v.reshape(MT, P, -1).transpose(1, 0, 2)
    layers = [layer_chunks(i, a) for i in range(DEPTH)]
    parts = [c for chunks, _ in layers for c in chunks]
    if STAGE >= 2:
        second, params2 = second_chunks(a)
        parts += second
    else:
        parts += [np.zeros((SLOTS, P, CHUNK), np.float32)]
    freq = np.concatenate([np.power(np.float32(10000.0), -np.arange(0, d, 2, dtype=np.float32) / d) for d in (64, 32)])
    arrays = {
        "x": tok(a["x"][0]),
        "positions": a["positions"].reshape(MT, P).T,
        "freq": every(freq.astype(np.float32)),
        "pT": a["p"][:, 0].transpose(0, 2, 1).reshape(DEPTH, 2, P, T).transpose(0, 2, 1, 3),
        "params1": np.stack([p for _, p in layers]),
        "gain_rows": np.stack([every(v) for v in (a["final_norm"], a["norm_ffn_2"][0], a["norm_ffn_2"][1], a["norm_final_2"])]),
        "stream": np.concatenate(parts),
    }
    if STAGE >= 2:
        arrays.update(params2)
    arrays = {f"in_{n}": np.ascontiguousarray(v) for n, v in arrays.items()}
    nc = bacc.Bacc("TRN2", target_bir_lowering=False, num_devices=1)
    dram = {n[3:]: nc.dram_tensor(n, v.shape, mybir.dt.from_np(v.dtype), kind="ExternalInput").ap() for n, v in arrays.items()}
    dram["out"] = nc.dram_tensor("out", (P, MT, D), F32, kind="ExternalOutput").ap()
    build(nc, dram)
    result = run_bass_kernel_spmd(nc, [arrays], core_ids=[0]).results[0]["out"]
    return result.transpose(1, 0, 2).reshape(1, T, D)
```

```python
from contextlib import ExitStack, contextmanager

import numpy as np
import concourse.bass as bass
from concourse import mybir

F32 = mybir.dt.float32
F32R = mybir.dt.float32r
I32 = mybir.dt.int32
U32 = mybir.dt.uint32
ALU = mybir.AluOpType
ACT = mybir.ActivationFunctionType
AX = mybir.AxisListType.X

P = 128
D = 1024
KT = D // P
T = 256
MT = T // P
DEPTH = 2
EPS = 1e-6
NEG = -1e30
HD = 64
BLK = 512
CHUNK_BLOCKS = 4
CHUNK = BLK * CHUNK_BLOCKS
ARENA = 28600
SLOTS = 8
N_CMP = (T - 32) // 16 + 1
D_FF = 2816
FF_T = D_FF // P
XBC_T = 12
PE_HEADS, PE_KEYS, PE_TOP = 8, 128, 16
SLOTS_PER_TOKEN = PE_HEADS * PE_TOP
GATHER = 4
N_GATHER = SLOTS_PER_TOKEN // GATHER



def columns(*sizes):
    at, out = 0, {}
    for name, n in sizes:
        out[name] = (at, n)
        at += n
    return out, at


P1, P1_W = columns(("mix_norm", KT), ("ffn_norm", KT), ("ple_norm", KT), ("cq_norm", 2), ("ckv_norm", 2),
                   ("w_small", KT * 56), ("w2k", 2 * HD), ("w2v", 2 * HD), ("posT", 32), ("sinks", 8))
P2, P2_W = columns(("norm_mix", KT), ("norm_xattn", KT), ("norm_mem", KT), ("norm_ffn", KT),
                   ("w_small", KT * 24), ("small_bias", 24), ("a_log", 16), ("d_skip", 16),
                   ("conv_w", XBC_T * 4), ("conv_b", XBC_T), ("ssd_norm", KT),
                   ("ml_conv_w", KT * 4), ("ml_conv_b", KT), ("ml_norm", KT),
                   ("lb_logits", DEPTH * KT), ("hgrn_norm", KT))
PAR_W = max(P1_W, P2_W)


STREAM_1 = [("rot0", 8, 1), ("rot1", 8, 1), ("rot2", 8, 1), ("values", 8, 1), ("latents", 8, 1),
            ("gates", 8, 6), ("cmp_w1", 16, 1), ("q_up", 2, 2), ("kv_up", 2, 2),
            ("branch_a", 4, 2), ("branch_b", 4, 2), ("branch_c", 4, 2), ("w_out", 8, 2),
            ("ffn_in", 8, 11), ("ffn_down", FF_T, 2), ("ple_gate", 8, 2), ("ple_proj", 2, 2)]
ATTEND_2 = [("xa_q", 8, 2), ("xa_k", 8, 2), ("xa_v", 8, 2), ("xa_o", 8, 2), ("peer_q", 8, 4), ("subkeys", 4, 1)]
STREAM_2 = ([("ssd_z", 8, 2), ("xbc", 8, 3), ("xm", 8, 2), ("og", 8, 2), ("ml_wq", 4, 1), ("ml_wk", 4, 1),
             ("ml_wv", 4, 1), ("ev_out", 16, 2)] + ATTEND_2
            + [("hgrn_f", 8, 2), ("hgrn_q", 8, 2), ("hgrn_v", 8, 2), ("hgrn_g", 8, 2), ("od_out", 8, 2)] + ATTEND_2)


def chunks_of(k, n):
    return -(-k * n // CHUNK_BLOCKS)


CHUNKS_1 = sum(chunks_of(k, n) for _, k, n in STREAM_1)
CHUNKS_2 = sum(chunks_of(k, n) for _, k, n in STREAM_2)
VIRTUAL_1 = -(-CHUNKS_1 // SLOTS) * SLOTS
USES_1 = [sum(1 for v in range(CHUNKS_1) if v % SLOTS == s) for s in range(SLOTS)]


def bc(ap, shape):
    return ap.to_broadcast(list(shape))


class Chain:

    def __init__(self, eng, sem):
        self.eng, self.sem, self.n = eng, sem, 0

    def note(self, ins):
        ins.then_inc(self.sem, 1)
        self.n += 1

    def sync(self):
        self.eng.wait_ge(self.sem, self.n)

    def __call__(self, ins):
        self.note(ins)
        self.sync()


class Linear:

    def __init__(self, k, n, chunk0, group0):
        self.k, self.n, self.chunk0, self.group0 = k, n, chunk0, group0

    def chunk_ends(self, block):
        return block % CHUNK_BLOCKS == CHUNK_BLOCKS - 1 or block == self.k * self.n - 1


class Split:

    HIGH_SLOTS = 3

    def __init__(self, k, ph, start, without=0):
        self.k, self.ph = k, ph
        self.first, self.last = ph.first_chunk, k.next_chunk - without
        self.done = {"high": self.first, "low": self.first}
        self.high, self.end = k.at_parts(start, self.HIGH_SLOTS, CHUNK)

    def chunk_high(self, act, v):
        k, c = self.k, v - self.first
        k.wait_chunk(act, v)
        if c >= self.HIGH_SLOTS:
            old = v - self.HIGH_SLOTS
            act.wait_ge(k.ring_free[old % SLOTS], k.uses_before(old) + 1)
        act.activation(self.high[:, c % self.HIGH_SLOTS, :], k.ring[:, v % SLOTS, :], ACT.Copy
                       ).then_inc(self.ph.sem("chunk_high"), 1)

    def chunk_low(self, dve, v):
        k, c = self.k, v - self.first
        dve.wait_ge(self.ph.sem("chunk_high"), c + 1)
        whole = k.ring[:, v % SLOTS, :]
        dve.tensor_tensor(k.ring_low[v % SLOTS], whole, self.high[:, c % self.HIGH_SLOTS, :].bitcast(F32), ALU.subtract
                          ).then_inc(self.ph.sem("chunk_split"), 1)

    def high_for(self, act, lin, n, ahead=2):
        for v in self.upto("high", lin, n, ahead):
            self.chunk_high(act, v)

    def low_for(self, dve, lin, n, ahead=2):
        for v in self.upto("low", lin, n, ahead):
            self.chunk_low(dve, v)

    def upto(self, part, lin, n, ahead):
        end = min(lin.chunk0 + -(-(n + 1) * lin.k // CHUNK_BLOCKS) + ahead, self.last)
        begin, self.done[part] = self.done[part], max(end, self.done[part])
        return range(begin, end)

    def parts(self, v, block):
        cols = slice(block % CHUNK_BLOCKS * BLK, (block % CHUNK_BLOCKS + 1) * BLK)
        return (self.high[:, (v - self.first) % self.HIGH_SLOTS, cols], self.k.ring_low[v % SLOTS][:, cols])


class Operand:

    def __init__(self, ph, name, whole, high, low):
        self.whole, self.parts = whole, (high, low)
        self.high_ready, self.split_ready = ph.sem(name + "_high"), ph.sem(name + "_split")

    def make_high(self, act):
        act.activation(self.parts[0], self.whole, ACT.Copy).then_inc(self.high_ready, 1)

    def make_low(self, dve):
        dve.wait_ge(self.high_ready, 1)
        dve.tensor_tensor(self.parts[1], self.whole, self.parts[0].bitcast(F32), ALU.subtract).then_inc(self.split_ready, 1)

    def wait(self, pe):
        pe.wait_ge(self.split_ready, 1)
        return self.parts


class Phase:

    def __init__(self, kern, name, stack):
        self.kern, self.name, self.stack, self.sems = kern, name, stack, {}
        self.first_chunk, self.groups = kern.next_chunk, 0

    def sem(self, what):
        if what not in self.sems:
            self.sems[what] = self.kern.nc.alloc_semaphore(name=f"{self.name}_{what}_{self.kern.n_phases}")
        return self.sems[what]

    def linear(self, name, grouped=True):
        k = self.kern
        want, kt, n = k.stream[k.stream_at]
        assert want == name, (want, name)
        lin = Linear(kt, n, k.next_chunk, self.groups)
        k.stream_at += 1
        k.next_chunk += chunks_of(kt, n)
        if grouped:
            self.groups += n
        return lin


class Kernel:
    def __init__(self, nc, dram, stack):
        self.nc, self.dram, self.stack = nc, dram, stack
        self.n_phases = self.n_parts = 0
        self.stream, self.stream_at, self.next_chunk = STREAM_1, 0, 0
        self.layer = None

        def sb(name, shape, dt=F32):
            return stack.enter_context(nc.sbuf_tensor(name, shape, dt))

        def sb_placed(name, shape):
            tile = sb(name, shape)
            return tile, nc.sbuf_base - int(np.prod(shape[1:])) * 4

        self.ring, ring_offset = sb_placed("ring", [P, SLOTS, CHUNK])
        self.x = sb("x", [P, MT, D])
        self.hT, hT_offset = sb_placed("hT", [P, KT, T])
        self.par = sb("par", [P, PAR_W])
        self.gain_row = sb("gain_row", [P, D])
        self.ident = sb("ident", [P, P])
        self.ones = sb("ones", [P, P])
        self.causal = sb("causal", [P, 2 * P])
        self.band = sb("band", [P, 2 * P])
        self.cmp_mask = sb("cmp_mask", [P, MT, N_CMP])
        self.row_valid = sb("row_valid", [P, MT])
        self.upper = sb("upper", [P, P])
        self.upper_add = sb("upper_add", [P, P])
        self.chunk_upper = sb("chunk_upper", [P, P])
        self.rope = sb("rope", [P, 2, MT, 48])
        self.stat = sb("stat", [P, 8, 64])
        self.stage_index = sb("stage_index", [P, 2, GATHER], U32)
        self.arena, self.arena_offset = sb_placed("arena", [P, ARENA])
        self.ring_low = [self.parts(f"ring_low{s}", ring_offset + s * CHUNK * 4, CHUNK)[:] for s in range(SLOTS)]
        self.hT_low = self.parts("hT_low", hT_offset, KT, T)[:]
        self.ps = stack.enter_context(nc.psum_tensor("ps", [P, 8, BLK], F32))
        self.ring_full = [stack.enter_context(nc.semaphore(f"ring_full{s}")) for s in range(SLOTS)]
        self.gathered = [[stack.enter_context(nc.semaphore(f"gathered{b}_{e}")) for e in range(GATHER)] for b in range(2)]
        self.ring_free = [stack.enter_context(nc.semaphore(f"ring_free{s}")) for s in range(SLOTS)]


    def parts(self, name, offset, *shape):
        return self.nc.alloc_sbuf_tensor_at(name, [P, *shape], F32R, offset=offset)

    def at_parts(self, start, *shape):
        self.n_parts += 1
        end = start + int(np.prod(shape))
        assert end <= ARENA, (start, shape)
        return self.parts(f"parts{self.n_parts}", self.arena_offset + 4 * start, *shape)[:], end

    def at(self, start, *shape):
        n = int(np.prod(shape))
        assert start + n <= ARENA, (start, shape)
        view = self.arena[:, start:start + n]
        if len(shape) > 1:
            names = "abcde"[:len(shape)]
            view = view.rearrange(f"p ({' '.join(names)}) -> p {' '.join(names)}",
                                  **{c: s for c, s in zip(names[1:], shape[1:])})
        return view, -(-(start + n) // 8) * 8

    def p1(self, name, n=None):
        a, w = P1[name]
        v = self.par[:, a:a + w]
        return v if n is None else v.rearrange("p (a b) -> p a b", a=n)

    def p2(self, name, n=None):
        a, w = P2[name]
        v = self.par[:, a:a + w]
        return v if n is None else v.rearrange("p (a b) -> p a b", a=n)


    @contextmanager
    def phase(self, name):
        with ExitStack() as stack:
            ph = Phase(self, name, stack)
            yield ph
        self.n_phases += 1

    @contextmanager
    def engines(self, ph):
        nc = self.nc
        with nc.Block(no_gpsimd_drain=True) as block:
            yield block
        for s in ph.sems.values():
            nc.gpsimd.sem_clear(s)
        nc.all_engine_barrier()
        for s in ph.sems.values():
            nc.release_semaphore(s)


    def uses_before(self, v):
        s = v % SLOTS
        if self.layer is not None:
            return self.layer * USES_1[s] + v // SLOTS
        return (DEPTH * USES_1[s] if self.stream is STREAM_2 else 0) + v // SLOTS

    def wait_chunk(self, eng, v):
        uses = self.uses_before(v)
        eng.wait_ge(self.ring_full[v % SLOTS], uses * 16 + 16)

    def load_ahead(self, sp, ph):
        for v in range(ph.first_chunk, self.next_chunk):
            a = v + SLOTS
            s = a % SLOTS
            if self.layer is not None:
                if a < CHUNKS_1:
                    source, uses = self.layer * CHUNKS_1 + a, self.uses_before(a)
                elif a >= VIRTUAL_1:
                    source, uses = (self.layer + 1) * CHUNKS_1 + (a - VIRTUAL_1), (self.layer + 1) * USES_1[s]
                else:
                    continue
            elif a < CHUNKS_2:
                source, uses = DEPTH * CHUNKS_1 + a, self.uses_before(a)
            else:
                continue
            sp.wait_ge(self.ring_free[s], uses)
            sp.dma_start(self.ring[:, s, :], self.dram["stream"][bass.ds(source, 1)].rearrange("a p c -> (a p) c")
                         ).then_inc(self.ring_full[s], 16)
        if self.layer is not None and self.next_chunk == CHUNKS_1:
            for a in range(max(CHUNKS_1 + SLOTS, VIRTUAL_1), VIRTUAL_1 + SLOTS):
                s = a % SLOTS
                sp.wait_ge(self.ring_free[s], (self.layer + 1) * USES_1[s])
                sp.dma_start(self.ring[:, s, :], self.dram["stream"][
                    bass.ds((self.layer + 1) * CHUNKS_1 + (a - VIRTUAL_1), 1)].rearrange("a p c -> (a p) c")
                             ).then_inc(self.ring_full[s], 16)


    def linear_tok(self, pe, ph, lin, xT, widths=None, split=None):
        self._linear(pe, ph, lin, xT, False, widths, split)

    def linear_T(self, pe, ph, lin, xT, split=None):
        self._linear(pe, ph, lin, xT, True, None, split)

    def _linear(self, pe, ph, lin, xT, feature_major, widths, split):
        for n in range(lin.n):
            g = lin.group0 + n
            pair = g % 2
            if g >= 2:
                pe.wait_ge(ph.sem(f"pair_free{pair}"), g // 2)
            for k in range(lin.k):
                block = n * lin.k + k
                v = lin.chunk0 + block // CHUNK_BLOCKS
                if split:
                    if block % CHUNK_BLOCKS == 0:
                        pe.wait_ge(ph.sem("chunk_split"), v - split.first + 1)
                    high, low = split.parts(v, block)
                    passes = [(xT[0], high), (xT[1], high), (xT[0], low)]
                else:
                    if block % CHUNK_BLOCKS == 0:
                        self.wait_chunk(pe, v)
                    passes = [(xT, self.ring[:, v % SLOTS, (block % CHUNK_BLOCKS) * BLK:(block % CHUNK_BLOCKS + 1) * BLK])]
                if feature_major:
                    for f in range(4):
                        for i, (x, w) in enumerate(passes):
                            last = pe.matmul(self.ps[:, 2 * pair + f // 2, (f % 2) * T:(f % 2 + 1) * T],
                                             w[:, f * P:(f + 1) * P], x[:, k, :], start=(k == 0 and i == 0 and f % 2 == 0),
                                             stop=(k == lin.k - 1 and i == len(passes) - 1 and f % 2 == 1),
                                             skip_group_check=True)
                else:
                    width = widths[n] if widths else BLK
                    for m in range(MT):
                        for i, (x, w) in enumerate(passes):
                            last = pe.matmul(self.ps[:, 2 * pair + m, 0:width], x[:, k, m * P:(m + 1) * P], w[:, 0:width],
                                             start=(k == 0 and i == 0), stop=(k == lin.k - 1 and i == len(passes) - 1))
                if lin.chunk_ends(block) and k < lin.k - 1:
                    last.then_inc(self.ring_free[v % SLOTS], 1)
            last.then_inc(ph.sem("pair_done"), 1)

    def take(self, eng, ph, lin, n, release=True):
        g = lin.group0 + n
        eng.wait_ge(ph.sem("pair_done"), g + 1)
        block = n * lin.k + lin.k - 1
        if release and lin.chunk_ends(block):
            eng.sem_inc(self.ring_free[(lin.chunk0 + block // CHUNK_BLOCKS) % SLOTS], 1)
        pair = g % 2
        return self.ps[:, 2 * pair:2 * pair + 2, :], ph.sem(f"pair_free{pair}")


    def transposes(self, pe, ph, name, groups, banks):
        for i, group in enumerate(groups):
            if i >= len(banks):
                pe.wait_ge(ph.sem(f"{name}_copied"), i - len(banks) + 1)
            for src, col in group:
                p, f = src.shape[0], int(np.prod(src.shape[1:]))
                last = pe.transpose(self.ps[0:f, banks[i % len(banks)], col:col + p], src, self.ident[0:p, 0:p])
            last.then_inc(ph.sem(f"{name}_turned"), 1)

    def turned(self, eng, ph, name, i, banks):
        eng.wait_ge(ph.sem(f"{name}_turned"), i + 1)
        return self.ps[:, banks[i % len(banks)], :]


    def rstd_vector_before(self, dve, ph, link, ss, ms, width, tag=""):
        ins = dve.tensor_scalar(ms, ss, 1.0 / width, EPS, ALU.mult, ALU.add)
        ins.then_inc(ph.sem("mean_ready" + tag), 1)

    def rstd_scalar(self, act, ph, link, ms, y, tag="", turn=1):
        act.wait_ge(ph.sem("mean_ready" + tag), turn)
        act.activation(y, ms, ACT.Sqrt).then_inc(ph.sem("rough_ready" + tag), 1)

    def rstd_vector_after(self, dve, ph, link, ms, y, t, tag="", turn=1):
        dve.wait_ge(ph.sem("rough_ready" + tag), turn)
        link(dve.reciprocal(y, y))
        link(dve.tensor_tensor(t, y, y, ALU.mult))
        link(dve.tensor_tensor(t, t, ms, ALU.mult))
        link(dve.tensor_scalar(t, t, -0.5, 1.5, ALU.mult, ALU.add))
        link(dve.tensor_tensor(y, y, t, ALU.mult))


def feature_groups(tile, first, count):
    return [[(tile[:, m, (first + 2 * j + i) * P:(first + 2 * j + i + 1) * P], i * T + m * P)
             for i in range(2) for m in range(MT)] for j in range(count // 2)]


def norm_phase(k, name, src, gain, dst, loads=None, out_tok=None, scratch=0, parts=None):
    with k.phase(name) as ph:
        junk, a = k.at(scratch, D)
        xn, _ = k.at(a, MT, D)
        ss, ms, y, t = (k.stat[:, i, 0:MT] for i in range(4))
        banks = [4, 5, 6, 7]
        jobs = feature_groups(xn, 0, KT) if dst is not None else []
        with k.engines(ph) as block:
            @block.sync
            def _(sp):
                for i, (to, frm) in enumerate(loads or []):
                    sp.dma_start(to, frm).then_inc(ph.sem(f"small_loaded{i}"), 16)
                for i in range(len(loads or [])):
                    sp.wait_ge(ph.sem(f"small_loaded{i}"), 16)

            @block.scalar
            def _(act):
                link = Chain(act, ph.sem("act_chain"))
                act.activation(junk, src[:, 0, :], ACT.Square, accum_out=ss[:, 0:1]).then_inc(ph.sem("squares_summed"), 1)
                k.rstd_scalar(act, ph, link, ms, y)
                if parts is not None:
                    for i in range(len(jobs)):
                        act.wait_ge(ph.sem("gained"), i + 1)
                        tiles = slice(2 * i, 2 * i + 2)
                        act.activation(parts[0][:, tiles, :], dst[:, tiles, :], ACT.Copy).then_inc(ph.sem("high"), 1)

            @block.vector
            def _(dve):
                link = Chain(dve, ph.sem("dve_chain"))
                link(dve.tensor_tensor_reduce(xn[:, 1, :], src[:, 1, :], src[:, 1, :], 1.0, 0.0, ALU.mult, ALU.add, ss[:, 1:2]))
                dve.wait_ge(ph.sem("squares_summed"), 1)
                k.rstd_vector_before(dve, ph, link, ss, ms, D)
                k.rstd_vector_after(dve, ph, link, ms, y, t)
                for m in range(MT):
                    dve.tensor_scalar(xn[:, m, :], src[:, m, :], y[:, m:m + 1], None, ALU.mult
                                      ).then_inc(ph.sem("normed"), 1)
                for i in range(len(loads or [])):
                    dve.wait_ge(ph.sem(f"small_loaded{i}"), 16)

                def low(i):
                    dve.wait_ge(ph.sem("high"), i + 1)
                    tiles = slice(2 * i, 2 * i + 2)
                    dve.tensor_tensor(parts[1][:, tiles, :], dst[:, tiles, :], parts[0][:, tiles, :].bitcast(F32), ALU.subtract)

                for i in range(len(jobs)):
                    bank = k.turned(dve, ph, "h", i, banks)
                    dve.tensor_tensor(dst[:, 2 * i:2 * i + 2, :], bank.rearrange("p (a t) -> p a t", a=2),
                                      bc(gain[:, 2 * i:2 * i + 2].unsqueeze(2), [P, 2, T]), ALU.mult).then_inc(ph.sem("gained"), 1)
                    if parts is not None and i >= 1:
                        low(i - 1)
                if parts is not None:
                    low(len(jobs) - 1)
                if out_tok is not None:
                    dve.wait_ge(ph.sem("normed"), MT)
                    dve.tensor_tensor(out_tok[:], xn, bc(k.gain_row[:].unsqueeze(1), [P, MT, D]), ALU.mult)

            @block.tensor
            def _(pe):
                if jobs:
                    pe.wait_ge(ph.sem("normed"), MT)
                    k.transposes(pe, ph, "h", jobs, banks)


def constants_phase(k):
    with k.phase("constants") as ph:
        pos, a = k.at(0, MT)
        posi, a = k.at(a, MT)
        freq, a = k.at(a, 48)
        ang, a = k.at(a, MT, 48)
        turns, a = k.at(a, MT, 48)
        turnsi, a = k.at(a, MT, 48)
        red, a = k.at(a, MT, 48)
        posi, turnsi = posi.bitcast(I32), turnsi.bitcast(I32)
        two_pi = [float(np.float32(6.28125)), float(np.float32(2 * np.pi - 6.28125))]
        two_pi.append(float(2 * np.pi - two_pi[0] - two_pi[1]))
        with k.engines(ph) as block:
            @block.sync
            def _(sp):
                sp.dma_start(posi, k.dram["positions"]).then_inc(ph.sem("positions_loaded"), 16)
                sp.dma_start(freq, k.dram["freq"]).then_inc(ph.sem("freq_loaded"), 16)
                sp.dma_start(k.x[:], k.dram["x"]).then_inc(ph.sem("x_loaded"), 16)
                for s in range(SLOTS):
                    sp.dma_start(k.ring[:, s, :], k.dram["stream"][s]).then_inc(k.ring_full[s], 16)
                sp.wait_ge(ph.sem("x_loaded"), 16)

            @block.gpsimd
            def _(pool):
                link = Chain(pool, ph.sem("pool_chain"))
                for tile, value in ((k.ident, 0.0), (k.ones, 1.0), (k.causal, 0.0), (k.band, 0.0),
                                    (k.cmp_mask, 0.0), (k.row_valid, 1.0), (k.upper, 1.0),
                                    (k.upper_add, 0.0), (k.chunk_upper, 1.0)):
                    link.note(pool.memset(tile[:], value))
                link.sync()

                def select(tile, op, fill, base, pattern, channel):
                    link(pool.affine_select(out=tile, in_=tile, compare_op=op, fill=fill, base=base,
                                            pattern=pattern, channel_multiplier=channel))

                select(k.ident[:], ALU.not_equal, 1.0, 0, [[-1, P]], 1)
                select(k.causal[:], ALU.is_ge, NEG, P, [[-1, 2 * P]], 1)
                select(k.band[:], ALU.is_ge, NEG, P, [[-1, 2 * P]], 1)
                select(k.band[:], ALU.is_gt, NEG, 0, [[1, 2 * P]], -1)
                select(k.cmp_mask[:], ALU.is_ge, NEG, -31, [[P, MT], [-16, N_CMP]], 1)
                select(k.row_valid[:], ALU.is_ge, 0.0, -31, [[P, MT]], 1)
                select(k.upper[:], ALU.is_ge, 0.0, 0, [[1, P]], -1)
                select(k.upper_add[:], ALU.is_ge, NEG, 0, [[1, P]], -1)
                select(k.chunk_upper[:], ALU.is_ge, 0.0, 0, [[1, P]], -1)
                select(k.chunk_upper[:, HD:P], ALU.is_ge, 0.0, -HD, [[0, HD]], 1)

            @block.vector
            def _(dve):
                link = Chain(dve, ph.sem("dve_chain"))
                dve.wait_ge(ph.sem("positions_loaded"), 16)
                dve.wait_ge(ph.sem("freq_loaded"), 16)
                link(dve.tensor_copy(pos, posi))
                link(dve.tensor_tensor(ang, bc(pos.unsqueeze(2), [P, MT, 48]), bc(freq.unsqueeze(1), [P, MT, 48]), ALU.mult))
                link(dve.tensor_scalar(turns, ang, float(1 / (2 * np.pi)), None, ALU.mult))
                link(dve.tensor_copy(turnsi, turns))
                link(dve.tensor_copy(turns, turnsi))
                for part in two_pi:
                    link(dve.scalar_tensor_tensor(out=ang, in0=turns, scalar=-part, in1=ang, op0=ALU.mult, op1=ALU.add))
                for sign, op in ((-1.0, ALU.is_gt), (1.0, ALU.is_lt)):
                    link(dve.tensor_scalar(red, ang, float(-sign * np.pi), float(sign * 2 * np.pi), op, ALU.mult))
                    link(dve.tensor_tensor(ang, ang, red, ALU.add))
                pi = float(np.nextafter(np.float32(np.pi), np.float32(0)))
                link(dve.tensor_scalar(ang, ang, pi, -pi, ALU.min, ALU.max))
                link(dve.tensor_scalar(red, ang, -1.0, None, ALU.mult))
                link(dve.tensor_tensor(red, red, ang, ALU.max))
                link(dve.tensor_scalar(red, red, -1.0, float(np.pi / 2), ALU.mult, ALU.add))
                dve.sem_inc(ph.sem("angles_ready"), 1)

            @block.scalar
            def _(act):
                act.wait_ge(ph.sem("angles_ready"), 1)
                act.activation(k.rope[:, 0], red, ACT.Sin)
                act.activation(k.rope[:, 1], ang, ACT.Sin)


def rotate(dve, link, x, out, cos, sin, t1, t2):
    _, mt, heads, width = x.shape
    half = width // 2
    shape = [P, mt, heads, half]
    c, s = bc(cos.unsqueeze(2), shape), bc(sin.unsqueeze(2), shape)
    x1, x2 = x[:, :, :, 0:half], x[:, :, :, half:width]
    link.note(dve.tensor_tensor(t1, x1, s, ALU.mult))
    link.note(dve.tensor_tensor(t2, x2, s, ALU.mult))
    link.note(dve.tensor_tensor(out[:, :, :, 0:half], x1, c, ALU.mult))
    link(dve.tensor_tensor(out[:, :, :, half:width], x2, c, ALU.mult))
    link.note(dve.tensor_tensor(out[:, :, :, 0:half], out[:, :, :, 0:half], t2, ALU.subtract))
    return dve.tensor_tensor(out[:, :, :, half:width], out[:, :, :, half:width], t1, ALU.add)


class Tiles1:

    def __init__(self, k):
        a = 0
        self.gT, a = k.at(a, 24, T)
        self.qaT, a = k.at(a, 4, T)
        self.qbT, a = k.at(a, 4, T)
        self.keysT, a = k.at(a, 3, T)
        self.kvcT, a = k.at(a, 2, T)
        self.values, a = k.at(a, MT, 8, HD)
        self.cqkv, a = k.at(a, MT, 2, T)
        self.small, a = k.at(a, MT, 56)
        self.sgate, a = k.at(a, MT, 24)
        self.x_high, b = k.at_parts(a, KT, T)
        self.x_low, b = k.at_parts(b, KT, T)
        self.kcmpT, a = k.at(a, N_CMP)
        self.vcmp, a = k.at(a, 2, HD)
        self.vC, a = k.at(a, MT, 8, HD)
        self.oT_low, _ = k.at_parts(a, 3, 4, T)
        self.oT, a = k.at(a, 3, 4, T)
        shared = a
        assert b <= shared
        self.rot, a = k.at(shared, MT, 3, 8, HD)
        self.kvc, a = k.at(a, MT, 2, P)
        self.t1, a = k.at(a, MT, 8, 32)
        self.t2, a = k.at(a, MT, 8, 32)
        self.project_end = a
        self.qcT, a = k.at(shared, 8, T)
        self.kcT, a = k.at(a, 8, T)
        latent = a
        self.qC, a = k.at(latent, MT, 8, 96)
        self.kC, a = k.at(a, MT, 8, 96)
        self.cT, a = k.at(a, 4, T)
        self.cn, a = k.at(a, MT, 2, T)
        self.t3, a = k.at(a, MT, 8, 16)
        self.t4, a = k.at(a, MT, 8, 16)
        self.kpr, a = k.at(a, MT, 32)
        self.win, a = k.at(a, 32, 4 * N_CMP)
        self.hid, a = k.at(a, T)
        self.hid2, a = k.at(a, T)
        self.hidT, a = k.at(a, 2, 4, N_CMP)
        self.probs, a = k.at(latent, 3, 4, T)
        self.probsT, a = k.at(a, 2, 2, 4, P)
        self.sum, a = k.at(a, 32, 4)
        self.nmax, a = k.at(a, 32, 4)
        self.merged_low, _ = k.at_parts(shared, KT, T)
        self.mergedT, a = k.at(shared, KT, T)
        self.tmp, a = k.at(a, 4, T)
        self.branch_end = a
        self.merged_high, _ = k.at_parts(0, KT, T)
        self.heads_high, b = k.at_parts(24 * T, 3, 4, T)
        assert b <= shared - 3 * 4 * T


def project_phase(k, z):
    with k.phase("project") as ph:
        lins = [ph.linear(n) for n in ("rot0", "rot1", "rot2", "values", "latents")]
        gates = ph.linear("gates")
        cos, sin = k.rope[:, 0, :, 0:32], k.rope[:, 1, :, 0:32]
        w_small = k.p1("w_small", KT)
        small_ps = k.ps[:, 4:6, 0:56]
        parts = (z.x_high, z.x_low)
        split = Split(k, ph, z.project_end)
        with k.engines(ph) as block:
            @block.sync
            def _(sp):
                k.load_ahead(sp, ph)

            @block.tensor
            def _(pe):
                for lin in lins:
                    k.linear_tok(pe, ph, lin, parts, split=split)
                for kt in range(KT):
                    for m in range(MT):
                        last = pe.matmul(small_ps[:, m, :], k.hT[:, kt, m * P:(m + 1) * P], w_small[:, kt, :],
                                         start=(kt == 0), stop=(kt == KT - 1))
                last.then_inc(ph.sem("small_done"), 1)
                k.linear_T(pe, ph, gates, parts, split)
                pe.wait_ge(ph.sem("rotated"), 3)
                rot = z.rot
                jobs = [[(rot[:, m, j, 2 * (first + i):2 * (first + i) + 2, :].rearrange("p a b -> p (a b)"), i * T + m * P)
                         for i in range(2) for m in range(MT)] for j, first in ((0, 0), (0, 2), (1, 0), (2, 0), (2, 2))]
                jobs.append([(rot[:, m, 1, 4:6, :].rearrange("p a b -> p (a b)"), m * P) for m in range(MT)])
                jobs.append([(z.kvc[:, m, g, :], g * T + m * P) for g in range(2) for m in range(MT)])
                k.transposes(pe, ph, "heads", jobs, [6, 7])

            @block.vector
            def _(dve):
                link = Chain(dve, ph.sem("dve_chain"))
                for j in range(3):
                    split.low_for(dve, lins[j], 0)
                    pair, free = k.take(dve, ph, lins[j], 0)
                    x = pair.rearrange("p m (h d) -> p m h d", h=8)
                    if j == 1:
                        rotate(dve, link, x[:, :, 0:6, :], z.rot[:, :, 1, 0:6, :], cos, sin, z.t1[:, :, 0:6], z.t2[:, :, 0:6]
                               ).then_inc(ph.sem("keys_rotated"), 1)
                        dve.wait_ge(ph.sem("keys_rotated"), 1)
                        last = rotate(dve, link, x[:, :, 6:8, :], z.kvc[:, :, :, 0:HD], cos, sin,
                                      z.t1[:, :, 6:8], z.t2[:, :, 6:8])
                    else:
                        last = rotate(dve, link, x, z.rot[:, :, j], cos, sin, z.t1, z.t2)
                    last.then_inc(free, 1)
                    dve.wait_ge(free, (lins[j].group0 + 2) // 2)
                    dve.sem_inc(ph.sem("rotated"), 1)
                split.low_for(dve, gates, gates.n - 1)
                dve.wait_ge(ph.sem("small_gates"), 1)
                for m in range(MT):
                    link(dve.tensor_scalar(z.sgate[:, m, 0:8], z.sgate[:, m, 0:8], k.row_valid[:, m:m + 1], None, ALU.mult))
                for i in range(7):
                    bank = k.turned(dve, ph, "heads", i, [6, 7])
                    dst = [z.qaT[:, 0:2], z.qaT[:, 2:4], z.keysT[:, 0:2], z.qbT[:, 0:2], z.qbT[:, 2:4],
                           z.keysT[:, 2:3], z.kvcT][i]
                    n = T if i == 5 else 2 * T
                    dve.tensor_copy(dst.rearrange("p a t -> p (a t)"), bank[:, 0:n]
                                    ).then_inc(ph.sem("heads_copied"), 1)

            @block.scalar
            def _(act):
                link = Chain(act, ph.sem("act_chain"))
                split.high_for(act, lins[3], 0)
                pair, free = k.take(act, ph, lins[3], 0)
                values = pair.rearrange("p m (h d) -> p m h d", h=8)
                link(act.activation(z.kvc[:, :, :, HD:P], values[:, :, 0:2, :], ACT.Copy))
                link(act.activation(z.values, values, ACT.Copy))
                act.sem_inc(free, 1)
                split.high_for(act, lins[4], 0)
                pair, free = k.take(act, ph, lins[4], 0)
                act.activation(z.cqkv, pair.rearrange("p m (a b) -> p m a b", a=2), ACT.Copy).then_inc(free, 1)
                act.wait_ge(ph.sem("small_done"), 1)
                link(act.activation(z.small, small_ps, ACT.Copy))
                link(act.activation(z.sgate, z.small[:, :, 32:56], ACT.Sigmoid))
                act.sem_inc(ph.sem("small_gates"), 1)
                for n in range(gates.n):
                    split.high_for(act, gates, n)
                    pair, free = k.take(act, ph, gates, n)
                    act.activation(z.gT[:, 4 * n:4 * n + 4, :].rearrange("p a t -> p (a t)"),
                                   pair.rearrange("p a b -> p (a b)"), ACT.Sigmoid).then_inc(free, 1)


def latent_phase(k, z):
    with k.phase("latent") as ph:
        w1, qup, kvup = ph.linear("cmp_w1", grouped=False), ph.linear("q_up"), ph.linear("kv_up")
        cos, sin = k.rope[:, 0, :, 32:48], k.rope[:, 1, :, 32:48]
        ss, ms, y, t = (k.stat[:, i, 0:4] for i in range(4))
        ss2, ms2, y2, t2 = (k.stat[:, i, 0:4].rearrange("p (a b) -> p a b", a=MT) for i in range(4))
        pos = k.p1("posT")
        w2k, w2v = k.p1("w2k", 2), k.p1("w2v", 2)
        n4 = 4 * N_CMP
        hid, hid2 = z.hid[0:n4], z.hid2[0:n4]
        with k.engines(ph) as block:
            @block.sync
            def _(sp):
                k.load_ahead(sp, ph)

            @block.gpsimd
            def _(pool):
                pool.memset(z.win[0:HD, :, 2 * N_CMP:n4], 0.0).then_inc(ph.sem("windows_padded"), 1)
                pool.memset(z.win[HD:P, :, 0:2 * N_CMP], 0.0).then_inc(ph.sem("windows_padded"), 1)

            @block.scalar
            def _(act):
                link = Chain(act, ph.sem("act_chain"))
                for m in range(MT):
                    for j in range(2):
                        link(act.activation(z.cn[:, m, j], z.cqkv[:, m, j], ACT.Square,
                                            accum_out=ss[:, 2 * m + j:2 * m + j + 1]))
                act.sem_inc(ph.sem("squares_summed"), 1)
                k.rstd_scalar(act, ph, link, ms, y)
                act.wait_ge(ph.sem("cubes_ready"), 1)
                act.activation(hid2, hid2, ACT.Sigmoid, scale=1.5957691216057308).then_inc(ph.sem("hidden_sigmoid"), 1)
                pair, free = k.take(act, ph, qup, 0)
                q = z.qC.rearrange("p m h d -> p m (h d)")
                act.activation(q[:, :, 0:BLK], pair, ACT.Copy).then_inc(free, 1)
                pair, free = k.take(act, ph, qup, 1)
                act.activation(q[:, :, BLK:768], pair[:, :, 0:256], ACT.Copy).then_inc(free, 1)
                act.wait_ge(free, qup.group0 // 2 + 1)
                act.wait_ge(ph.sem("pair_free0"), qup.group0 // 2 + 1)
                act.sem_inc(ph.sem("queries_up"), 1)
                for n in range(2):
                    pair, free = k.take(act, ph, kvup, n)
                    x = pair.rearrange("p m (h d) -> p m h d", h=4)
                    for m in range(MT):
                        link(act.activation(z.kC[:, m, 4 * n:4 * n + 4, 0:HD], x[:, m, :, 0:HD], ACT.Copy))
                        link(act.activation(z.vC[:, m, 4 * n:4 * n + 4, :], x[:, m, :, HD:P], ACT.Copy))
                    act.sem_inc(free, 1)
                act.sem_inc(ph.sem("keys_up"), 1)

            @block.vector
            def _(dve):
                link = Chain(dve, ph.sem("dve_chain"))
                for g in range(2):
                    steps = z.kvcT[:, g, :].rearrange("p (n s) -> p s n", s=16)
                    for a in range(2):
                        for kv in range(2):
                            rows, at = slice(HD * kv, HD * kv + HD), (2 * kv + g) * N_CMP
                            link.note(dve.tensor_tensor(z.win[rows, 16 * a:16 * a + 16, at:at + N_CMP], steps[rows, :, a:a + N_CMP],
                                                        bc(pos[rows, 16 * a:16 * a + 16].unsqueeze(2), [HD, 16, N_CMP]), ALU.add))
                link.sync()
                dve.sem_inc(ph.sem("windows_ready"), 1)
                dve.wait_ge(ph.sem("squares_summed"), 1)
                k.rstd_vector_before(dve, ph, link, ss, ms, T)
                k.rstd_vector_after(dve, ph, link, ms, y, t)
                dve.tensor_tensor(z.cn, z.cqkv, bc(y2.unsqueeze(3), [P, MT, 2, T]), ALU.mult).then_inc(ph.sem("latents_normed"), 1)
                for i in range(2):
                    bank = k.turned(dve, ph, "latents", i, [4, 5])
                    gain = k.p1(("cq_norm", "ckv_norm")[i])
                    dve.tensor_tensor(z.cT[:, 2 * i:2 * i + 2, :], bank.rearrange("p (a t) -> p a t", a=2),
                                      bc(gain.unsqueeze(2), [P, 2, T]), ALU.mult).then_inc(ph.sem("latents_turned_gained"), 1)
                dve.wait_ge(ph.sem("hidden_done"), 1)
                link(dve.tensor_copy(hid, k.ps[0:n4, 6, 0:T]))
                link(dve.tensor_tensor(hid2, hid, hid, ALU.mult))
                link(dve.tensor_scalar(hid2, hid2, 0.044715, 1.0, ALU.mult, ALU.add))
                dve.tensor_tensor(hid2, hid2, hid, ALU.mult).then_inc(ph.sem("cubes_ready"), 1)
                dve.wait_ge(ph.sem("hidden_sigmoid"), 1)
                dve.tensor_tensor(hid, hid, hid2, ALU.mult).then_inc(ph.sem("hidden_gelu"), 1)
                dve.wait_ge(ph.sem("hidden_turned"), 1)
                dve.tensor_copy(z.hidT.rearrange("p j a n -> p (j a n)"), k.ps[:, 7, 0:2 * n4]).then_inc(ph.sem("hidden_ready"), 1)
                kpe = z.small[:, :, 0:32].unsqueeze(2)
                rotate(dve, link, kpe, z.kpr.unsqueeze(2), cos, sin, z.t3[:, :, 0:1], z.t4[:, :, 0:1]).then_inc(ph.sem("kpe_rotated"), 1)
                dve.wait_ge(ph.sem("kpe_rotated"), 1)
                link(dve.tensor_copy(z.kC[:, :, :, HD:96], bc(z.kpr.unsqueeze(2), [P, MT, 8, 32])))
                dve.wait_ge(ph.sem("queries_up"), 1)
                x1, x2 = z.qC[:, :, :, HD:HD + 16], z.qC[:, :, :, HD + 16:96]
                shape = [P, MT, 8, 16]
                c, s = bc(cos.unsqueeze(2), shape), bc(sin.unsqueeze(2), shape)
                link.note(dve.tensor_tensor(z.t3, x1, s, ALU.mult))
                link(dve.tensor_tensor(z.t4, x2, s, ALU.mult))
                link.note(dve.tensor_tensor(x1, x1, c, ALU.mult))
                link(dve.tensor_tensor(x2, x2, c, ALU.mult))
                link.note(dve.tensor_tensor(x1, x1, z.t4, ALU.subtract))
                link(dve.tensor_tensor(x2, x2, z.t3, ALU.add))
                dve.sem_inc(ph.sem("queries_rotated"), 1)
                dve.wait_ge(ph.sem("compressed_done"), 1)
                link(dve.tensor_copy(z.kcmpT, k.ps[:, 4, 0:N_CMP]))
                link(dve.tensor_copy(z.vcmp[0:N_CMP], k.ps[0:N_CMP, 5, 0:P].rearrange("p (a b) -> p a b", a=2)))
                dve.sem_inc(ph.sem("compressed_copied"), 1)
                for i in range(8):
                    bank = k.turned(dve, ph, "c", i, [4, 5])
                    dst = (z.qcT if i < 4 else z.kcT)[0:96, 2 * (i % 4):2 * (i % 4) + 2, :]
                    dve.tensor_copy(dst.rearrange("p a t -> p (a t)"), bank[0:96, :]).then_inc(ph.sem("c_copied"), 1)

            @block.tensor
            def _(pe):
                pe.wait_ge(ph.sem("windows_ready"), 1)
                pe.wait_ge(ph.sem("windows_padded"), 2)
                for step in range(32):
                    v = w1.chunk0 + step // 8
                    if step % 8 == 0:
                        k.wait_chunk(pe, v)
                    last = pe.matmul(k.ps[0:n4, 6, 0:T], z.win[:, step, :], k.ring[:, v % SLOTS, (step % 8) * T:(step % 8 + 1) * T],
                                     start=(step == 0), stop=(step == 31))
                    if step % 8 == 7 and step < 31:
                        last.then_inc(k.ring_free[v % SLOTS], 1)
                last.then_inc(ph.sem("hidden_done"), 1)
                pe.wait_ge(ph.sem("latents_normed"), 1)
                jobs = [[(z.cn[:, m, j, i * P:(i + 1) * P], i * T + m * P) for i in range(2) for m in range(MT)] for j in range(2)]
                k.transposes(pe, ph, "latents", jobs, [4, 5])
                pe.wait_ge(ph.sem("latents_turned_gained"), 2)
                k.linear_tok(pe, ph, qup, z.cT[:, 0:2], [BLK, 256])
                pe.wait_ge(ph.sem("hidden_gelu"), 1)
                pe.sem_inc(k.ring_free[(w1.chunk0 + 3) % SLOTS], 1)
                for j in range(2):
                    last = pe.transpose(k.ps[:, 7, j * n4:(j + 1) * n4], hid[:, j * P:(j + 1) * P], k.ident[0:n4, 0:n4])
                last.then_inc(ph.sem("hidden_turned"), 1)
                k.linear_tok(pe, ph, kvup, z.cT[:, 2:4])
                pe.wait_ge(ph.sem("hidden_ready"), 1)
                for g in range(2):
                    for j in range(2):
                        pe.matmul(k.ps[HD * g:HD * g + HD, 4, 0:N_CMP], w2k[:, j, :], z.hidT[:, j, g, :],
                                  start=(j == 0), stop=(j == 1))
                for g in range(2):
                    for j in range(2):
                        last = pe.matmul(k.ps[0:N_CMP, 5, g * HD:(g + 1) * HD], z.hidT[:, j, 2 + g, :],
                                         w2v[:, j, :], start=(j == 0), stop=(j == 1))
                last.then_inc(ph.sem("compressed_done"), 1)
                pe.wait_ge(ph.sem("queries_rotated"), 1)
                pe.wait_ge(ph.sem("keys_up"), 1)
                jobs = [[(src[:, m, 2 * j + i, :], i * T + m * P) for i in range(2) for m in range(MT)]
                        for src in (z.qC, z.kC) for j in range(4)]
                pe.wait_ge(ph.sem("compressed_copied"), 1)
                k.transposes(pe, ph, "c", jobs, [4, 5])


class Batch:

    def __init__(self, q, key, value, n_keys, scale, out, mask=None, coef=None, sink=None, add=False,
                 contract=1, pieces=1):
        self.q, self.key, self.value, self.n_keys, self.scale, self.out = q, key, value, n_keys, scale, out
        self.mask, self.coef, self.sink, self.add = mask, coef, sink, add
        self.contract, self.pieces = contract, pieces
        self.key_tiles = [(i, min(P, n_keys - i)) for i in range(0, n_keys, P)]


def attention_phase(k, name, batches, probs, probsT, sums, nmax, out_banks):
    nb = len(batches)
    with k.phase(name) as ph:
        def scores_ps(b):
            return k.ps[:, 2 * (b % 2):2 * (b % 2) + 2, :].rearrange("p a (h n) -> p (a h) n", h=2)

        def out_ps(b):
            return out_banks[b % len(out_banks)]

        with k.engines(ph) as block:
            @block.tensor
            def _(pe):
                def scores(b):
                    bt = batches[b]
                    if b >= 2:
                        pe.wait_ge(ph.sem("scores_masked"), b - 1)
                    for h in range(4):
                        for c in range(bt.contract):
                            last = pe.matmul(scores_ps(b)[:, h, 0:bt.n_keys], bt.q(h, c), bt.key(h, c),
                                             start=(c == 0), stop=(c == bt.contract - 1))
                    last.then_inc(ph.sem("scores_ready"), 1)

                def turn(b):
                    bt = batches[b]
                    pe.wait_ge(ph.sem("probs_scaled"), b + 1)
                    if b >= 1:
                        pe.wait_ge(ph.sem("probs_turned_copied"), b)
                    for i, (k0, n) in enumerate(bt.key_tiles):
                        for h in range(4):
                            last = pe.transpose(k.ps[0:n, 4 + i, h * P:(h + 1) * P], probs[:, b % 3, h, k0:k0 + n], k.ident[:])
                    last.then_inc(ph.sem("probs_turned"), 1)

                def values(b):
                    bt = batches[b]
                    pe.wait_ge(ph.sem("probs_turned_copied"), b + 1)
                    if b >= len(out_banks):
                        pe.wait_ge(ph.sem("out_copied"), b - len(out_banks) + 1)
                    for h in range(4):
                        for j in range(bt.pieces):
                            for i, (k0, n) in enumerate(bt.key_tiles):
                                v = bt.value(h, i, j)
                                first = v.shape[1]
                                base = bt.out.start_partition() if bt.pieces == 1 else 0
                                last = pe.matmul(out_ps(b)[base:base + first, (h * bt.pieces + j) // 4,
                                                           ((h * bt.pieces + j) % 4) * P:((h * bt.pieces + j) % 4 + 1) * P],
                                                 v, probsT[0:n, b % 2, i, h, :], start=(i == 0), stop=(i == len(bt.key_tiles) - 1))
                    last.then_inc(ph.sem("out_ready"), 1)

                scores(0)
                scores(1)
                for b in range(nb):
                    if b + 2 < nb:
                        scores(b + 2)
                    if b >= 1:
                        values(b - 1)
                    turn(b)
                values(nb - 1)

            @block.vector
            def _(dve):
                link = Chain(dve, ph.sem("dve_chain"))

                def mask(b):
                    bt = batches[b]
                    dve.wait_ge(ph.sem("scores_ready"), b + 1)
                    if b >= 3:
                        dve.wait_ge(ph.sem("probs_turned"), b - 2)
                    s, p = scores_ps(b)[:, :, 0:bt.n_keys], probs[:, b % 3, :, 0:bt.n_keys]
                    if bt.mask is not None:
                        ins = dve.scalar_tensor_tensor(out=p, in0=s, scalar=bt.scale, in1=bc(bt.mask.unsqueeze(1), [P, 4, bt.n_keys]),
                                                       op0=ALU.mult, op1=ALU.add)
                    else:
                        ins = dve.tensor_scalar(p, s, bt.scale, None, ALU.mult)
                    ins.then_inc(ph.sem("scores_masked"), 1)
                    dve.wait_ge(ph.sem("scores_masked"), b + 1)
                    link(dve.tensor_reduce(nmax[:, b, :], p, AX, ALU.max))
                    if bt.sink is not None:
                        link(dve.tensor_tensor(nmax[:, b, :], nmax[:, b, :], bt.sink, ALU.max))
                    negated = dve.tensor_scalar(nmax[:, b, :], nmax[:, b, :], -1.0, None, ALU.mult)
                    if bt.sink is None:
                        negated.then_inc(ph.sem("max_ready"), 1)
                    else:
                        link(negated)
                        dve.tensor_tensor(k.stat[:, 7, 4 * (b % 16):4 * (b % 16) + 4], nmax[:, b, :], bt.sink, ALU.add
                                          ).then_inc(ph.sem("max_ready"), 1)

                def scale(b):
                    bt = batches[b]
                    dve.wait_ge(ph.sem("probs_exp"), b + 1)
                    s = sums[:, b, :]
                    if bt.sink is not None:
                        link(dve.tensor_tensor(s, s, nmax[:, b, :], ALU.add))
                    link(dve.reciprocal(s, s))
                    if bt.coef is not None:
                        link(dve.tensor_tensor(s, s, bt.coef, ALU.mult))
                    p = probs[:, b % 3, :, 0:bt.n_keys]
                    dve.tensor_tensor(p, p, bc(s.unsqueeze(2), [P, 4, bt.n_keys]), ALU.mult).then_inc(ph.sem("probs_scaled"), 1)

                def out(b):
                    bt = batches[b]
                    dve.wait_ge(ph.sem("out_ready"), b + 1)
                    base = bt.out.start_partition()
                    rows = bt.out.shape[0]
                    o = out_ps(b)[base:base + rows].rearrange("p a (h n) -> p (a h) n", h=4)
                    if bt.add:
                        dve.wait_ge(ph.sem("out_copied"), b)
                        ins = dve.tensor_tensor(bt.out, o, bt.out, ALU.add)
                    else:
                        ins = dve.tensor_copy(bt.out, o)
                    ins.then_inc(ph.sem("out_copied"), 1)

                mask(0)
                mask(1)
                for b in range(nb):
                    scale(b)
                    if b + 2 < nb:
                        mask(b + 2)
                    if b >= 2:
                        out(b - 2)
                for b in range(max(0, nb - 2), nb):
                    out(b)

            @block.scalar
            def _(act):
                link = Chain(act, ph.sem("act_chain"))

                def exps(b):
                    bt = batches[b]
                    act.wait_ge(ph.sem("max_ready"), b + 1)
                    for h in range(4):
                        p = probs[:, b % 3, h, 0:bt.n_keys]
                        link.note(act.activation(p, p, ACT.Exp, bias=nmax[:, b, h:h + 1], accum_out=sums[:, b, h:h + 1]))
                    link.sync()
                    if bt.sink is not None:
                        link(act.activation(nmax[:, b, :], k.stat[:, 7, 4 * (b % 16):4 * (b % 16) + 4], ACT.Exp))
                    act.sem_inc(ph.sem("probs_exp"), 1)

                def copy(b):
                    bt = batches[b]
                    act.wait_ge(ph.sem("probs_turned"), b + 1)
                    if b >= 2:
                        act.wait_ge(ph.sem("out_ready"), b - 1)
                    n = bt.key_tiles[-1][1]
                    tiles = len(bt.key_tiles)
                    act.activation(probsT[0:n, b % 2, 0:tiles].rearrange("p a h q -> p a (h q)"), k.ps[0:n, 4:4 + tiles, :],
                                   ACT.Copy).then_inc(ph.sem("probs_turned_copied"), 1)

                exps(0)
                exps(1)
                for b in range(nb):
                    copy(b)
                    if b + 2 < nb:
                        exps(b + 2)


def branches_phase(k, z):
    with k.phase("branches") as ph:
        lins = [ph.linear(f"branch_{c}") for c in "abc"]
        w_out = ph.linear("w_out")
        heads = Operand(ph, "heads", z.oT, z.heads_high, z.oT_low)
        merged = Operand(ph, "merged", z.mergedT, z.merged_high, z.merged_low)
        split = Split(k, ph, z.branch_end)
        with k.engines(ph) as block:
            @block.sync
            def _(sp):
                k.load_ahead(sp, ph)

            @block.tensor
            def _(pe):
                parts = heads.wait(pe)
                for i, lin in enumerate(lins):
                    k.linear_T(pe, ph, lin, [part[:, i] for part in parts], split)
                k.linear_tok(pe, ph, w_out, merged.wait(pe), split=split)

            @block.scalar
            def _(act):
                heads.make_high(act)
                split.high_for(act, lins[2], 1)
                act.wait_ge(ph.sem("merged_ready"), 1)
                merged.make_high(act)
                split.high_for(act, w_out, 1)

            @block.vector
            def _(dve):
                link = Chain(dve, ph.sem("dve_chain"))
                heads.make_low(dve)
                for i, lin in enumerate(lins):
                    for n in range(2):
                        split.low_for(dve, lin, n)
                        pair, free = k.take(dve, ph, lin, n)
                        x = pair.rearrange("p a (b t) -> p (a b) t", b=2)
                        gate = z.gT[:, KT * i + 4 * n:KT * i + 4 * n + 4, :]
                        part = z.mergedT[:, 4 * n:4 * n + 4, :]
                        to = part if i == 0 else z.tmp
                        dve.tensor_tensor(to, x, gate, ALU.mult).then_inc(free, 1)
                        dve.wait_ge(free, (lin.group0 + n + 2) // 2)
                        if i > 0:
                            link(dve.tensor_tensor(part, part, z.tmp, ALU.add))
                dve.sem_inc(ph.sem("merged_ready"), 1)
                merged.make_low(dve)
                add_to_x(k, dve, ph, w_out, split)


def add_to_x(k, dve, ph, lin, split):
    for n in range(lin.n):
        split.low_for(dve, lin, n)
        pair, free = k.take(dve, ph, lin, n)
        x = k.x[:, :, n * BLK:(n + 1) * BLK]
        dve.tensor_tensor(x, pair, x, ALU.add).then_inc(free, 1)


def ffn_phase(k, h_parts):
    with k.phase("ffn") as ph:
        lin, down = ph.linear("ffn_in"), ph.linear("ffn_down")
        hidden_high, a = k.at_parts(KT * T, FF_T, T)
        hidden_low, a = k.at_parts(a, FF_T, T)
        whole, a = k.at(a, 2, 2, T)
        sig, a = k.at(a, 2, 2, T)
        split = Split(k, ph, a)
        with k.engines(ph) as block:
            @block.sync
            def _(sp):
                k.load_ahead(sp, ph)

            @block.tensor
            def _(pe):
                k.linear_T(pe, ph, lin, h_parts, split)
                pe.wait_ge(ph.sem("hidden_low"), lin.n)
                k.linear_tok(pe, ph, down, (hidden_high, hidden_low), split=split)

            @block.scalar
            def _(act):
                def round_hidden(n):
                    act.wait_ge(ph.sem("hidden_ready"), n + 1)
                    act.activation(hidden_high[:, 2 * n:2 * n + 2, :], whole[:, n % 2], ACT.Copy).then_inc(ph.sem("hidden_high"), 1)

                for n in range(lin.n):
                    split.high_for(act, lin, n)
                    if n >= 1:
                        round_hidden(n - 1)
                    pair, _ = k.take(act, ph, lin, n)
                    if n >= 2:
                        act.wait_ge(ph.sem("hidden_ready"), n - 1)
                    act.activation(sig[:, n % 2].rearrange("p a t -> p (a t)"), pair[:, 0, :], ACT.Silu
                                   ).then_inc(ph.sem("gate_done"), 1)
                round_hidden(lin.n - 1)
                split.high_for(act, down, 1)

            @block.vector
            def _(dve):
                def low_of_hidden(n):
                    dve.wait_ge(ph.sem("hidden_high"), n + 1)
                    high = hidden_high[:, 2 * n:2 * n + 2, :]
                    dve.tensor_tensor(hidden_low[:, 2 * n:2 * n + 2, :], whole[:, n % 2], high.bitcast(F32), ALU.subtract
                                      ).then_inc(ph.sem("hidden_low"), 1)

                for n in range(lin.n):
                    split.low_for(dve, lin, n)
                    if n >= 1:
                        low_of_hidden(n - 1)
                    pair, free = k.take(dve, ph, lin, n, release=False)
                    up = pair[:, 1, :].rearrange("p (a t) -> p a t", a=2)
                    dve.wait_ge(ph.sem("gate_done"), n + 1)
                    if n >= 2:
                        dve.wait_ge(ph.sem("hidden_low"), n - 1)
                    dve.tensor_tensor(whole[:, n % 2], up, sig[:, n % 2], ALU.mult).then_inc(ph.sem("hidden_ready"), 1)
                    dve.wait_ge(ph.sem("hidden_ready"), n + 1)
                    dve.sem_inc(free, 1)
                low_of_hidden(lin.n - 1)
                add_to_x(k, dve, ph, down, split)


def ple_phase(k, h_parts):
    with k.phase("ple") as ph:
        gate, proj = ph.linear("ple_gate"), ph.linear("ple_proj")
        g, a = k.at(KT * T, MT, D)
        p_low, _ = k.at_parts(a, 2, T)
        pT, a = k.at(a, 2, T)
        p_high, a = k.at_parts(a, 2, T)
        p = Operand(ph, "p", pT, p_high, p_low)
        split = Split(k, ph, a)
        with k.engines(ph) as block:
            @block.sync
            def _(sp):
                sp.dma_start(pT, k.dram["pT"][bass.ds(k.layer, 1)].rearrange("a p k t -> (a p) k t")
                             ).then_inc(ph.sem("p_loaded"), 16)
                k.load_ahead(sp, ph)

            @block.tensor
            def _(pe):
                k.linear_tok(pe, ph, gate, h_parts, split=split)
                k.linear_tok(pe, ph, proj, p.wait(pe), split=split)

            @block.scalar
            def _(act):
                for n in range(2):
                    split.high_for(act, gate, n)
                    if n == 0:
                        act.wait_ge(ph.sem("p_loaded"), 16)
                        p.make_high(act)
                    pair, free = k.take(act, ph, gate, n)
                    act.activation(g[:, :, n * BLK:(n + 1) * BLK], pair, ACT.Sigmoid).then_inc(free, 1)

            @block.vector
            def _(dve):
                link = Chain(dve, ph.sem("dve_chain"))
                split.low_for(dve, gate, 1)
                p.make_low(dve)
                for n in range(2):
                    dve.wait_ge(ph.sem(f"pair_free{n}"), 1)
                    pair, free = k.take(dve, ph, proj, n)
                    part = g[:, :, n * BLK:(n + 1) * BLK]
                    link(dve.tensor_tensor(part, pair, part, ALU.mult))
                    dve.sem_inc(free, 1)
                    x_part = k.x[:, :, n * BLK:(n + 1) * BLK]
                    link(dve.tensor_tensor(x_part, x_part, part, ALU.add))


def first_layer(k):
    k.next_chunk, k.stream_at = 0, 0
    z = Tiles1(k)
    params = k.dram["params1"][bass.ds(k.layer, 1)].rearrange("a p n -> (a p) n")
    norm_phase(k, "mix_norm", k.x, k.p1("mix_norm"), k.hT, loads=[(k.par[:, 0:P1_W], params)], parts=(z.x_high, z.x_low))
    project_phase(k, z)
    latent_phase(k, z)
    batches = []
    gate = z.sgate.rearrange("p m (c h) -> p m c h", c=3)
    sinks = k.p1("sinks")
    for g in range(2):
        rows = slice(HD * g, HD * g + HD)
        for m in range(MT):
            toks = slice(m * P, (m + 1) * P)
            n_keys = (m + 1) * P
            causal = k.causal[:, P:2 * P] if m == 0 else k.causal[:]
            band = k.band[:, P:2 * P] if m == 0 else k.band[:]
            heads = slice(4 * g, 4 * g + 4)
            q_a = lambda h, c, rows=rows, toks=toks: z.qaT[rows, h, toks]
            q_b = lambda h, c, rows=rows, toks=toks: z.qbT[rows, h, toks]
            q_c = lambda h, c, g=g, toks=toks: z.qcT[0:96, 4 * g + h, toks]
            keys = lambda i, n=n_keys, rows=rows: (lambda h, c: z.keysT[rows, i, 0:n])
            vals = lambda i, g=g: (lambda h, kt, j: z.values[:, kt, 2 * i + g, :])
            outs = [z.oT[rows, i, :, toks] for i in range(3)]
            batches += [
                Batch(q_a, lambda h, c, rows=rows: z.kcmpT[rows, :], lambda h, kt, j, g=g: z.vcmp[0:N_CMP, g, :], N_CMP,
                      HD ** -0.5, outs[0], k.cmp_mask[:, m], gate[:, m, 0, heads]),
                Batch(q_a, keys(0), vals(1), n_keys, HD ** -0.5, outs[0], causal, gate[:, m, 1, heads], add=True),
                Batch(q_a, keys(1), vals(2), n_keys, HD ** -0.5, outs[0], causal, gate[:, m, 2, heads], add=True),
                Batch(q_b, keys(2), vals(3), n_keys, HD ** -0.5, outs[1], band, sink=sinks[:, heads]),
                Batch(q_c, lambda h, c, g=g, n=n_keys: z.kcT[0:96, 4 * g + h, 0:n],
                      lambda h, kt, j, g=g: z.vC[:, kt, 4 * g + h, :], n_keys, 96 ** -0.5, outs[2], causal),
            ]
    attention_phase(k, "attention", batches, z.probs, z.probsT, z.sum, z.nmax, [k.ps[:, 6:7, :], k.ps[:, 7:8, :]])
    branches_phase(k, z)
    h_parts = (k.at_parts(0, KT, T)[0], k.hT_low)
    norm_phase(k, "ffn_norm", k.x, k.p1("ffn_norm"), k.hT, parts=h_parts, scratch=KT * T)
    ffn_phase(k, h_parts)
    norm_phase(k, "ple_norm", k.x, k.p1("ple_norm"), k.hT, parts=h_parts, scratch=KT * T)
    ple_phase(k, h_parts)
    assert k.stream_at == len(STREAM_1) and k.next_chunk == CHUNKS_1


class TilesEven:

    def __init__(self, k):
        a = 0
        self.xcT, a = k.at(a, 20, T)
        self.xmT, a = k.at(a, KT, T + 3)
        self.z, a = k.at(a, MT, D)
        self.og, a = k.at(a, MT, D)
        self.small, a = k.at(a, MT, 24)
        self.h_high, b = k.at_parts(a, KT, T)
        self.h_low, _ = k.at_parts(b, KT, T)
        self.h_parts = (self.h_high, self.h_low)
        self.ya, a = k.at(a, MT, D)
        self.yb, a = k.at(a, MT, D)
        self.shared = a
        self.xbcT, a = k.at(self.shared, XBC_T, T + 3)
        self.in_end = a


def even_in_phase(k, z):
    with k.phase("even_in") as ph:
        lz, lx, lm, lo = (ph.linear(n) for n in ("ssd_z", "xbc", "xm", "og"))
        small_ps = k.ps[:, 4:6, 0:24]
        w_small = k.p2("w_small", KT)
        ssd_w, ssd_b = k.p2("conv_w", XBC_T), k.p2("conv_b")
        ml_w, ml_b = k.p2("ml_conv_w", KT), k.p2("ml_conv_b")
        fours = ([(z.xbcT[:, 4 * n:4 * n + 4], ssd_w[:, 4 * n:4 * n + 4], ssd_b[:, 4 * n:4 * n + 4], 4 * n) for n in range(3)]
                 + [(z.xmT[:, 4 * n:4 * n + 4], ml_w[:, 4 * n:4 * n + 4], ml_b[:, 4 * n:4 * n + 4], XBC_T + 4 * n) for n in range(2)])
        parts = z.h_parts
        split = Split(k, ph, z.in_end)

        def silu(act, i):
            x = z.xcT[:, fours[i][3]:fours[i][3] + 4, :]
            act.wait_ge(ph.sem("convolved"), i + 1)
            act.activation(x, x, ACT.Silu)

        with k.engines(ph) as block:
            @block.sync
            def _(sp):
                k.load_ahead(sp, ph)

            @block.tensor
            def _(pe):
                k.linear_tok(pe, ph, lz, parts, split=split)
                for kt in range(KT):
                    for m in range(MT):
                        last = pe.matmul(small_ps[:, m, :], k.hT[:, kt, m * P:(m + 1) * P], w_small[:, kt, :],
                                         start=(kt == 0), stop=(kt == KT - 1))
                last.then_inc(ph.sem("small_done"), 1)
                k.linear_T(pe, ph, lx, parts, split)
                k.linear_T(pe, ph, lm, parts, split)
                k.linear_tok(pe, ph, lo, parts, split=split)

            @block.gpsimd
            def _(pool):
                pool.memset(z.xbcT[:, :, 0:3], 0.0).then_inc(ph.sem("padded"), 1)
                pool.memset(z.xmT[:, :, 0:3], 0.0).then_inc(ph.sem("padded"), 1)

            @block.scalar
            def _(act):
                link = Chain(act, ph.sem("act_chain"))
                for n in range(2):
                    split.high_for(act, lz, n)
                    pair, free = k.take(act, ph, lz, n)
                    act.activation(z.z[:, :, n * BLK:(n + 1) * BLK], pair, ACT.Silu).then_inc(free, 1)
                act.wait_ge(ph.sem("small_done"), 1)
                link(act.activation(z.small, small_ps, ACT.Copy))
                act.wait_ge(ph.sem("padded"), 2)
                for i, (pad, w, b, at) in enumerate(fours):
                    lin, n = (lx, i) if i < 3 else (lm, i - 3)
                    split.high_for(act, lin, n)
                    pair, free = k.take(act, ph, lin, n)
                    link(act.activation(pad[:, :, 3:3 + T], pair.rearrange("p a (b t) -> p (a b) t", b=2), ACT.Copy))
                    act.sem_inc(free, 1)
                    for f in range(4):
                        link.note(act.activation(z.xcT[:, at + f, :], pad[:, f, 3:3 + T], ACT.Identity,
                                                 bias=b[:, f:f + 1], scale=w[:, f, 3:4]))
                    link.sync()
                    act.sem_inc(ph.sem("last_tap"), 1)
                    if i >= 1:
                        silu(act, i - 1)
                for n in range(2):
                    split.high_for(act, lo, n)
                    if n == 1:
                        silu(act, 4)
                    pair, free = k.take(act, ph, lo, n)
                    act.activation(z.og[:, :, n * BLK:(n + 1) * BLK], pair, ACT.Sigmoid).then_inc(free, 1)

            @block.vector
            def _(dve):
                link = Chain(dve, ph.sem("dve_chain"))
                split.low_for(dve, lx, 0)
                for i, (pad, w, b, at) in enumerate(fours):
                    lin, n = (lx, i) if i < 3 else (lm, i - 3)
                    split.low_for(dve, lin, n)
                    dve.wait_ge(ph.sem("last_tap"), i + 1)
                    for j in range(3):
                        for f in range(4):
                            y = z.xcT[:, at + f, :]
                            link.note(dve.scalar_tensor_tensor(out=y, in0=pad[:, f, j:j + T], scalar=w[:, f, j:j + 1],
                                                               in1=y, op0=ALU.mult, op1=ALU.add))
                        link.sync()
                    dve.sem_inc(ph.sem("convolved"), 1)
                split.low_for(dve, lo, 1)


def ssd_phase(k, z):
    with k.phase("ssd") as ph:
        G, E, HP, N = 2, 8, HD, P
        a = z.shared
        xs, a = k.at(a, MT, 16, HP)
        xdt, a = k.at(a, MT, 16, HP)
        bmat, a = k.at(a, G, N)
        states, a = k.at(a, G, E * HP)
        decay, a = k.at(a, 16, P)
        dt, a = k.at(a, MT, 16)
        dta, a = k.at(a, MT, 16)
        ncs, a = k.at(a, MT, 16)
        ecs, a = k.at(a, 16)
        dend, a = k.at(a, 16)
        neg_a, a = k.at(a, 16)
        tmp, a = k.at(a, MT, 16)
        tmp2, a = k.at(a, MT, 16)
        yoff, a = k.at(a, E * HP)
        bias, a_log, d_skip = k.p2("small_bias")[:, 0:16], k.p2("a_log"), k.p2("d_skip")
        ya = z.ya.rearrange("p m (h d) -> p m h d", h=16)
        ss, ms, y, t = (k.stat[:, i, 0:4] for i in range(4))
        jobs = [[(z.xcT[:, 4 * j + i, m * P:(m + 1) * P], i * P) for i in range(4)] for m in range(MT) for j in range(2)]
        jobs.append([(z.xcT[:, KT + g, 0:P], g * P) for g in range(G)])
        with k.engines(ph) as block:
            @block.sync
            def _(sp):
                k.load_ahead(sp, ph)

            @block.scalar
            def _(act):
                link = Chain(act, ph.sem("act_chain"))
                act.wait_ge(ph.sem("neg_abs_ready"), 1)
                link(act.activation(tmp, tmp, ACT.Exp))
                link(act.activation(tmp, tmp, ACT.Ln, bias=1.0))
                act.sem_inc(ph.sem("log_ready"), 1)
                link(act.activation(neg_a, a_log, ACT.Exp))
                act.sem_inc(ph.sem("a_ready"), 1)
                for i in range(4):
                    bank = k.turned(act, ph, "x", i, [6, 7])
                    m, j = i // 2, i % 2
                    act.activation(xs[:, m, 8 * j:8 * j + 8, :].rearrange("p a b -> p (a b)"), bank, ACT.Copy
                                   ).then_inc(ph.sem("x_copied"), 1)
                bank = k.turned(act, ph, "x", 4, [6, 7])
                act.activation(bmat.rearrange("p a b -> p (a b)"), bank[:, 0:G * N], ACT.Copy).then_inc(ph.sem("x_copied"), 1)
                act.wait_ge(ph.sem("ends_ready"), 1)
                link(act.activation(dend, dend, ACT.Exp))
                link(act.activation(ecs, ncs[:, 1, :], ACT.Exp, scale=-1.0))
                act.sem_inc(ph.sem("ends_exp"), 1)
                for c in range(MT):
                    act.wait_ge(ph.sem("decay_masked"), c + 1)
                    for h in range(16):
                        link.note(act.activation(decay[:, h, :], decay[:, h, :], ACT.Exp, bias=ncs[:, c, h:h + 1]))
                    link.sync()
                    act.sem_inc(ph.sem("decay_exp"), 1)
                for c in range(MT):
                    act.wait_ge(ph.sem("y_ready"), 1)
                    for g in range(G):
                        link(act.activation(yoff, z.ya[:, c, g * 512:(g + 1) * 512], ACT.Square,
                                            accum_out=ss[:, 2 * c + g:2 * c + g + 1]))
                act.sem_inc(ph.sem("squares_summed"), 1)
                k.rstd_scalar(act, ph, link, ms, y)

            @block.vector
            def _(dve):
                link = Chain(dve, ph.sem("dve_chain"))
                link(dve.tensor_tensor(dt, z.small[:, :, 0:16], bc(bias.unsqueeze(1), [P, MT, 16]), ALU.add))
                link(dve.tensor_scalar(tmp, dt, -1.0, None, ALU.mult))
                dve.tensor_tensor(tmp, tmp, dt, ALU.min).then_inc(ph.sem("neg_abs_ready"), 1)
                link(dve.tensor_scalar(dt, dt, 0.0, None, ALU.max))
                dve.wait_ge(ph.sem("log_ready"), 1)
                link(dve.tensor_tensor(dt, dt, tmp, ALU.add))
                dve.wait_ge(ph.sem("a_ready"), 1)
                link(dve.scalar_tensor_tensor(out=dta, in0=dt, scalar=-1.0, in1=bc(neg_a.unsqueeze(1), [P, MT, 16]),
                                              op0=ALU.mult, op1=ALU.mult))
                dve.sem_inc(ph.sem("dta_ready"), 1)
                dve.wait_ge(ph.sem("cumsum_done"), 1)
                link(dve.tensor_scalar(ncs, k.ps[:, 4, 0:32].rearrange("p (m h) -> p m h", m=MT), -1.0, None, ALU.mult))
                link(dve.tensor_tensor(dend, k.ps[:, 4, 32:48], ncs[:, 0, :], ALU.add))
                dve.sem_inc(ph.sem("ends_ready"), 1)
                dve.wait_ge(ph.sem("x_copied"), 5)
                link(dve.tensor_tensor(xdt, xs, bc(dt.unsqueeze(3), [P, MT, 16, HP]), ALU.mult))
                dve.wait_ge(ph.sem("ends_exp"), 1)
                for c in range(MT):
                    dve.wait_ge(ph.sem("rows_done"), c + 1)
                    if c == 1:
                        dve.wait_ge(ph.sem("diag_done"), 1)
                    rows = k.ps[:, 0:4, :].rearrange("p a (h l) -> p (a h) l", l=P)
                    link(dve.tensor_tensor(decay, rows, bc(k.upper_add[:].unsqueeze(1), [P, 16, P]), ALU.add))
                    dve.sem_inc(ph.sem("decay_masked"), 1)
                    dve.wait_ge(ph.sem("decay_exp"), c + 1)
                    dve.wait_ge(ph.sem("cb_done"), c + 1)
                    for g in range(G):
                        part = decay[:, 8 * g:8 * g + 8, :]
                        link(dve.tensor_tensor(part, bc(k.ps[:, 5, g * P:(g + 1) * P].unsqueeze(1), [P, 8, P]), part, ALU.mult))
                    dve.sem_inc(ph.sem("mixing_ready"), 1)
                    if c == 0:
                        late = ya[:, 1]
                        link(dve.tensor_tensor(late, xdt[:, 0], bc(dend.unsqueeze(2), [P, 16, HP]), ALU.mult))
                        dve.sem_inc(ph.sem("late_ready"), 1)
                        dve.wait_ge(ph.sem("states_done"), 1)
                        link(dve.tensor_copy(states, k.ps[:, 0:2, :]))
                        dve.sem_inc(ph.sem("states_ready"), 1)
                    dve.wait_ge(ph.sem("diag_done"), c + 1)
                    out = z.ya[:, c]
                    link(dve.tensor_tensor(ya[:, c], xs[:, c], bc(d_skip.unsqueeze(2), [P, 16, HP]), ALU.mult))
                    link(dve.tensor_tensor(out, k.ps[:, 6:8, :].rearrange("p a b -> p (a b)"), out, ALU.add))
                    dve.sem_inc(ph.sem("diag_taken"), 1)
                    if c == 1:
                        for g in range(G):
                            dve.wait_ge(ph.sem("carried_done"), 1)
                            link(dve.tensor_tensor(yoff.rearrange("p (h d) -> p h d", h=8),
                                                   k.ps[:, 2 + g, :].rearrange("p (h d) -> p h d", h=8),
                                                   bc(ecs[:, 8 * g:8 * g + 8].unsqueeze(2), [P, 8, HP]), ALU.mult))
                            half = z.ya[:, 1, g * 512:(g + 1) * 512]
                            link(dve.tensor_tensor(half, half, yoff, ALU.add))
                link(dve.tensor_tensor(z.ya, z.ya, z.z, ALU.mult))
                dve.sem_inc(ph.sem("y_ready"), 1)
                dve.wait_ge(ph.sem("squares_summed"), 1)
                k.rstd_vector_before(dve, ph, link, ss, ms, 512)
                k.rstd_vector_after(dve, ph, link, ms, y, t)
                link(dve.tensor_tensor(z.ya.rearrange("p m (g d) -> p m g d", g=2), z.ya.rearrange("p m (g d) -> p m g d", g=2),
                                       bc(y.rearrange("p (m g) -> p m g", m=MT).unsqueeze(3), [P, MT, 2, 512]), ALU.mult))

            @block.tensor
            def _(pe):
                k.transposes(pe, ph, "x", jobs, [6, 7])
                pe.wait_ge(ph.sem("dta_ready"), 1)
                for c in range(MT):
                    pe.matmul(k.ps[:, 4, 16 * c:16 * c + 16], k.upper[:], dta[:, c, :], start=True, stop=True)
                pe.matmul(k.ps[:, 4, 32:48], k.ones[:], dta[:, 0, :], start=True, stop=True).then_inc(ph.sem("cumsum_done"), 1)
                for c in range(MT):
                    if c == 1:
                        pe.wait_ge(ph.sem("states_ready"), 1)
                    for h in range(16):
                        last = pe.matmul(k.ps[:, h // 4, (h % 4) * P:(h % 4 + 1) * P], bc(dta[:, c, h:h + 1], [P, P]),
                                         k.upper[:], start=True, stop=True)
                    last.then_inc(ph.sem("rows_done"), 1)
                    for g in range(G):
                        last = pe.matmul(k.ps[:, 5, g * P:(g + 1) * P], z.xcT[:, 8 + g, c * P:(c + 1) * P],
                                         z.xcT[:, 10 + g, c * P:(c + 1) * P], start=True, stop=True)
                    last.then_inc(ph.sem("cb_done"), 1)
                    pe.wait_ge(ph.sem("mixing_ready"), c + 1)
                    if c == 1:
                        pe.wait_ge(ph.sem("diag_taken"), 1)
                    for h in range(16):
                        last = pe.matmul(k.ps[:, 6 + h // 8, (h % 8) * HP:(h % 8 + 1) * HP], decay[:, h, :], xdt[:, c, h, :],
                                         start=True, stop=True)
                    last.then_inc(ph.sem("diag_done"), 1)
                    if c == 0:
                        pe.wait_ge(ph.sem("late_ready"), 1)
                        for g in range(G):
                            last = pe.matmul(k.ps[:, g, :], bmat[:, g, :], z.ya[:, 1, g * 512:(g + 1) * 512], start=True, stop=True)
                        last.then_inc(ph.sem("states_done"), 1)
                    else:
                        for g in range(G):
                            last = pe.matmul(k.ps[:, 2 + g, :], z.xcT[:, 10 + g, P:2 * P], states[:, g, :], start=True, stop=True)
                        last.then_inc(ph.sem("carried_done"), 1)


def mlstm_phase(k, z):
    with k.phase("mlstm") as ph:
        H, DH = 4, 256
        lq, lk, lv = (ph.linear(n, grouped=False) for n in ("ml_wq", "ml_wk", "ml_wv"))
        a = z.shared
        qT, a = k.at(a, KT, T)
        kT, a = k.at(a, KT, T)
        v, a = k.at(a, MT, H, DH + 1)
        kw, a = k.at(a, H, DH)
        state, a = k.at(a, H, 2, DH + 1)
        g, a = k.at(a, 2, P)
        qk, a = k.at(a, 2, P)
        qkT, a = k.at(a, P)
        num, a = k.at(a, DH + 1)
        st = lambda i, n=8: k.stat[:, i // 8, 8 * (i % 8):8 * (i % 8) + n]
        it, logf, bcum, r, mt, at_, emt, rb = (st(i).rearrange("p (m h) -> p m h", m=MT) for i in range(8))
        tmp, mintra, bend, rmax, m_prev, wt, den, bmt = (st(8 + i) for i in range(8))
        tmp2 = tmp.rearrange("p (m h) -> p m h", m=MT)
        ss, ms, y, t = (st(16 + i) for i in range(4))
        bias = k.p2("small_bias")[:, 16:24]
        w = lambda lin: k.ring[:, lin.chunk0 % SLOTS, :].rearrange("p (h a e) -> p h a e", h=H, a=2)
        xc = z.xcT[:, XBC_T:20, :]
        with k.engines(ph) as block:
            @block.sync
            def _(sp):
                k.load_ahead(sp, ph)

            @block.scalar
            def _(act):
                link = Chain(act, ph.sem("act_chain"))
                act.wait_ge(ph.sem("neg_abs_ready"), 1)
                link(act.activation(tmp2, tmp2, ACT.Exp))
                link(act.activation(tmp2, tmp2, ACT.Ln, bias=1.0))
                act.sem_inc(ph.sem("log_ready"), 1)
                for i in range(4):
                    act.wait_ge(ph.sem("qk_done"), i + 1)
                    dst = (qT if i < 2 else kT)[:, 4 * (i % 2):4 * (i % 2) + 4, :].rearrange("p a t -> p (a t)")
                    act.activation(dst, k.ps[:, 2 * (i % 2):2 * (i % 2) + 2, :].rearrange("p a b -> p (a b)"), ACT.Copy,
                                   scale=1.0 if i < 2 else DH ** -0.5).then_inc(ph.sem("qk_copied"), 1)
                for i in range(2):
                    act.wait_ge(ph.sem("v_done"), i + 1)
                    act.activation(v[:, i, :, 0:DH], k.ps[:, 2 * i:2 * i + 2, :].rearrange("p a (h d) -> p (a h) d", h=2), ACT.Copy
                                   ).then_inc(ph.sem("v_copied"), 1)
                act.wait_ge(ph.sem("weights_arg"), 1)
                act.activation(wt[:, 0:H], wt[:, 0:H], ACT.Exp).then_inc(ph.sem("weights_exp"), 1)
                act.wait_ge(ph.sem("steady"), 1)
                link(act.activation(at_, at_, ACT.Exp))
                link(act.activation(emt, mt, ACT.Exp, scale=-1.0))
                act.sem_inc(ph.sem("steady_exp"), 1)

                def exp_of(i):
                    act.wait_ge(ph.sem("g_ready"), i + 1)
                    act.activation(g[:, i % 2, :], g[:, i % 2, :], ACT.Exp, bias=bmt[:, i:i + 1]).then_inc(ph.sem("g_exp"), 1)

                exp_of(0)
                for i in range(2 * H):
                    if i + 1 < 2 * H:
                        exp_of(i + 1)
                    act.wait_ge(ph.sem("qk_turned"), i + 1)
                    act.activation(qkT, k.ps[:, 6, 0:P], ACT.Copy).then_inc(ph.sem("qkT_ready"), 1)
                act.wait_ge(ph.sem("hid_ready"), 1)
                for i in range(2 * H):
                    c, h = divmod(i, H)
                    link(act.activation(num[:, 0:DH], z.yb[:, c, h * DH:(h + 1) * DH], ACT.Square, accum_out=ss[:, i:i + 1]))
                act.sem_inc(ph.sem("squares_summed"), 1)
                k.rstd_scalar(act, ph, link, ms, y)

            @block.gpsimd
            def _(pool):
                pool.memset(v[:, :, :, DH:DH + 1], 1.0).then_inc(ph.sem("ones_column"), 1)

            @block.vector
            def _(dve):
                link = Chain(dve, ph.sem("dve_chain"))
                link(dve.tensor_tensor(it, z.small[:, :, 16:20], bc(bias[:, 0:4].unsqueeze(1), [P, MT, H]), ALU.add))
                link(dve.tensor_tensor(logf, z.small[:, :, 20:24], bc(bias[:, 4:8].unsqueeze(1), [P, MT, H]), ALU.add))
                link(dve.tensor_scalar(tmp2, logf, -1.0, None, ALU.mult))
                dve.tensor_tensor(tmp2, tmp2, logf, ALU.min).then_inc(ph.sem("neg_abs_ready"), 1)
                link(dve.tensor_scalar(logf, logf, 0.0, None, ALU.min))
                dve.wait_ge(ph.sem("log_ready"), 1)
                link(dve.tensor_tensor(logf, logf, tmp2, ALU.subtract))
                dve.sem_inc(ph.sem("logf_ready"), 1)
                dve.wait_ge(ph.sem("cumsum_done"), 1)
                link(dve.tensor_copy(bcum, k.ps[:, 4, 0:8].rearrange("p (m h) -> p m h", m=MT)))
                link(dve.tensor_copy(bend[:, 0:H], k.ps[:, 4, 8:12]))
                link(dve.tensor_tensor(r, it, bcum, ALU.subtract))
                dve.sem_inc(ph.sem("r_ready"), 1)
                dve.wait_ge(ph.sem("rows_done"), 1)
                rows = [k.ps[:, 4 + c, :].rearrange("p (h s) -> p h s", h=H) for c in range(MT)]
                link(dve.tensor_reduce(rmax[:, 0:H], rows[0], AX, ALU.max))
                link(dve.tensor_scalar(rmax[:, 0:H], rmax[:, 0:H], 0.0, None, ALU.max))
                link(dve.tensor_tensor(wt[:, 0:H], r[:, 0, :], rmax[:, 0:H], ALU.subtract))
                dve.sem_inc(ph.sem("weights_arg"), 1)
                link(dve.memset(m_prev[:, 0:H], 0.0))
                link(dve.tensor_tensor(m_prev[:, H:2 * H], bend[:, 0:H], rmax[:, 0:H], ALU.add))
                for i in range(2 * H):
                    c, h = divmod(i, H)
                    link(dve.tensor_tensor(num[:, 0:P], rows[c][:, h, :], k.causal[:, P:2 * P], ALU.add))
                    link(dve.tensor_reduce(mintra[:, i:i + 1], num[:, 0:P], AX, ALU.max))
                b8, m8, a8 = st(2), st(4), st(5)
                link(dve.tensor_tensor(mintra, mintra, m_prev, ALU.max))
                link(dve.tensor_tensor(m8, mintra, b8, ALU.add))
                link(dve.tensor_tensor(bmt, b8, m8, ALU.subtract))
                link(dve.tensor_tensor(a8, bmt, m_prev, ALU.add))
                dve.sem_inc(ph.sem("steady"), 1)
                dve.wait_ge(ph.sem("weights_exp"), 1)
                dve.wait_ge(ph.sem("k_done"), 1)
                link(dve.tensor_scalar(wt[:, 0:H], wt[:, 0:H], DH ** -0.5, None, ALU.mult))
                link(dve.tensor_tensor(kw, k.ps[:, 0:2, :].rearrange("p a (h d) -> p (a h) d", h=2),
                                       bc(wt[:, 0:H].unsqueeze(2), [P, H, DH]), ALU.mult))
                dve.sem_inc(ph.sem("kw_ready"), 1)
                dve.wait_ge(ph.sem("steady_exp"), 1)
                for j in range(8):
                    dve.wait_ge(ph.sem("state_done"), j + 1)
                    dve.tensor_copy(state[:, j // 2, j % 2, :], k.ps[:, 2 * (j % 2), 0:DH + 1]).then_inc(ph.sem("state_copied"), 1)

                def mix(i):
                    c, h = divmod(i, H)
                    link(dve.tensor_tensor(g[:, i % 2, :], rows[c][:, h, :], k.causal[:, P:2 * P], ALU.add))
                    dve.sem_inc(ph.sem("g_ready"), 1)
                    dve.wait_ge(ph.sem("g_exp"), i + 1)
                    dve.wait_ge(ph.sem("scores_done"), i + 1)
                    if i >= 2:
                        dve.wait_ge(ph.sem("qk_turned"), i - 1)
                    dve.tensor_tensor(qk[:, i % 2], k.ps[:, 7 - 4 * (i % 2), 0:P], g[:, i % 2, :], ALU.mult
                                      ).then_inc(ph.sem("mixed"), 1)

                def take_out(i):
                    c, h = divmod(i, H)
                    dve.wait_ge(ph.sem("out_done"), i + 1)
                    link(dve.tensor_copy(num, k.ps[:, 0, 0:DH + 1]))
                    if c == 1:
                        link(dve.scalar_tensor_tensor(out=num, in0=k.ps[:, 1, 0:DH + 1], scalar=a8[:, i:i + 1], in1=num,
                                                      op0=ALU.mult, op1=ALU.add))
                    dve.sem_inc(ph.sem("out_taken"), 1)
                    link(dve.tensor_scalar(den[:, i:i + 1], num[:, DH:DH + 1], -1.0, None, ALU.mult))
                    link(dve.tensor_tensor(den[:, i:i + 1], den[:, i:i + 1], num[:, DH:DH + 1], ALU.max))
                    link(dve.tensor_tensor(den[:, i:i + 1], den[:, i:i + 1], st(6)[:, i:i + 1], ALU.max))
                    link(dve.reciprocal(den[:, i:i + 1], den[:, i:i + 1]))
                    link(dve.tensor_scalar(z.yb[:, c, h * DH:(h + 1) * DH], num[:, 0:DH], den[:, i:i + 1], None, ALU.mult))

                mix(0)
                for i in range(2 * H):
                    if i + 1 < 2 * H:
                        mix(i + 1)
                    take_out(i)
                dve.sem_inc(ph.sem("hid_ready"), 1)
                dve.wait_ge(ph.sem("squares_summed"), 1)
                k.rstd_vector_before(dve, ph, link, ss, ms, DH)
                k.rstd_vector_after(dve, ph, link, ms, y, t)
                link(dve.tensor_tensor(z.yb, z.yb, z.og, ALU.mult))
                heads = z.yb.rearrange("p m (h d) -> p m h d", h=H)
                link(dve.tensor_tensor(heads, heads, bc(y.rearrange("p (m h) -> p m h", m=MT).unsqueeze(3), [P, MT, H, DH]), ALU.mult))

            @block.tensor
            def _(pe):
                for i in range(4):
                    lin = lq if i < 2 else lk
                    if i % 2 == 0:
                        k.wait_chunk(pe, lin.chunk0)
                    if i >= 2:
                        pe.wait_ge(ph.sem("qk_copied"), i - 1)
                    for f in range(4):
                        h, e = divmod(4 * (i % 2) + f, 2)
                        for d in range(2):
                            last = pe.matmul(k.ps[:, 2 * (i % 2) + f // 2, (f % 2) * T:(f % 2 + 1) * T],
                                             w(lin)[:, h, d, e * P:(e + 1) * P], xc[:, 2 * h + d, :], start=(d == 0), stop=(d == 1))
                    last.then_inc(ph.sem("qk_done"), 1)
                pe.wait_ge(ph.sem("logf_ready"), 1)
                for c in range(MT):
                    pe.matmul(k.ps[:, 4, 4 * c:4 * c + 4], k.upper[:], logf[:, c, :], start=True, stop=True)
                pe.matmul(k.ps[:, 4, 8:12], k.ones[:], logf[:, 0, :], start=True, stop=True).then_inc(ph.sem("cumsum_done"), 1)
                pe.wait_ge(ph.sem("qk_copied"), 4)
                pe.sem_inc(k.ring_free[lq.chunk0 % SLOTS], 1)
                k.wait_chunk(pe, lv.chunk0)
                for c in range(MT):
                    for h in range(H):
                        for d in range(2):
                            last = pe.matmul(k.ps[:, 2 * c + h // 2, (h % 2) * DH:(h % 2 + 1) * DH],
                                             z.xmT[:, 2 * h + d, 3 + c * P:3 + (c + 1) * P], w(lv)[:, h, d, :], start=(d == 0), stop=(d == 1))
                    last.then_inc(ph.sem("v_done"), 1)
                pe.wait_ge(ph.sem("r_ready"), 1)
                for c in range(MT):
                    for h in range(H):
                        last = pe.matmul(k.ps[:, 4 + c, h * P:(h + 1) * P], bc(r[:, c, h:h + 1], [P, P]), k.ident[:], start=True, stop=True)
                last.then_inc(ph.sem("rows_done"), 1)
                pe.wait_ge(ph.sem("v_copied"), 2)
                pe.sem_inc(k.ring_free[lv.chunk0 % SLOTS], 1)
                for h in range(H):
                    for d in range(2):
                        last = pe.matmul(k.ps[:, h // 2, (h % 2) * DH:(h % 2 + 1) * DH], xc[:, 2 * h + d, 0:P], w(lk)[:, h, d, :],
                                         start=(d == 0), stop=(d == 1))
                last.then_inc(ph.sem("k_done"), 1)
                pe.wait_ge(ph.sem("kw_ready"), 1)
                pe.sem_inc(k.ring_free[lk.chunk0 % SLOTS], 1)
                pe.wait_ge(ph.sem("ones_column"), 1)
                for j in range(8):
                    if j >= 2:
                        pe.wait_ge(ph.sem("state_copied"), j - 1)
                    h, d = divmod(j, 2)
                    pe.matmul(k.ps[:, 2 * (j % 2), 0:DH + 1], kw[:, h, d * P:(d + 1) * P], v[:, 0, h, :], start=True, stop=True
                              ).then_inc(ph.sem("state_done"), 1)
                pe.wait_ge(ph.sem("state_copied"), 8)

                def scores(i):
                    c, h = divmod(i, H)
                    toks = slice(c * P, (c + 1) * P)
                    if i >= 2:
                        pe.wait_ge(ph.sem("mixed"), i - 1)
                    for d in range(2):
                        last = pe.matmul(k.ps[:, 7 - 4 * (i % 2), 0:P], qT[:, 2 * h + d, toks], kT[:, 2 * h + d, toks],
                                         start=(d == 0), stop=(d == 1))
                    last.then_inc(ph.sem("scores_done"), 1)

                scores(0)
                for i in range(2 * H):
                    c, h = divmod(i, H)
                    toks = slice(c * P, (c + 1) * P)
                    if i + 1 < 2 * H:
                        scores(i + 1)
                    pe.wait_ge(ph.sem("mixed"), i + 1)
                    if i >= 1:
                        pe.wait_ge(ph.sem("qkT_ready"), i)
                    pe.transpose(k.ps[:, 6, 0:P], qk[:, i % 2], k.ident[:]).then_inc(ph.sem("qk_turned"), 1)
                    if i >= 1:
                        pe.wait_ge(ph.sem("out_taken"), i)
                    if c == 1:
                        for d in range(2):
                            pe.matmul(k.ps[:, 1, 0:DH + 1], qT[:, 2 * h + d, toks], state[:, h, d, :], start=(d == 0), stop=(d == 1))
                    pe.wait_ge(ph.sem("qkT_ready"), i + 1)
                    pe.matmul(k.ps[:, 0, 0:DH + 1], qkT, v[:, c, h, :], start=True, stop=True).then_inc(ph.sem("out_done"), 1)


def mixer_out_phase(k, name, sources, gains, lin_name, at, spare):
    with k.phase(name) as ph:
        lin = ph.linear(lin_name)
        mixT, _ = k.at(at, KT * len(sources), T)
        mix_low, _ = k.at_parts(at, KT * len(sources), T)
        mix_high, a = k.at_parts(spare, KT * len(sources), T)
        split = Split(k, ph, a)
        jobs = [j for s in sources for j in feature_groups(s, 0, KT)]
        banks = [4, 5, 6, 7]
        with k.engines(ph) as block:
            @block.sync
            def _(sp):
                k.load_ahead(sp, ph)

            @block.tensor
            def _(pe):
                k.transposes(pe, ph, "mix", jobs, banks)
                pe.wait_ge(ph.sem("mix_low"), len(jobs))
                k.linear_tok(pe, ph, lin, (mix_high, mix_low), split=split)

            @block.scalar
            def _(act):
                for i in range(len(jobs)):
                    act.wait_ge(ph.sem("mix_copied"), i + 1)
                    act.activation(mix_high[:, 2 * i:2 * i + 2, :], mixT[:, 2 * i:2 * i + 2, :], ACT.Copy).then_inc(ph.sem("mix_high"), 1)
                split.high_for(act, lin, 1)

            @block.vector
            def _(dve):
                def low(i):
                    dve.wait_ge(ph.sem("mix_high"), i + 1)
                    part = slice(2 * i, 2 * i + 2)
                    dve.tensor_tensor(mix_low[:, part, :], mixT[:, part, :], mix_high[:, part, :].bitcast(F32), ALU.subtract
                                      ).then_inc(ph.sem("mix_low"), 1)

                for i in range(len(jobs)):
                    bank = k.turned(dve, ph, "mix", i, banks)
                    dst = mixT[:, 2 * i:2 * i + 2, :]
                    src = bank.rearrange("p (a t) -> p a t", a=2)
                    gain = gains[i // 4]
                    if gain is None:
                        ins = dve.tensor_copy(dst, src)
                    else:
                        ins = dve.tensor_tensor(dst, src, bc(gain[:, 2 * (i % 4):2 * (i % 4) + 2].unsqueeze(2), [P, 2, T]), ALU.mult)
                    ins.then_inc(ph.sem("mix_copied"), 1)
                    if i >= 1:
                        low(i - 1)
                low(len(jobs) - 1)
                add_to_x(k, dve, ph, lin, split)


class TilesOdd:

    def __init__(self, k):
        a = 0
        self.h_parts = (k.at_parts(a, KT, T)[0], k.hT_low)
        self.y, a = k.at(a, MT, D)
        self.v, a = k.at(a, MT, D)
        self.gate, a = k.at(a, MT, D)
        self.mixer = a
        self.fT, a = k.at(a, KT, T)
        self.kT, a = k.at(a, KT, T)
        self.qT, a = k.at(a, KT, T)
        self.e1, a = k.at(a, KT, T)
        self.e2, a = k.at(a, KT, T)
        self.reset, a = k.at(a, KT * T)
        self.lb, a = k.at(a, KT)
        self.oml, a = k.at(a, KT)
        self.t1, a = k.at(a, KT)
        self.t2, a = k.at(a, KT)
        shared = a
        self.in_end = a
        self.att, a = k.at(shared, 8, P)
        self.kd, a = k.at(a, MT, 8, P)
        self.state, a = k.at(a, 2, 8, P)
        self.adec, a = k.at(a, 8, 4)


def odd_in_phase(k, z):
    with k.phase("odd_in") as ph:
        lf, lq, lv, lg = (ph.linear(n) for n in ("hgrn_f", "hgrn_q", "hgrn_v", "hgrn_g"))
        logits = k.p2("lb_logits", DEPTH)
        e = z.e1
        parts = z.h_parts
        split = Split(k, ph, z.in_end)
        with k.engines(ph) as block:
            @block.sync
            def _(sp):
                k.load_ahead(sp, ph)

            @block.tensor
            def _(pe):
                k.linear_T(pe, ph, lf, parts, split)
                k.linear_T(pe, ph, lq, parts, split)
                k.linear_tok(pe, ph, lv, parts, split=split)
                k.linear_tok(pe, ph, lg, parts, split=split)

            @block.gpsimd
            def _(pool):
                link = Chain(pool, ph.sem("pool_chain"))
                link(pool.memset(z.reset, 1.0))
                link(pool.memset(z.reset.rearrange("p (c l) -> p c l", l=HD)[:, :, 0:1], 0.0))
                pool.sem_inc(ph.sem("reset_ready"), 1)

            @block.scalar
            def _(act):
                link = Chain(act, ph.sem("act_chain"))
                act.wait_ge(ph.sem("logits_shifted"), 1)
                link(act.activation(z.t1, z.t1, ACT.Exp))
                link(act.activation(z.t2, z.t2, ACT.Exp))
                act.sem_inc(ph.sem("logits_exp"), 1)
                for n in range(2):
                    split.high_for(act, lf, n)
                    pair, free = k.take(act, ph, lf, n)
                    link(act.activation(e[:, 4 * n:4 * n + 4, :].rearrange("p a t -> p (a t)"), pair.rearrange("p a b -> p (a b)"),
                                        ACT.Exp, scale=-1.0))
                    act.sem_inc(free, 1)
                act.sem_inc(ph.sem("f_exp"), 1)
                split.high_for(act, lq, 0)
                act.wait_ge(ph.sem("f_sigmoid"), 1)
                for i in range(KT):
                    link.note(act.activation(z.fT[:, i, :], z.fT[:, i, :], ACT.Ln, bias=z.lb[:, i:i + 1], scale=z.oml[:, i:i + 1]))
                link.sync()
                act.sem_inc(ph.sem("logf_ready"), 1)
                for n in range(2):
                    split.high_for(act, lq, n)
                    pair, free = k.take(act, ph, lq, n)
                    act.activation(z.qT[:, 4 * n:4 * n + 4, :].rearrange("p a t -> p (a t)"), pair.rearrange("p a b -> p (a b)"), ACT.Silu
                                   ).then_inc(free, 1)
                for n in range(2):
                    split.high_for(act, lv, n)
                    pair, free = k.take(act, ph, lv, n)
                    act.activation(z.v[:, :, n * BLK:(n + 1) * BLK], pair, ACT.Copy).then_inc(free, 1)
                for n in range(2):
                    split.high_for(act, lg, n)
                    pair, free = k.take(act, ph, lg, n)
                    act.activation(z.gate[:, :, n * BLK:(n + 1) * BLK], pair, ACT.Silu).then_inc(free, 1)

            @block.vector
            def _(dve):
                link = Chain(dve, ph.sem("dve_chain"))
                link(dve.tensor_tensor(z.lb, logits[:, 0], logits[:, 1], ALU.max))
                link(dve.tensor_tensor(z.t1, logits[:, 0], z.lb, ALU.subtract))
                link(dve.tensor_tensor(z.t2, logits[:, 1], z.lb, ALU.subtract))
                dve.sem_inc(ph.sem("logits_shifted"), 1)
                dve.wait_ge(ph.sem("logits_exp"), 1)
                link(dve.tensor_tensor(z.oml, z.t1, z.t2, ALU.add))
                link(dve.reciprocal(z.oml, z.oml))
                link(dve.tensor_tensor(z.lb, z.t1, z.oml, ALU.mult))
                link(dve.tensor_tensor(z.oml, z.t2, z.oml, ALU.mult))
                split.low_for(dve, lf, 1)
                dve.wait_ge(ph.sem("f_exp"), 1)
                link(dve.tensor_scalar(e, e, 1e30, None, ALU.min))
                link(dve.tensor_scalar(z.fT, e, 1.0, None, ALU.add))
                split.low_for(dve, lq, 0)
                link(dve.reciprocal(z.fT, z.fT))
                link(dve.tensor_tensor(z.kT, e, z.fT, ALU.mult))
                dve.sem_inc(ph.sem("f_sigmoid"), 1)
                link(dve.tensor_tensor(z.kT, z.kT, bc(z.oml.unsqueeze(2), [P, KT, T]), ALU.mult))
                dve.wait_ge(ph.sem("logf_ready"), 1)
                dve.wait_ge(ph.sem("reset_ready"), 1)
                flat = z.fT.rearrange("p a t -> p (a t)")
                link(dve.tensor_tensor_scan(e.rearrange("p a t -> p (a t)"), z.reset, flat, 0.0, ALU.mult, ALU.add))
                link(dve.tensor_copy(z.fT, e))
                split.low_for(dve, lg, 1)


def hgrn_phase(k, z):
    with k.phase("hgrn") as ph:
        gc = z.fT.rearrange("p h (c l) -> p (h c) l", l=HD)
        e1 = z.e1.rearrange("p h (c l) -> p (h c) l", l=HD)
        e2 = z.e2.rearrange("p h (c l) -> p (h c) l", l=HD)
        qg = z.reset.rearrange("p (h t) -> p h t", h=8)
        kT = z.kT.rearrange("p h (c l) -> p (h c) l", l=HD)
        ref = bc(gc[:, :, HD // 2:HD // 2 + 1], [P, 32, HD])
        end = bc(gc[:, :, HD - 1:HD], [P, 32, HD])
        ss, ms, y, t = (k.stat[:, i, 0:16] for i in range(4))
        jobs = [[(z.e1[:, 4 * j + i, m * P:(m + 1) * P], i * P) for i in range(4)] for m in range(MT) for j in range(2)]
        with k.engines(ph) as block:
            @block.sync
            def _(sp):
                k.load_ahead(sp, ph)

            @block.vector
            def _(dve):
                link = Chain(dve, ph.sem("dve_chain"))
                link(dve.tensor_tensor(e1, end, gc, ALU.subtract))
                dve.sem_inc(ph.sem("to_end"), 1)
                dve.wait_ge(ph.sem("to_end_exp"), 1)
                link(dve.tensor_tensor(e1, e1, kT, ALU.mult))
                dve.sem_inc(ph.sem("keys_decayed"), 1)
                link(dve.tensor_tensor(e2, gc, ref, ALU.subtract))
                dve.sem_inc(ph.sem("to_middle"), 1)
                dve.wait_ge(ph.sem("middle_exp"), 1)
                link(dve.tensor_tensor(qg, qg, z.qT, ALU.mult))
                link(dve.tensor_tensor(z.qT, z.qT, z.e2, ALU.mult))
                link(dve.tensor_tensor(z.kT, z.kT, z.fT, ALU.mult))
                dve.sem_inc(ph.sem("operands_ready"), 1)
                for m in range(MT):
                    dve.wait_ge(ph.sem("att_done"), m + 1)
                    if m == 1:
                        dve.wait_ge(ph.sem("own_done"), 1)
                    link(dve.tensor_scalar(z.att.rearrange("p h l -> p (h l)"), k.ps[:, 0:2, :].rearrange("p a b -> p (a b)"),
                                           3e38, -3e38, ALU.min, ALU.max))
                    link(dve.tensor_tensor(z.att, z.att, bc(k.chunk_upper[:].unsqueeze(1), [P, 8, P]), ALU.mult))
                    dve.sem_inc(ph.sem("att_masked"), 1)
                    dve.wait_ge(ph.sem("own_done"), m + 1)
                    link(dve.tensor_copy(z.y[:, m, :], k.ps[:, 2:4, :].rearrange("p a b -> p (a b)")))
                    dve.sem_inc(ph.sem("own_taken"), 1)
                for c in range(1, 4):
                    dve.wait_ge(ph.sem("local_done"), c)
                    new, old = z.state[:, c % 2], z.state[:, (c + 1) % 2]
                    local = k.ps[:, 6:8, :].rearrange("p a (h e) -> p (a h) e", h=4)
                    if c == 1:
                        link(dve.tensor_copy(new, local))
                    else:
                        for h in range(8):
                            link.note(dve.scalar_tensor_tensor(out=new[:, h, :], in0=old[:, h, :], scalar=z.adec[:, h, c - 1:c],
                                                               in1=local[:, h, :], op0=ALU.mult, op1=ALU.add))
                        link.sync()
                    dve.sem_inc(ph.sem("state_ready"), 1)
                    dve.wait_ge(ph.sem("carried_done"), c)
                    rows = slice(HD * (c % 2), HD * (c % 2) + HD)
                    o = z.y[rows, c // 2, :]
                    link(dve.tensor_tensor(o, k.ps[rows, 4:6, :].rearrange("p a b -> p (a b)"), o, ALU.add))
                    dve.sem_inc(ph.sem("carried_taken"), 1)
                dve.sem_inc(ph.sem("y_ready"), 1)
                dve.wait_ge(ph.sem("squares_summed"), 1)
                k.rstd_vector_before(dve, ph, link, ss, ms, P)
                k.rstd_vector_after(dve, ph, link, ms, y, t)
                link(dve.tensor_tensor(z.y, z.y, z.gate, ALU.mult))
                heads = z.y.rearrange("p m (h d) -> p (m h) d", h=8)
                link(dve.tensor_tensor(heads, heads, bc(y.unsqueeze(2), [P, 16, P]), ALU.mult))

            @block.scalar
            def _(act):
                link = Chain(act, ph.sem("act_chain"))
                act.wait_ge(ph.sem("to_end"), 1)
                link(act.activation(z.e1, z.e1, ACT.Exp))
                act.sem_inc(ph.sem("to_end_exp"), 1)
                act.wait_ge(ph.sem("to_middle"), 1)
                link.note(act.activation(z.adec, z.fT.rearrange("p h (c l) -> p h c l", l=HD)[:, :, :, HD - 1], ACT.Exp))
                link(act.activation(qg, z.fT, ACT.Exp))
                link(act.activation(z.fT, z.e2, ACT.Exp, scale=-1.0))
                link(act.activation(z.e2, z.e2, ACT.Exp))
                act.sem_inc(ph.sem("middle_exp"), 1)
                for i in range(4):
                    bank = k.turned(act, ph, "kd", i, [4, 5])
                    act.activation(z.kd[:, i // 2, 4 * (i % 2):4 * (i % 2) + 4, :].rearrange("p a b -> p (a b)"), bank, ACT.Copy
                                   ).then_inc(ph.sem("kd_copied"), 1)
                act.wait_ge(ph.sem("y_ready"), 1)
                for i in range(16):
                    m, h = divmod(i, 8)
                    link.note(act.activation(z.e1[:, h, 0:P] if m == 0 else z.e1[:, h, P:T], z.y[:, m, h * P:(h + 1) * P], ACT.Square,
                                             accum_out=ss[:, i:i + 1]))
                link.sync()
                act.sem_inc(ph.sem("squares_summed"), 1)
                k.rstd_scalar(act, ph, link, ms, y)

            @block.tensor
            def _(pe):
                pe.wait_ge(ph.sem("keys_decayed"), 1)
                k.transposes(pe, ph, "kd", jobs, [4, 5])
                pe.wait_ge(ph.sem("operands_ready"), 1)
                for m in range(MT):
                    toks = slice(m * P, (m + 1) * P)
                    if m == 1:
                        pe.wait_ge(ph.sem("att_masked"), 1)
                    for h in range(8):
                        last = pe.matmul(k.ps[:, h // 4, (h % 4) * P:(h % 4 + 1) * P], z.kT[:, h, toks], z.qT[:, h, toks], start=True, stop=True)
                    last.then_inc(ph.sem("att_done"), 1)
                    pe.wait_ge(ph.sem("att_masked"), m + 1)
                    if m == 1:
                        pe.wait_ge(ph.sem("own_taken"), 1)
                    for h in range(8):
                        last = pe.matmul(k.ps[:, 2 + h // 4, (h % 4) * P:(h % 4 + 1) * P], z.att[:, h, :], z.v[:, m, h * P:(h + 1) * P],
                                         start=True, stop=True)
                    last.then_inc(ph.sem("own_done"), 1)
                pe.wait_ge(ph.sem("kd_copied"), 4)
                for c in range(3):
                    rows, m = slice(HD * (c % 2), HD * (c % 2) + HD), c // 2
                    for h in range(8):
                        last = pe.matmul(k.ps[:, 6 + h // 4, (h % 4) * P:(h % 4 + 1) * P], z.kd[rows, m, h, :], z.v[rows, m, h * P:(h + 1) * P],
                                         start=True, stop=True)
                    last.then_inc(ph.sem("local_done"), 1)
                    pe.wait_ge(ph.sem("state_ready"), c + 1)
                    if c >= 1:
                        pe.wait_ge(ph.sem("carried_taken"), c)
                    n = c + 1
                    out = slice(HD * (n % 2), HD * (n % 2) + HD)
                    for h in range(8):
                        last = pe.matmul(k.ps[out, 4 + h // 4, (h % 4) * P:(h % 4 + 1) * P], qg[:, h, n * HD:(n + 1) * HD], z.state[:, n % 2, h, :],
                                         start=True, stop=True)
                    last.then_inc(ph.sem("carried_done"), 1)


def cross_attention(k, layer):
    a = 0
    mem_low, _ = k.at_parts(a, KT, T)
    memT, a = k.at(a, KT, T)
    qT, a = k.at(a, KT, T)
    kT, a = k.at(a, KT, T)
    v, a = k.at(a, MT, D)
    mem_high, _ = k.at_parts(a, KT, T)
    o_low, _ = k.at_parts(a, KT, T)
    oT, a = k.at(a, KT, T)
    x_high, _ = k.at_parts(a, KT, T)
    probs, a = k.at(a, 3, 4, T)
    probsT, a = k.at(a, 2, 2, 4, P)
    sums, a = k.at(a, MT, 4)
    nmax, a = k.at(a, MT, 4)
    memory = qT.rearrange("p a t -> p (a t)").rearrange("p (m d) -> p m d", m=MT)
    norm_phase(k, "norm_xattn", k.x, k.p2("norm_xattn"), k.hT, loads=[(memory, k.dram["mem"])], scratch=a, parts=(x_high, k.hT_low))
    norm_phase(k, "norm_mem", memory, k.p2("norm_mem"), memT, scratch=a, parts=(mem_high, mem_low))
    with k.phase("xa_in") as ph:
        lq, lk, lv = (ph.linear(n) for n in ("xa_q", "xa_k", "xa_v"))
        split = Split(k, ph, a)
        with k.engines(ph) as block:
            @block.sync
            def _(sp):
                k.load_ahead(sp, ph)

            @block.tensor
            def _(pe):
                k.linear_T(pe, ph, lq, (x_high, k.hT_low), split)
                k.linear_T(pe, ph, lk, (mem_high, mem_low), split)
                k.linear_tok(pe, ph, lv, (mem_high, mem_low), split=split)

            @block.scalar
            def _(act):
                for lin, dst in ((lq, qT), (lk, kT)):
                    for n in range(2):
                        split.high_for(act, lin, n)
                        pair, free = k.take(act, ph, lin, n)
                        act.activation(dst[:, 4 * n:4 * n + 4, :].rearrange("p a t -> p (a t)"), pair.rearrange("p a b -> p (a b)"), ACT.Copy
                                       ).then_inc(free, 1)
                for n in range(2):
                    split.high_for(act, lv, n)
                    pair, free = k.take(act, ph, lv, n)
                    act.activation(v[:, :, n * BLK:(n + 1) * BLK], pair, ACT.Copy).then_inc(free, 1)

            @block.vector
            def _(dve):
                split.low_for(dve, lv, 1)

    batches = []
    for m in range(MT):
        toks = slice(m * P, (m + 1) * P)
        batches.append(Batch(lambda h, c, toks=toks: qT[:, 2 * h + c, toks], lambda h, c: kT[:, 2 * h + c, :],
                             lambda h, kt, j: v[:, kt, h * T + j * P:h * T + (j + 1) * P], T, T ** -0.5, oT[:, :, toks],
                             contract=2, pieces=2))
    attention_phase(k, "xa_attend", batches, probs, probsT, sums, nmax, [k.ps[:, 6:8, :]])
    with k.phase("xa_out") as ph:
        lin = ph.linear("xa_o")
        heads = Operand(ph, "heads", oT, k.at_parts(0, KT, T)[0], o_low)
        split = Split(k, ph, a)
        with k.engines(ph) as block:
            @block.sync
            def _(sp):
                k.load_ahead(sp, ph)

            @block.tensor
            def _(pe):
                k.linear_tok(pe, ph, lin, heads.wait(pe), split=split)

            @block.scalar
            def _(act):
                heads.make_high(act)
                split.high_for(act, lin, 1)

            @block.vector
            def _(dve):
                heads.make_low(dve)
                add_to_x(k, dve, ph, lin, split)


class Peer:

    def __init__(self, k):
        a = 0
        self.xt, a = k.at(a, MT, D)
        self.index, a = k.at(a, MT * SLOTS_PER_TOKEN + 2 * GATHER)
        self.gates, a = k.at(a, MT * SLOTS_PER_TOKEN)
        self.scores1, a = k.at(a, 16, PE_KEYS)
        self.best, a = k.at(a, MT, 16, PE_TOP)
        self.best_at, a = k.at(a, MT, 16, PE_TOP)
        self.cand, a = k.at(a, PE_HEADS, PE_TOP * PE_TOP)
        self.chosen, a = k.at(a, PE_HEADS, PE_TOP)
        self.chosen_at, a = k.at(a, 2, SLOTS_PER_TOKEN)
        raw, a = k.at(a, 16, PE_TOP)
        raw2, a = k.at(a, PE_HEADS, PE_TOP)
        self.hot, a = k.at(a, SLOTS_PER_TOKEN, PE_TOP)
        self.iota, a = k.at(a, PE_TOP)
        self.part, a = k.at(a, 2, SLOTS_PER_TOKEN)
        self.raw, self.raw2, self.parti = raw.bitcast(U32), raw2.bitcast(U32), self.part.bitcast(U32)
        self.kept = a
        self.qT, a = k.at(a, 16, T)
        self.scores0, a = k.at(a, 16, PE_KEYS)
        self.x_high, a = k.at_parts(a, KT, T)
        self.route_end = a
        self.scores = [self.scores0, self.scores1]
        self.rows, a = k.at(self.kept, 2, GATHER, 2 * D)
        self.dots, a = k.at(a, 2, 2, GATHER)

    def top16(self, dve, link, jobs):
        for values, to, at in jobs:
            link.note(dve.max(to[:, 0:8], values))
        link.sync()
        for values, to, at in jobs:
            link.note(dve.max_index(at[:, 0:8], to[:, 0:8], values))
        link.sync()
        for values, to, at in jobs:
            link.note(dve.match_replace(values, to[:, 0:8], values, -3e38))
        link.sync()
        for values, to, at in jobs:
            link.note(dve.max(to[:, 8:16], values))
        link.sync()
        for values, to, at in jobs:
            link.note(dve.max_index(at[:, 8:16], to[:, 8:16], values))
        link.sync()

    def keys(self, dve, link, m, which):
        self.top16(dve, link, [(self.scores[m][:, hp, :], self.best[:, m, hp, :], self.raw[:, hp, :]) for hp in which])

    def pairs(self, dve, link, m):
        link.note(dve.tensor_copy(self.best_at[:, m], self.raw))
        pairs = self.best[:, m].rearrange("p (h two) i -> p h two i", two=2)
        grid = [P, PE_HEADS, PE_TOP, PE_TOP]
        link(dve.tensor_tensor(self.cand.rearrange("p h (i j) -> p h i j", i=PE_TOP), bc(pairs[:, :, 0, :].unsqueeze(3), grid),
                               bc(pairs[:, :, 1, :].unsqueeze(2), grid), ALU.add))

    def heads(self, dve, link, which):
        self.top16(dve, link, [(self.cand[:, h, :], self.chosen[:, h, :], self.raw2[:, h, :]) for h in which])

    def shift(self, dve, ph, link):
        link(dve.tensor_copy(self.hot[:, 0:PE_HEADS, 0:1], self.chosen[:, :, 0:1]))
        dve.tensor_tensor(self.chosen, self.chosen, bc(self.hot[:, 0:PE_HEADS, 0:1], [P, PE_HEADS, PE_TOP]), ALU.subtract
                          ).then_inc(ph.sem("chosen_shifted"), 1)
        dve.wait_ge(ph.sem("chosen_shifted"), 1)
        flat = self.raw2.rearrange("p h i -> p (h i)")
        link.note(dve.tensor_scalar(self.parti[:, 0], flat, 4, None, ALU.logical_shift_right))
        link(dve.tensor_scalar(self.parti[:, 1], flat, 15, None, ALU.bitwise_and))
        link(dve.tensor_copy(self.chosen_at, self.parti))

    def look_up(self, dve, link, m, i):
        wide = [P, SLOTS_PER_TOKEN, PE_TOP]
        grid = [P, PE_HEADS, PE_TOP, PE_TOP]
        link(dve.tensor_tensor(self.hot, bc(self.chosen_at[:, i].unsqueeze(2), wide), bc(self.iota.unsqueeze(1), wide), ALU.is_equal))
        hot = self.hot.rearrange("p (h s) i -> p h s i", h=PE_HEADS)
        at_pairs = self.best_at[:, m].rearrange("p (h two) i -> p h two i", two=2)
        link(dve.tensor_tensor(hot, hot, bc(at_pairs[:, :, i, :].unsqueeze(2), grid), ALU.mult))
        link(dve.tensor_reduce(self.part[:, i], self.hot, AX, ALU.add))

    def finish(self, dve, ph, link, m):
        slots = slice(m * SLOTS_PER_TOKEN, (m + 1) * SLOTS_PER_TOKEN)
        link.note(dve.scalar_tensor_tensor(out=self.index[:, slots], in0=self.part[:, 0], scalar=float(PE_KEYS), in1=self.part[:, 1],
                                           op0=ALU.mult, op1=ALU.add))
        dve.wait_ge(ph.sem("chosen_exp"), 1)
        total = self.hot[:, 0:PE_HEADS, 1:2]
        link(dve.tensor_reduce(total, self.chosen, AX, ALU.add))
        link(dve.reciprocal(total, total))
        link(dve.tensor_tensor(self.gates[:, slots].rearrange("p (h i) -> p h i", h=PE_HEADS), self.chosen,
                               bc(total, [P, PE_HEADS, PE_TOP]), ALU.mult))

    def part_of_routing(self, dve, ph, link, m, i):
        if i < 8:
            self.keys(dve, link, m, (2 * i, 2 * i + 1))
        if i == 8:
            self.pairs(dve, link, m)
            self.heads(dve, link, (0,))
        if 9 <= i < 12:
            self.heads(dve, link, (2 * i - 17, 2 * i - 16))
        if i == 12:
            self.heads(dve, link, (7,))
            self.shift(dve, ph, link)
        if i in (13, 14):
            self.look_up(dve, link, m, i - 13)
        if i == 15:
            self.finish(dve, ph, link, m)


ROUTE_PARTS = 16


def peer(k, layer):
    z = Peer(k)
    norm_phase(k, "norm_ffn", k.x, k.p2("norm_ffn"), k.hT, loads=[(k.gain_row[:], k.dram["gain_rows"][1 + layer])], out_tok=z.xt,
               scratch=z.kept, parts=(z.x_high, k.hT_low))
    with k.phase("peer_route") as ph:
        lq, sub = ph.linear("peer_q"), ph.linear("subkeys", grouped=False)
        split = Split(k, ph, z.route_end, without=1)
        with k.engines(ph) as block:
            @block.sync
            def _(sp):
                k.load_ahead(sp, ph)

            @block.gpsimd
            def _(pool):
                pool.iota(z.iota, pattern=[[1, PE_TOP]], base=0, channel_multiplier=0, allow_small_or_imprecise_dtypes=True
                          ).then_inc(ph.sem("iota_ready"), 1)

            @block.tensor
            def _(pe):
                k.linear_T(pe, ph, lq, (z.x_high, k.hT_low), split)
                k.wait_chunk(pe, sub.chunk0)
                keys = k.ring[:, sub.chunk0 % SLOTS, :]
                pe.wait_ge(ph.sem("queries_ready"), 4)
                for m in range(MT):
                    for hp in range(16):
                        last = pe.matmul(k.ps[:, 4 * m + hp // 4, (hp % 4) * P:(hp % 4 + 1) * P], z.qT[:, hp, m * P:(m + 1) * P],
                                         keys[:, hp * P:(hp + 1) * P], start=True, stop=True)
                    last.then_inc(ph.sem("scores_done"), 1)

            @block.scalar
            def _(act):
                link = Chain(act, ph.sem("act_chain"))
                for n in range(4):
                    split.high_for(act, lq, n)
                    pair, free = k.take(act, ph, lq, n)
                    link(act.activation(z.qT[:, 4 * n:4 * n + 4, :].rearrange("p a t -> p (a t)"), pair.rearrange("p a b -> p (a b)"), ACT.Copy))
                    act.sem_inc(free, 1)
                    act.sem_inc(ph.sem("queries_ready"), 1)
                for m in range(MT):
                    act.wait_ge(ph.sem("scores_done"), m + 1)
                    act.activation(z.scores[m].rearrange("p a b -> p (a b)"), k.ps[:, 4 * m:4 * m + 4, :].rearrange("p a b -> p (a b)"), ACT.Copy
                                   ).then_inc(ph.sem("scores_copied"), 1)
                act.sem_inc(k.ring_free[sub.chunk0 % SLOTS], 1)
                act.wait_ge(ph.sem("chosen_shifted"), 1)
                act.activation(z.chosen, z.chosen, ACT.Exp).then_inc(ph.sem("chosen_exp"), 1)

            @block.vector
            def _(dve):
                link = Chain(dve, ph.sem("dve_chain"))
                split.low_for(dve, lq, 3)
                link(dve.memset(z.index, 0.0))
                dve.wait_ge(ph.sem("iota_ready"), 1)
                dve.wait_ge(ph.sem("scores_copied"), 1)
                for i in range(ROUTE_PARTS):
                    z.part_of_routing(dve, ph, link, 0, i)

    table = k.dram[f"experts{layer}"]
    rows, dots, index, gates, staged = z.rows, z.dots, z.index, z.gates, k.stage_index
    steps = N_GATHER // 2
    assert steps == ROUTE_PARTS
    with k.phase("peer_experts") as ph:
        with k.engines(ph) as block:
            @block.gpsimd
            def _(pool):
                with pool.Fori(0, MT * steps) as step:
                    for b in range(2):
                        pool.wait_ge(ph.sem(f"slot_ready{b}"), step + 1)
                        pool.sem_inc(ph.sem("gathers_begun"), 1)
                        for e in range(GATHER):
                            pool.indirect_dma_start(rows[:, b, e, :], None, table, bass.IndirectOffsetOnAxis(ap=staged[:, b, e:e + 1], axis=0)
                                                    ).then_inc(k.gathered[b][e], 16)

            @block.vector
            def _(dve):
                chain = ph.sem("dve_chain")
                link = Chain(dve, ph.sem("route_chain"))

                def experts(m, step):
                    per_step = 2 * (GATHER + 2)
                    for b in range(2):
                        base = step * per_step + b * (GATHER + 2)
                        for e in range(GATHER):
                            dve.wait_ge(k.gathered[b][e], step * 16 + 16 + layer * MT * steps * 16)
                            dve.tensor_tensor_reduce(rows[:, b, e, 0:D], rows[:, b, e, 0:D], z.xt[:, m, :], 1.0, 0.0, ALU.mult, ALU.add,
                                                     dots[:, 0, b, e:e + 1]).then_inc(ph.sem("dots_done"), 1)
                        dve.tensor_copy(staged[:, b, :], index[:, bass.ds((step + 1) * 2 * GATHER + b * GATHER, GATHER)]).then_inc(chain, 1)
                        dve.wait_ge(ph.sem("gelu_done"), step * 2 + b + 1)
                        dve.tensor_tensor(dots[:, 1, b, :], dots[:, 1, b, :], gates[:, bass.ds(step * 2 * GATHER + b * GATHER, GATHER)], ALU.mult
                                          ).then_inc(chain, 1)
                        dve.wait_ge(chain, base + 2)
                        for e in range(GATHER):
                            x = k.x[:, m, :]
                            dve.scalar_tensor_tensor(out=x, in0=rows[:, b, e, D:2 * D], scalar=dots[:, 1, b, e:e + 1], in1=x,
                                                     op0=ALU.mult, op1=ALU.add).then_inc(chain, 1)
                            dve.wait_ge(chain, base + 3 + e)
                        dve.sem_inc(ph.sem(f"slot_ready{b}"), 1)

                for b in range(2):
                    dve.tensor_copy(staged[:, b, :], index[:, b * GATHER:(b + 1) * GATHER]).then_inc(ph.sem(f"slot_ready{b}"), 1)
                for step in range(steps):
                    z.part_of_routing(dve, ph, link, 1, step)
                    experts(0, step)
                with dve.Fori(steps, 2 * steps) as step:
                    experts(1, step)

            @block.scalar
            def _(act):
                def gelus(step):
                    for b in range(2):
                        act.wait_ge(ph.sem("dots_done"), step * 2 * GATHER + (b + 1) * GATHER)
                        act.activation(dots[:, 1, b, :], dots[:, 0, b, :], ACT.Gelu).then_inc(ph.sem("gelu_done"), 1)

                with act.Fori(0, 13) as step:
                    gelus(step)
                act.wait_ge(ph.sem("chosen_shifted"), 1)
                act.activation(z.chosen, z.chosen, ACT.Exp).then_inc(ph.sem("chosen_exp"), 1)
                with act.Fori(13, MT * steps) as step:
                    gelus(step)


def second_stack(k):
    even, odd = TilesEven(k), TilesOdd(k)
    for layer in range(DEPTH):
        norm_phase(k, "norm_mix", k.x, k.p2("norm_mix"), k.hT, loads=[(k.par[:, 0:P2_W], k.dram["params2"][layer])],
                   parts=even.h_parts if layer % 2 == 0 else odd.h_parts, scratch=odd.in_end)
        if layer % 2 == 0:
            even_in_phase(k, even)
            ssd_phase(k, even)
            mlstm_phase(k, even)
            mixer_out_phase(k, "even_out", [even.ya, even.yb], [k.p2("ssd_norm"), k.p2("ml_norm")], "ev_out", at=0, spare=even.shared)
        else:
            odd_in_phase(k, odd)
            hgrn_phase(k, odd)
            mixer_out_phase(k, "odd_out", [odd.y], [k.p2("hgrn_norm")], "od_out", at=odd.mixer, spare=odd.in_end)
        cross_attention(k, layer)
        peer(k, layer)
    norm_phase(k, "final_norm", k.x, None, None, loads=[(k.gain_row[:], k.dram["gain_rows"][3])], out_tok=k.x)
    assert k.stream_at == len(STREAM_2) and k.next_chunk == CHUNKS_2


def build(nc, dram):
    with ExitStack() as stack:
        k = Kernel(nc, dram, stack)
        constants_phase(k)
        with nc.Fori(0, DEPTH) as layer:
            k.layer = layer
            first_layer(k)
        k.layer = None
        final = [(k.gain_row[:], dram["gain_rows"][0])]
        norm_phase(k, "first_final_norm", k.x, None, None, loads=final, out_tok=k.x)
        k.stream, k.stream_at, k.next_chunk = STREAM_2, 0, 0
        second_stack(k)
        with k.phase("store") as ph:
            with k.engines(ph) as block:
                @block.sync
                def _(sp):
                    sp.dma_start(dram["out"], k.x[:]).then_inc(ph.sem("stored"), 16)
                    sp.wait_ge(ph.sem("stored"), 16)




def rows_of(w, order=None):
    return w.reshape(w.shape[0] // P, P, w.shape[1]).transpose(1, 0, 2)


def chunked(w):
    kk, n = w.shape
    if n % BLK:
        w = np.concatenate([w, np.zeros((kk, BLK - n % BLK), w.dtype)], axis=1)
        n = w.shape[1]
    b = w.reshape(kk // P, P, n // BLK, BLK).transpose(2, 0, 1, 3).reshape(-1, P, BLK)
    if len(b) % CHUNK_BLOCKS:
        b = np.concatenate([b, np.zeros((CHUNK_BLOCKS - len(b) % CHUNK_BLOCKS, P, BLK), w.dtype)])
    return b.reshape(-1, CHUNK_BLOCKS, P, BLK).transpose(0, 2, 1, 3).reshape(-1, P, CHUNK)


def col(v):
    return v.reshape(-1, P).T


def every(v):
    return np.broadcast_to(v.reshape(1, -1), (P, v.size))


PAIRED = [h for i in range(4) for h in (i, 4 + i)]


def paired(w, width=HD):
    return w.reshape(w.shape[0], 8, width)[:, PAIRED].reshape(w.shape[0], -1)


def layer_chunks(i, a):
    sizes = [512, 128, 128, 128, 128, 128, 128, 24, 512, 128, 128, 256, 256, 32]
    names = ["q", "kc", "vc", "ks", "vs", "kw", "vw", "g", "bq", "bk", "bv", "cq", "ckv", "kpe"]
    cut = dict(zip(names, np.split(a["w_in"][i], np.cumsum(sizes)[:-1], axis=1)))
    cat = lambda *names: np.concatenate([cut[n] for n in names], axis=1)
    gate, up = a["w_ffn_gate"][i], a["w_ffn_up"][i]
    both = np.stack([gate.reshape(D, FF_T // 2, 256), up.reshape(D, FF_T // 2, 256)], axis=2).reshape(D, -1)
    w1 = np.concatenate([a["a_cmp_w1_k"][i].reshape(32, HD, 256).transpose(1, 0, 2),
                         a["a_cmp_w1_v"][i].reshape(32, HD, 256).transpose(1, 0, 2)])
    w1 = w1.reshape(P, 4, CHUNK).transpose(1, 0, 2)
    pair_rows = lambda w: paired(w.T).T
    parts = [chunked(paired(cut["q"])), chunked(cat("ks", "kw", "bk", "kc")), chunked(paired(cut["bq"])),
             chunked(cat("vc", "vs", "vw", "bv")), chunked(cat("cq", "ckv")), chunked(a["w_branch_gate"][i]), w1,
             chunked(a["c_w_q_up"][i]), chunked(a["c_w_kv_up"][i])]
    parts += [chunked(pair_rows(a[f"w_branch_{c}"][i])) for c in "abc"]
    parts += [chunked(a["w_out"][i]), chunked(both), chunked(a["w_ffn_down"][i]), chunked(a["w_ple_gate"][i]),
              chunked(a["w_ple_proj"][i])]
    small = np.concatenate([cut["kpe"], cut["g"].reshape(D, 8, 3).transpose(0, 2, 1).reshape(D, 24)], axis=1)
    two = lambda w: rows_of(w).reshape(P, -1)
    pos = np.concatenate([a["a_cmp_pos_k"][i].T, a["a_cmp_pos_v"][i].T])
    params = np.concatenate([col(a["mix_norm"][i]), col(a["ffn_norm"][i]), col(a["ple_norm"][i]), col(a["c_q_norm"][i]),
                             col(a["c_kv_norm"][i]), two(small), two(a["a_cmp_w2_k"][i]), two(a["a_cmp_w2_v"][i]), pos,
                             every(a["b_sinks"][i])], axis=1)
    return parts, params


def in_pairs(w):
    return w.reshape(4, 2, P, T).transpose(2, 0, 1, 3).reshape(1, P, CHUNK)


def second_chunks(a):
    w = a["ev_w_in_2"][0]
    z, xbc, dt, xm, og, ig, fg = np.split(w, np.cumsum([D, 1536, 16, D, D, 4])[:6], axis=1)
    attend = lambda i: [chunked(a["xa_wq_2"][i]), chunked(a["xa_wkv_2"][i][:, :D]), chunked(a["xa_wkv_2"][i][:, D:]),
                        chunked(a["xa_wo_2"][i]), chunked(a["peer_wq_2"][i]),
                        a["peer_subkeys_2"][i].reshape(16, PE_KEYS, P).transpose(2, 0, 1).reshape(1, P, CHUNK)]
    q, f, v, g = np.split(a["od_w_in_2"][0], 4, axis=1)
    parts = ([chunked(z), chunked(xbc), chunked(xm), chunked(og), in_pairs(a["ml_wq_2"][0]), in_pairs(a["ml_wk_2"][0]),
              in_pairs(a["ml_wv_2"][0]), chunked(a["ev_w_out_2"][0])] + attend(0)
             + [chunked(f), chunked(q), chunked(v), chunked(g), chunked(a["od_w_out_2"][0])] + attend(1))
    taps = lambda w: w.T.reshape(-1, P, 4).transpose(1, 0, 2).reshape(P, -1)
    small = rows_of(np.concatenate([dt, ig, fg], axis=1)).reshape(P, -1)
    bias = np.concatenate([a["ssd_dt_bias_2"][0], a["ml_i_bias_2"][0], a["ml_f_bias_2"][0]])
    params = []
    for i in range(DEPTH):
        params.append(np.concatenate(
            [col(a[n][i]) for n in ("norm_mix_2", "norm_xattn_2", "norm_mem_2", "norm_ffn_2")]
            + [small, every(bias), every(a["ssd_a_log_2"][0]), every(a["ssd_d_skip_2"][0]), taps(a["ssd_conv_w_2"][0]),
               col(a["ssd_conv_b_2"][0]), col(a["ssd_norm_2"][0]), taps(a["ml_conv_w_2"][0]), col(a["ml_conv_b_2"][0]),
               col(a["ml_norm_2"][0]), col(a["hgrn_lb_logits_2"].reshape(-1)), col(a["hgrn_norm_2"][0])], axis=1))
    arrays = {"params2": np.stack(params), "mem": a["mem_2"][0].reshape(MT, P, D).transpose(1, 0, 2)}
    for i in range(DEPTH):
        arrays[f"experts{i}"] = np.concatenate([a["peer_u_2"][i], a["peer_v_2"][i]], axis=1)
    return parts, arrays


def kernel(**inputs):
    import concourse.bacc as bacc
    from concourse.bass_utils import run_bass_kernel_spmd

    a = {n: np.asarray(v) for n, v in inputs.items()}
    tok = lambda v: v.reshape(MT, P, -1).transpose(1, 0, 2)
    layers = [layer_chunks(i, a) for i in range(DEPTH)]
    parts = [c for chunks, _ in layers for c in chunks]
    second, second_arrays = second_chunks(a)
    freq = np.concatenate([np.power(np.float32(10000.0), -np.arange(0, d, 2, dtype=np.float32) / d) for d in (64, 32)])
    arrays = {
        "x": tok(a["x"][0]),
        "positions": a["positions"].reshape(MT, P).T,
        "freq": every(freq.astype(np.float32)),
        "pT": a["p"][:, 0].transpose(0, 2, 1).reshape(DEPTH, 2, P, T).transpose(0, 2, 1, 3),
        "params1": np.stack([p for _, p in layers]),
        "gain_rows": np.stack([every(v) for v in (a["final_norm"], a["norm_ffn_2"][0], a["norm_ffn_2"][1], a["norm_final_2"])]),
        "stream": np.concatenate(parts + second),
        **second_arrays,
    }
    arrays = {f"in_{n}": np.ascontiguousarray(v) for n, v in arrays.items()}
    nc = bacc.Bacc("TRN2", target_bir_lowering=False, num_devices=1)
    dram = {n[3:]: nc.dram_tensor(n, v.shape, mybir.dt.from_np(v.dtype), kind="ExternalInput").ap() for n, v in arrays.items()}
    dram["out"] = nc.dram_tensor("out", (P, MT, D), F32, kind="ExternalOutput").ap()
    build(nc, dram)
    result = run_bass_kernel_spmd(nc, [arrays], core_ids=[0]).results[0]["out"]
    return result.transpose(1, 0, 2).reshape(1, T, D)
```
